# Optimizing a Trainium2 kernel written in Bass

```python
import jax, jax.numpy as jnp
from jax import lax
import numpy as np

D_MODEL = 1024
BATCH = 1
SEQ = 1024
DEPTH = 1

CHUNK = 64
Q_BLOCK = 128
HEAD_DIM = 64
N_SB_HEADS = 8
N_FOX_HEADS = 8
SB_WIDTH = N_SB_HEADS * HEAD_DIM
FOX_WIDTH = N_FOX_HEADS * HEAD_DIM
N_BRANCHES = 2
D_FF = 2816
CONV_WIDTH = 3
EPS = 1e-6
OFF_SB = 0
OFF_FOX = OFF_SB + 3 * SB_WIDTH
OFF_FORGET = OFF_FOX + 3 * FOX_WIDTH
OFF_GATE = OFF_FORGET + N_FOX_HEADS
IN_COLS = OFF_GATE + N_BRANCHES * D_MODEL

kernel_name = "hybrid_stickbreak_fox_convffn"

def rms_norm(x, g):
    xf = x.astype(jnp.float32)
    y = xf * lax.rsqrt(jnp.mean(xf * xf, axis=-1, keepdims=True) + EPS)
    return y.astype(x.dtype) * g

def split_heads(t, n_heads):
    b, s, _ = t.shape
    return t.reshape(b, s, n_heads, HEAD_DIM).transpose(0, 2, 1, 3)

def merge_heads(t):
    b, h, s, d = t.shape
    return t.transpose(0, 2, 1, 3).reshape(b, s, h * d)

def stick_breaking_attention(q, k, v):
    seq = q.shape[2]
    scale = HEAD_DIM ** -0.5
    outs = []
    for start in range(0, seq, Q_BLOCK):
        end = start + Q_BLOCK
        qb = q[:, :, start:end]
        kp, vp = k[:, :, :end], v[:, :, :end]
        z = jnp.einsum("bhqd,bhkd->bhqk", qb, kp).astype(jnp.float32) * scale
        q_pos = start + jnp.arange(Q_BLOCK)[:, None]
        k_pos = jnp.arange(end)[None, :]
        strict = k_pos < q_pos
        log_fail = jnp.where(strict, jax.nn.log_sigmoid(-z), 0.0)
        after = lax.cumsum(log_fail, axis=3, reverse=True) - log_fail
        w = jnp.where(strict, jnp.exp(jax.nn.log_sigmoid(z) + after), 0.0)
        outs.append(jnp.einsum("bhqk,bhkd->bhqd", w.astype(v.dtype), vp))
    return jnp.concatenate(outs, axis=2)

def forgetting_attention(q, k, v, log_f):
    seq = q.shape[2]
    scale = HEAD_DIM ** -0.5
    c = lax.cumsum(log_f, axis=2)
    outs = []
    for start in range(0, seq, Q_BLOCK):
        end = start + Q_BLOCK
        qb = q[:, :, start:end]
        kp, vp = k[:, :, :end], v[:, :, :end]
        z = jnp.einsum("bhqd,bhkd->bhqk", qb, kp).astype(jnp.float32) * scale
        z = z + c[:, :, start:end, None] - c[:, :, None, :end]
        q_pos = start + jnp.arange(Q_BLOCK)[:, None]
        k_pos = jnp.arange(end)[None, :]
        z = jnp.where(k_pos <= q_pos, z, -jnp.inf)
        p = jax.nn.softmax(z, axis=-1)
        outs.append(jnp.einsum("bhqk,bhkd->bhqd", p.astype(v.dtype), vp))
    return jnp.concatenate(outs, axis=2)

def causal_depthwise_conv(u, w, b):
    c = u.shape[-1]
    y = lax.conv_general_dilated(
        u, w.astype(u.dtype)[:, None, :],
        window_strides=(1,), padding=[(CONV_WIDTH - 1, 0)],
        dimension_numbers=("NWC", "WIO", "NWC"), feature_group_count=c)
    return y + b

def setup_inputs(seed: int = 0) -> dict:
    key = jax.random.key(seed)
    ks = jax.random.split(key, 16)
    nrm = lambda k, shape, fan_in: jax.random.normal(k, shape, jnp.float32) * fan_in ** -0.5
    gain = lambda k, shape: 1.0 + 0.1 * jax.random.normal(k, shape, jnp.float32)
    return {
        "x": jax.random.normal(ks[0], (BATCH, SEQ, D_MODEL), jnp.float32),
        "g_mix": gain(ks[1], (DEPTH, D_MODEL)),
        "w_in": nrm(ks[2], (DEPTH, D_MODEL, IN_COLS), D_MODEL),
        "b_forget": jax.random.uniform(ks[3], (DEPTH, N_FOX_HEADS), jnp.float32, 1.0, 5.0),
        "b_gate": 0.01 * jax.random.normal(ks[4], (DEPTH, N_BRANCHES * D_MODEL), jnp.float32),
        "g_q": gain(ks[5], (DEPTH, HEAD_DIM)),
        "g_k": gain(ks[6], (DEPTH, HEAD_DIM)),
        "w_o_sb": nrm(ks[7], (DEPTH, SB_WIDTH, D_MODEL), SB_WIDTH),
        "w_o_fox": nrm(ks[8], (DEPTH, FOX_WIDTH, D_MODEL), FOX_WIDTH),
        "w_out": nrm(ks[9], (DEPTH, D_MODEL, D_MODEL), D_MODEL),
        "g_ffn": gain(ks[10], (DEPTH, D_MODEL)),
        "w_up": nrm(ks[11], (DEPTH, D_MODEL, 2 * D_FF), D_MODEL),
        "conv_w": nrm(ks[12], (DEPTH, CONV_WIDTH, 2 * D_FF), CONV_WIDTH),
        "conv_b": 0.01 * jax.random.normal(ks[13], (DEPTH, 2 * D_FF), jnp.float32),
        "w_down": nrm(ks[14], (DEPTH, D_FF, D_MODEL), D_FF),
    }

def reference(x, g_mix, w_in, b_forget, b_gate, g_q, g_k, w_o_sb, w_o_fox, w_out,
              g_ffn, w_up, conv_w, conv_b, w_down):
    b, s, _ = x.shape
    for layer in range(DEPTH):
        h = rms_norm(x, g_mix[layer])
        proj = h @ w_in[layer]
        q_sb = split_heads(proj[..., OFF_SB:OFF_SB + SB_WIDTH], N_SB_HEADS)
        k_sb = split_heads(proj[..., OFF_SB + SB_WIDTH:OFF_SB + 2 * SB_WIDTH], N_SB_HEADS)
        v_sb = split_heads(proj[..., OFF_SB + 2 * SB_WIDTH:OFF_FOX], N_SB_HEADS)
        q_fx = split_heads(proj[..., OFF_FOX:OFF_FOX + FOX_WIDTH], N_FOX_HEADS)
        k_fx = split_heads(proj[..., OFF_FOX + FOX_WIDTH:OFF_FOX + 2 * FOX_WIDTH], N_FOX_HEADS)
        v_fx = split_heads(proj[..., OFF_FOX + 2 * FOX_WIDTH:OFF_FORGET], N_FOX_HEADS)
        q_fx = rms_norm(q_fx, g_q[layer])
        k_fx = rms_norm(k_fx, g_k[layer])
        f_logit = (proj[..., OFF_FORGET:OFF_GATE] + b_forget[layer]).astype(jnp.float32)
        log_f = jax.nn.log_sigmoid(f_logit).transpose(0, 2, 1)
        gates = jax.nn.sigmoid(proj[..., OFF_GATE:] + b_gate[layer]).reshape(b, s, N_BRANCHES, D_MODEL)

        y_sb = merge_heads(stick_breaking_attention(q_sb, k_sb, v_sb)) @ w_o_sb[layer]
        y_fx = merge_heads(forgetting_attention(q_fx, k_fx, v_fx, log_f)) @ w_o_fox[layer]
        mixed = gates[:, :, 0] * y_sb + gates[:, :, 1] * y_fx
        x = x + mixed @ w_out[layer]

        h = rms_norm(x, g_ffn[layer])
        u = causal_depthwise_conv(h @ w_up[layer], conv_w[layer], conv_b[layer])
        gate, val = u[..., :D_FF], u[..., D_FF:]
        x = x + (jax.nn.silu(gate) * val) @ w_down[layer]
    return x


_drawn_inputs = setup_inputs


def setup_inputs(seed=0):
    import zlib

    import numpy as np

    out = dict(_drawn_inputs(seed))
    spreads = {}
    factors = {'b_gate': 25.936, 'g_q': 3.476, 'g_k': 3.37, 'conv_b': 8.0}
    for name, (base, spread) in spreads.items():
        noise = np.random.default_rng([zlib.crc32(name.encode()), seed]).standard_normal(out[name].shape)
        drawn = base * np.exp(spread * noise) if base else spread * noise
        out[name] = __import__('jax').numpy.asarray(drawn.astype(out[name].dtype))
    for name, factor in factors.items():
        out[name] = (out[name] * factor).astype(out[name].dtype)
    return out
```

```python
from contextlib import ExitStack

import concourse.bass as bass
from concourse import mybir

F32 = mybir.dt.float32
F32R = mybir.dt.float32r
ALU = mybir.AluOpType
ACT = mybir.ActivationFunctionType

P = 128
S = 1024
D = 1024
H = 8
HD = 64
FF = 2816
EPS = 1e-6
NEG = -1e30
KT = D // P
TB = S // P
HALF = 512
FT = FF // P
PAIRS = H // 2
OFF_FOX = 3 * H * HD
OFF_FORGET = 2 * OFF_FOX
OFF_GATE = OFF_FORGET + H
SB, FX = 0, 1


def after(eng, sem, value):
    if isinstance(value, int) and value <= 0:
        return
    eng.wait_ge(sem, value)


BLOCKS = 4 * TB
SLOTS = BLOCKS + 4
CHUNK_SLOTS = (0, 2, 5, 7, 10, 12)


def block_of(n):
    return n // TB, n % TB, (n // TB) % 2, n // (2 * TB)


def make_schedule(last):
    groups, aux, e, g = [[] for _ in range(SLOTS)], [None] * SLOTS, 0, 0
    for n in range(SLOTS):
        k = n - n % 2
        if k >= 4:
            q = (k - 4) // 2
            p = q % (TB // 2)
            mine = range(p + 1)
            split = (p + 2) // 2
            for j in (mine[:split] if n % 2 == 0 else mine[split:]):
                groups[n].append(dict(e=e, g=g, q=q, p=p, j=j, unit=(2 * q) // TB))
                e, g = e + 1, g + 1
        for c, a in enumerate(CHUNK_SLOTS):
            for br in (SB, FX):
                if n == 16 * br + a + 2:
                    target = 1 - br
                    if (c >= 4 or target == FX) and not (last and target == SB):
                        aux[n] = dict(e=e, c=c, target=target)
                        e += 1
    return groups, aux, e, g


SCHEDULES = {last: make_schedule(last) for last in (False, True)}
EVENTS, NGROUPS = SCHEDULES[False][2:]
assert EVENTS % 2 == 0 and NGROUPS % 2 == 0
PRO_EVENTS = 2


def chunk_at(n):
    br, s = n // 16, n % 16
    for c, a in enumerate(CHUNK_SLOTS):
        if n < BLOCKS and s in (a, a + 1):
            return 1 - br, c, s - a
    return None


def copied_at(n):
    br, s = n // 16, n % 16
    for c, a in enumerate(CHUNK_SLOTS):
        if n < BLOCKS and s == a + 2:
            return 1 - br, c
    return None


def v_event(aux, target, c):
    return next(a["e"] for a in aux if a and a["target"] == target and a["c"] == c)


def last_event_of_pair(groups, q):
    return max(g["e"] for gs in groups for g in gs if g["q"] == q)


def last_group_of_pair(groups, q):
    return max(g["g"] for gs in groups for g in gs if g["q"] == q)


def build(nc, x, g_mix, w_in, b_forget, b_gate, g_q, g_k, w_o_sb, w_o_fox, w_out, g_ffn, w_up,
          conv_w, conv_b, w_down, out):
    o_dram = nc.dram_tensor("attn_out_t", (2 * PAIRS * P, S), F32, kind="Internal").ap()
    cum_dram = nc.dram_tensor("neg_cum_forget", (H, S), F32, kind="Internal").ap()
    x2_dram = nc.dram_tensor("mid_residual", (S, D), F32, kind="Internal").ap()
    win_v = w_in[0].rearrange("(k p) n -> p k n", p=P)
    wup_v = w_up[0].rearrange("(k p) n -> p k n", p=P)
    wosb_v = w_o_sb[0].rearrange("(k p) n -> p k n", p=P)
    wofx_v = w_o_fox[0].rearrange("(k p) n -> p k n", p=P)

    with ExitStack() as whole:
        def maker(ctx):
            def sb(name, shape, dt=F32):
                return ctx.enter_context(nc.sbuf_tensor(name, shape, dt))

            def ps(name, shape=(P, S)):
                return ctx.enter_context(nc.psum_tensor(name, list(shape), F32))

            def sem(name):
                return ctx.enter_context(nc.semaphore(name))
            return sb, ps, sem

        sb, _, _ = maker(whole)
        ident = sb("ident", [P, P])
        head_ones = sb("head_ones", [P, P])
        mask_f = sb("mask_f", [P, 2, P])
        maskr = sb("maskr", [P, 2, P], F32R)
        identr = sb("identr", [P, P], F32R)
        zero = sb("zero", [P, 1])
        zero3 = zero[:].rearrange("p (a b) -> p a b", a=1).to_broadcast([P, KT, P])
        cols = sb("cols", [P, 5, FT * 2])
        gqk = sb("gqk", [P, 4])
        bfc = sb("bfc", [H, 1])

        early = whole.enter_context(ExitStack())
        sbh, _, _ = maker(early)
        hTh = sbh("hTh", [P, KT, S], F32R)
        hTl = sbh("hTl", [P, KT, S], F32R)
        with ExitStack() as ctx:
            sb, ps, sem = maker(ctx)
            gain = sb("gain", [P, D])
            rows = sb("rows", [2 * FT, 5, P])
            xt = [sb(f"xt{j}", [P, D]) for j in range(2)]
            xn = [sb(f"xn{j}", [P, D]) for j in range(2)]
            stat = sb("stat", [P, 3, 2])
            turned = [ps(f"turned{j}") for j in range(2)]
            turned_c = ps("turned_c", (P, 512))
            gain_in, consts_in, small_in = sem("gain_in"), sem("consts_in"), sem("small_in")
            x_in = [sem(f"x_in{j}") for j in range(2)]
            const0, const1, const2 = sem("const0"), sem("const1"), sem("const2")
            sq_done, root_done, inv_done, xn_done = (sem(n) for n in ("sq", "root", "inv", "xn"))
            tr_done, hi_done, lo_done = sem("tr1"), sem("hi1"), sem("lo1")
            colt_done, col_done, gq_done = sem("colt"), sem("col"), sem("gq8")
            eps_set = sem("eps_set")
            eps_t = sb("eps_t", [P, 1])
            eps_col = eps_t[:, 0:1]
            block = ctx.enter_context(nc.Block())

            @block.sync
            def _(sp):
                def load(t, j):
                    after(sp, xn_done, t - 1)
                    sp.dma_start(xt[j][:], x[0, bass.ds(t * P, P), :]).then_inc(x_in[j], 16)
                load(0, 0)
                sp.dma_start(gain[:], g_mix.to_broadcast([P, D])).then_inc(gain_in, 16)
                load(1, 1)
                for c in range(3):
                    sp.dma_start(rows[0:2 * FT, c, :], conv_w[0, c].rearrange("(a b) -> a b", b=P)).then_inc(consts_in, 16)
                sp.dma_start(rows[0:2 * FT, 3, :], conv_b[0].rearrange("(a b) -> a b", b=P)).then_inc(consts_in, 16)
                sp.dma_start(rows[0:16, 4, :], b_gate[0].rearrange("(a b) -> a b", b=P)).then_inc(consts_in, 16)
                with nc.allow_non_contiguous_dma(reason="a few gains, one to a partition"):
                    for half in range(2):
                        for c, g in ((0, g_q), (1, g_k)):
                            sp.dma_start(gqk[HD * half:HD * half + HD, c:c + 1], g.rearrange("a b -> b a")).then_inc(small_in, 16)
                    sp.dma_start(bfc[:], b_forget.rearrange("a b -> b a")).then_inc(small_in, 16)
                with sp.Fori(1, TB // 2) as i:
                    for j in range(2):
                        load(2 * i + j, j)

            @block.gpsimd
            def _(pool):
                pool.memset(ident[:], 0.0).then_inc(const0, 1)
                pool.memset(mask_f[:], 0.0).then_inc(const0, 1)
                pool.memset(zero[:], 0.0)
                pool.memset(head_ones[:], 0.0).then_inc(const0, 1)
                pool.wait_ge(const0, 3)
                pool.affine_select(out=ident[:], in_=ident[:], compare_op=ALU.not_equal, fill=1.0,
                                   base=0, pattern=[[-1, P]], channel_multiplier=1).then_inc(const1, 1)
                pool.affine_select(out=mask_f[:, SB, :], in_=mask_f[:, SB, :], compare_op=ALU.is_gt, fill=NEG,
                                   base=0, pattern=[[-1, P]], channel_multiplier=1).then_inc(const1, 1)
                pool.affine_select(out=mask_f[:, FX, :], in_=mask_f[:, FX, :], compare_op=ALU.is_ge, fill=NEG,
                                   base=0, pattern=[[-1, P]], channel_multiplier=1).then_inc(const1, 1)
                for half in range(2):
                    pool.wait_ge(const1, 3 + half)
                    r = slice(HD * half, HD * half + HD)
                    pool.memset(head_ones[r, r], 1.0).then_inc(const1, 1)
                pool.wait_ge(const1, 5)
                pool.tensor_copy(maskr[:], mask_f[:]).then_inc(const2, 1)
                pool.tensor_copy(identr[:], ident[:]).then_inc(const2, 1)

            @block.scalar
            def _(act):
                def stats(t, j):
                    act.wait_ge(x_in[j], (t // 2 + 1) * 16)
                    after(act, tr_done, t - 1)
                    act.activation(xn[j][:], xt[j][:], ACT.Square, accum_out=stat[:, 0, j:j + 1]).then_inc(sq_done, 1)
                    act.wait_ge(sq_done, t + 1)
                    after(act, inv_done, t - 1)
                    act.activation(stat[:, 1, j:j + 1], stat[:, 0, j:j + 1], ACT.Sqrt, scale=1.0 / D, bias=eps_col).then_inc(root_done, 1)

                def high(t, j):
                    act.wait_ge(tr_done, t + 1)
                    act.activation(hTh[:, :, bass.ds(t * P, P)], turned[j][:].rearrange("p (k t) -> p k t", k=KT), ACT.Copy).then_inc(hi_done, 1)
                act.wait_ge(eps_set, 1)
                stats(0, 0)
                stats(1, 1)
                high(0, 0)
                with act.Fori(1, TB // 2) as i:
                    stats(2 * i, 0)
                    high(2 * i - 1, 1)
                    stats(2 * i + 1, 1)
                    high(2 * i, 0)
                high(TB - 1, 1)

            @block.vector
            def _(dve):
                dve.memset(eps_t[:], EPS).then_inc(eps_set, 1)
                dve.wait_ge(gain_in, 16)

                def norm(t, j):
                    dve.wait_ge(root_done, t + 1)
                    after(dve, xn_done, t - 1)
                    dve.reciprocal(stat[:, 2, j:j + 1], stat[:, 1, j:j + 1]).then_inc(inv_done, 1)
                    dve.wait_ge(inv_done, t + 1)
                    dve.scalar_tensor_tensor(out=xn[j][:], in0=xt[j][:], scalar=stat[:, 2, j:j + 1], in1=gain[:],
                                             op0=ALU.mult, op1=ALU.mult).then_inc(xn_done, 1)

                def low(t, j):
                    dve.wait_ge(hi_done, t + 1)
                    dve.tensor_tensor(hTl[:, :, bass.ds(t * P, P)], turned[j][:].rearrange("p (k t) -> p k t", k=KT),
                                      hTh[:, :, bass.ds(t * P, P)].bitcast(F32), ALU.subtract).then_inc(lo_done, 1)
                norm(0, 0)
                norm(1, 1)
                low(0, 0)
                with dve.Fori(1, TB // 2) as i:
                    norm(2 * i, 0)
                    low(2 * i - 1, 1)
                    norm(2 * i + 1, 1)
                    low(2 * i, 0)
                low(TB - 1, 1)
                dve.wait_ge(colt_done, 1)
                dve.tensor_copy(cols[:].rearrange("p a b -> p (a b)")[:, 0:8 * FT + 16], turned_c[:, 0:8 * FT + 16]).then_inc(col_done, 1)
                dve.wait_ge(small_in, 80)
                dve.tensor_scalar(gqk[:, 2:3], gqk[:, 0:1], HD ** -0.5, None, ALU.mult).then_inc(gq_done, 1)

            @block.tensor
            def _(pe):
                def turn(t, j):
                    pe.wait_ge(xn_done, t + 1)
                    after(pe, hi_done, t - 1)
                    after(pe, lo_done, t - 1)
                    for k in range(KT):
                        mm = pe.transpose(turned[j][:, k * P:(k + 1) * P], xn[j][:, k * P:(k + 1) * P], ident[:])
                    mm.then_inc(tr_done, 1)
                pe.wait_ge(const1, 5)
                turn(0, 0)
                turn(1, 1)
                with pe.Fori(1, TB // 2) as i:
                    turn(2 * i, 0)
                    turn(2 * i + 1, 1)
                pe.wait_ge(consts_in, 80)
                for c in range(5):
                    n = 2 * FT if c < 4 else 16
                    mm = pe.transpose(turned_c[:, 2 * FT * c:2 * FT * c + n], rows[0:n, c, :], ident[0:n, 0:n])
                mm.then_inc(colt_done, 1)

        with ExitStack() as ctx:
            sb, ps, sem = maker(ctx)
            raw = [sb(f"raw{j}", [P, KT, P]) for j in range(2)]
            wh = [sb(f"wh{j}", [P, KT, P], F32R) for j in range(2)]
            wl = [sb(f"wl{j}", [P, KT, P], F32R) for j in range(2)]
            qs = [[sb(f"qs{b}{h}", [P, S], F32R) for h in range(2)] for b in range(2)]
            kh = [[sb(f"kh{b}{h}", [P, S], F32R) for h in range(2)] for b in range(2)]
            kl = [[sb(f"kl{b}{h}", [P, S], F32R) for h in range(2)] for b in range(2)]
            v = [sb(f"v{b}", [P, TB, 2, P], F32R) for b in range(2)]
            prob = [sb(f"prob{b}", [P, P * (b + 1)]) for b in range(TB)]
            pth = [sb(f"pth{j}", [P, HALF], F32R) for j in range(2)]
            ptl = [sb(f"ptl{j}", [P, HALF], F32R) for j in range(2)]
            stage = sb("stage", [P, HALF])
            sqt = sb("sqt", [P, HALF])
            cumf = [sb(f"cumf{h}", [P, S]) for h in range(2)]
            otmp = [sb(f"otmp{j}", [P, 2 * P]) for j in range(2)]
            ost = sb("ost", [P, S])
            tick = sb("tick", [P, BLOCKS])
            row_max = sb("row_max", [P, BLOCKS])
            den = sb("den", [P, BLOCKS])
            rden = sb("rden", [P, BLOCKS])
            scores = [ps(f"scores{j}") for j in range(2)]
            turn_ps = [ps(f"turn{j}", (P, HALF)) for j in range(2)]
            pv = ps("pv", (P, HALF))
            proj = ps("proj", (P, HALF))

            raw_in = [sem(f"raw_in{j}") for j in range(2)]
            w_high, w_low = sem("w_high"), sem("w_low")
            proj_done, staged, squared = sem("proj_done"), sem("staged"), sem("squared")
            inv_rms, qk_high, qk_low = sem("inv_rms"), sem("qk_high"), sem("qk_low")
            k_doubled = [sem(f"k_doubled{b}") for b in range(2)]
            turned, turned_h, turned_l = sem("turned"), sem("turned_h"), sem("turned_l")
            scored, score_used = sem("scored"), sem("score_used")
            absd, expd, lned, summed, scanned = (sem(n) for n in ("absd", "expd", "lned", "summed", "scanned"))
            sb_w, fx_exp, inv_den, fx_w = (sem(n) for n in ("sb_w", "fx_exp", "inv_den", "fx_w"))
            pv_done, half_out, o_done = sem("pv_done"), sem("half_out"), sem("o_done")
            o_stored = sem("o_stored")
            cum_in = sem("cum_in")
            fg, fgd, cum_stored = sem("fg"), sem("fgd"), sem("cum_stored")
            eps_set = sem("eps_set2")
            eps_t = sb("eps_t2", [P, 1])
            block = ctx.enter_context(nc.Block())

            def ordinal(i, target, c):
                return 8 + 12 * i + c + (6 if target == SB else 0)

            def qk_ordinal(i, target, c):
                return 4 + 8 * i + c + (4 if target == SB else 0)

            @block.sync
            def _(sp):
                def load(w, slot, col):
                    after(sp, w_low, w - 1)
                    sp.dma_start(raw[slot][:], win_v[:, :, bass.ds(col, P)]).then_inc(raw_in[slot], 16)

                def double_k(br, f):
                    sp.wait_ge(qk_low, f + 1)
                    sp.wait_ge(qk_high, f + 1)
                    for t in (kh, kl):
                        sp.dma_start(t[br][0][HD:P, :].bitcast(F32), t[br][0][0:HD, :].bitcast(F32)).then_inc(k_doubled[br], 16)
                        sp.dma_start(t[br][1][0:HD, :].bitcast(F32), t[br][1][HD:P, :].bitcast(F32)).then_inc(k_doubled[br], 16)

                def store(i, br):
                    sp.wait_ge(o_done, 16 * i + 8 * (br + 1))
                    sp.dma_start(o_dram[bass.ds((i + PAIRS * br) * P, P), :], ost[:]).then_inc(o_stored, 16)

                load(0, 0, OFF_FORGET)
                load(1, 1, 0)
                load(2, 0, H * HD)
                load(3, 1, 2 * H * HD)
                load(4, 0, OFF_FOX)
                load(5, 1, OFF_FOX + H * HD)
                sp.wait_ge(fgd, 4)
                sp.dma_start(cum_dram[:, :], prob[7][0:H, :]).then_inc(cum_stored, 16)
                double_k(SB, 3)
                sp.wait_ge(cum_stored, 16)

                def iteration(i, last):
                    w = 4 + 6 * i
                    load(w + 2, 0, OFF_FOX + 2 * H * HD + i * P)
                    after(sp, fx_w, 16 * i)
                    for h in range(2):
                        sp.dma_start(cumf[h][:], cum_dram[bass.ds(2 * i + h, 1), :].to_broadcast([P, S])).then_inc(cum_in, 16)
                    if not last:
                        load(w + 3, 1, (i + 1) * P)
                        load(w + 4, 0, H * HD + (i + 1) * P)
                    double_k(FX, qk_ordinal(i, FX, 3))
                    if not last:
                        load(w + 5, 1, 2 * H * HD + (i + 1) * P)
                    store(i, SB)
                    if not last:
                        load(w + 6, 0, OFF_FOX + (i + 1) * P)
                        load(w + 7, 1, OFF_FOX + H * HD + (i + 1) * P)
                        double_k(SB, qk_ordinal(i, SB, 3))
                    store(i, FX)
                with sp.Fori(0, PAIRS - 1) as i:
                    iteration(i, False)
                iteration(PAIRS - 1, True)
                sp.wait_ge(o_stored, 16 * 2 * PAIRS)

            @block.gpsimd
            def _(pool):
                def split(w, turn, slot):
                    pool.wait_ge(raw_in[slot], 16 * turn + 16)
                    after(pool, proj_done, 2 * w - 2)
                    pool.tensor_tensor(wh[slot][:], raw[slot][:], zero3, ALU.add).then_inc(w_high, 1)
                    pool.wait_ge(w_high, w + 1)
                    pool.tensor_tensor(wl[slot][:], raw[slot][:], wh[slot][:].bitcast(F32), ALU.subtract).then_inc(w_low, 1)
                for w in range(4):
                    split(w, w // 2, w % 2)
                with pool.Fori(0, PAIRS - 1) as i:
                    for c in range(6):
                        split(4 + 6 * i + c, 2 + 3 * i + c // 2, c % 2)
                for c in range(3):
                    i = PAIRS - 1
                    split(4 + 6 * i + c, 2 + 3 * i + c // 2, c % 2)

            @block.tensor
            def _(pe):
                def multiply(k, slot, w, c, part):
                    if part == 0:
                        pe.wait_ge(w_low, w + 1)
                        after(pe, staged, k)
                    t = slice(HALF * (c % 2), HALF * (c % 2) + HALF)
                    for n in range(12 * part, 12 * part + 12):
                        kt, kind = n // 3, n % 3
                        stat_ = wl if kind == 2 else wh
                        mov = hTl if kind == 1 else hTh
                        mm = pe.matmul(proj[:], stat_[slot][:, kt, :], mov[:, kt, t], start=(n == 0), stop=(n == 23))
                    if part == 1:
                        mm.then_inc(proj_done, 1)

                def turn_free(e, i):
                    after(pe, turned_h, PRO_EVENTS + EVENTS * i + max(e - 1, 0))
                    after(pe, turned_l, PRO_EVENTS + EVENTS * i + max(e - 1, 0))

                def turn_v(k, e):
                    pe.wait_ge(staged, k + 1)
                    for j in range(4):
                        mm = pe.transpose(turn_ps[e % 2][:, j * P:(j + 1) * P], stage[:, j * P:(j + 1) * P], ident[:])
                    mm.then_inc(turned, 1)

                for w in range(4):
                    for c in range(2):
                        k = 2 * w + c
                        multiply(k, w % 2, w, c, 0)
                        multiply(k, w % 2, w, c, 1)
                        if w == 3:
                            turn_v(k, c)

                def iteration(i, last):
                    groups, aux = SCHEDULES[last][:2]
                    pending = None

                    def weigh(g):
                        slot, h, br = g["g"] % 2, g["unit"] % 2, g["unit"] // 2
                        pe.wait_ge(turned_h, PRO_EVENTS + EVENTS * i + g["e"] + 1)
                        pe.wait_ge(turned_l, PRO_EVENTS + EVENTS * i + g["e"] + 1)
                        if g["j"] == 0:
                            after(pe, o_done, 16 * i + g["q"])
                        diag = g["j"] == g["p"]
                        for kb in range(2):
                            for pt in (pth, ptl):
                                first = g["j"] == 0 and kb == 0 and pt is pth
                                final = diag and kb == 1 and pt is ptl
                                if diag and kb == 1:
                                    mm = pe.matmul(pv[:, P:2 * P], v[br][:, 2 * g["j"] + kb, h, :],
                                                   pt[slot][:, 2 * P:3 * P], start=False, stop=final)
                                else:
                                    mm = pe.matmul(pv[:, 0:2 * P], v[br][:, 2 * g["j"] + kb, h, :],
                                                   pt[slot][:, 2 * P * kb:2 * P * kb + 2 * P], start=first, stop=False)
                        mm.then_inc(pv_done, 1)

                    def project(chunk):
                        if chunk:
                            target, c, part = chunk
                            tile = (0 if target == FX else 3) + c // 2
                            multiply(ordinal(i, target, c), tile % 2, 4 + 6 * i + tile, c, part)

                    for n in range(SLOTS):
                        if n < BLOCKS:
                            unit, b, h, br = block_of(n)
                            if b == 0 and h == 0:
                                if br == SB:
                                    pe.wait_ge(qk_low, 8 * i + 4)
                                    pe.wait_ge(qk_high, 8 * i + 4)
                                else:
                                    pe.wait_ge(qk_low, qk_ordinal(i, FX, 3) + 1)
                                    pe.wait_ge(qk_high, qk_ordinal(i, FX, 3) + 1)
                                pe.wait_ge(k_doubled[br], 64 * i + 64)
                            after(pe, score_used, BLOCKS * i + max(n - 1, 0))
                            width = P * (b + 1)
                            for c0 in range(0, width, HALF):
                                c1 = min(c0 + HALF, width)
                                o = scores[n % 2]
                                q_t = qs[br][h][:, b * P:(b + 1) * P]
                                pe.matmul(o[:, c0:c1], q_t, kh[br][h][:, c0:c1], start=True, stop=False)
                                mm = pe.matmul(o[:, c0:c1], q_t, kl[br][h][:, c0:c1], start=False, stop=(c1 < width))
                            mm = pe.matmul(o[:, width - P:width], identr[:], maskr[:, br, :], start=False, stop=True)
                            mm.then_inc(scored, 1)
                        chunk = chunk_at(n)
                        if last and chunk and chunk[0] == SB:
                            chunk = None
                        for g in groups[n]:
                            blk = 2 * g["q"] + 1
                            if blk < 2 * TB:
                                pe.wait_ge(sb_w, 16 * i + blk + 1)
                            else:
                                pe.wait_ge(fx_w, 16 * i + blk - 15)
                            turn_free(g["e"], i)
                            o, col = turn_ps[g["e"] % 2], 0
                            for kb in (2 * g["j"], 2 * g["j"] + 1):
                                for b in (2 * g["p"], 2 * g["p"] + 1):
                                    if kb <= b:
                                        mm = pe.transpose(o[:, col:col + P], prob[b][:, kb * P:(kb + 1) * P], ident[:])
                                        col += P
                            mm.then_inc(turned, 1)
                            if pending is not None:
                                weigh(pending)
                            pending = g
                            if g is groups[n][0]:
                                project(chunk)
                        if not groups[n]:
                            project(chunk)
                        a = aux[n]
                        if a:
                            turn_free(a["e"], i)
                            if a["c"] >= 4:
                                turn_v(ordinal(i, a["target"], a["c"]), a["e"])
                            else:
                                pe.wait_ge(squared, 4 * i + a["c"] + 1)
                                pe.matmul(turn_ps[a["e"] % 2][:], head_ones[:], sqt[:], start=True, stop=True).then_inc(turned, 1)
                    weigh(pending)
                with pe.Fori(0, PAIRS - 1) as i:
                    iteration(i, False)
                iteration(PAIRS - 1, True)

            @block.scalar
            def _(act):
                act.wait_ge(eps_set, 1)

                def stage_copy(k, c, scale, qk_before, e_before):
                    act.wait_ge(proj_done, k + 1)
                    if c in (0, 5):
                        after(act, turned, e_before)
                    else:
                        after(act, qk_low, qk_before)
                        after(act, qk_high, qk_before)
                    act.activation(stage[:], proj[:], ACT.Copy, scale=scale).then_inc(staged, 1)

                def split_high(target, c, ordi):
                    t = slice(HALF * (c % 2), HALF * (c % 2) + HALF)
                    dst = qs[target] if c < 2 else kh[target]
                    act.activation(dst[0][0:HD, t], stage[0:HD, :], ACT.Copy)
                    act.activation(dst[1][HD:P, t], stage[HD:P, :], ACT.Copy).then_inc(qk_high, 1)

                def v_high(target, c, e):
                    dst = v[target][:, 4 * (c % 2):4 * (c % 2) + 4, :, 0:HD]
                    for h in range(2):
                        a = act.activation(dst[:, :, h, :], turn_ps[e % 2][:].rearrange("p (t h c) -> p t h c", h=2, c=HD)[:, :, h, :], ACT.Copy)
                    a.then_inc(turned_h, 1)

                for c in range(2):
                    t = slice(HALF * c, HALF * c + HALF)
                    act.wait_ge(proj_done, c + 1)
                    act.activation(prob[6][0:H, 0:HALF] if c == 0 else prob[5][0:H, 0:HALF], proj[0:H, :], ACT.Identity, bias=bfc[:, 0:1]).then_inc(staged, 1)
                act.wait_ge(staged, 2)
                for c in range(2):
                    xg = prob[6][0:H, 0:HALF] if c == 0 else prob[5][0:H, 0:HALF]
                    act.activation(prob[7][0:H, HALF * c:HALF * c + HALF], xg, ACT.Abs).then_inc(fg, 1)
                act.wait_ge(fg, 2)
                act.activation(prob[7][0:H, :], prob[7][0:H, :], ACT.Exp, scale=-1.0).then_inc(fg, 1)
                act.wait_ge(fg, 3)
                act.activation(prob[7][0:H, :], prob[7][0:H, :], ACT.Ln, bias=1.0).then_inc(fg, 1)

                for c in range(6):
                    k = 2 + c
                    stage_copy(k, c, HD ** -0.5 if c < 2 else 1.0, c if c else 0, 1 if c == 5 else 0)
                    act.wait_ge(staged, k + 1)
                    if c < 4:
                        split_high(SB, c, c)
                    else:
                        act.wait_ge(turned, c - 4 + 1)
                        v_high(SB, c, c - 4)

                def iteration(i, last):
                    groups, aux = SCHEDULES[last][:2]
                    e0 = PRO_EVENTS + EVENTS * i

                    def group_high(g):
                        w = (4 if g["j"] < g["p"] else 3) * P
                        act.wait_ge(turned, e0 + g["e"] + 1)
                        after(act, pv_done, NGROUPS * i + max(g["g"] - 1, 0))
                        act.activation(pth[g["g"] % 2][:, 0:w], turn_ps[g["e"] % 2][:, 0:w], ACT.Copy).then_inc(turned_h, 1)

                    for n in range(SLOTS + 1):
                        gs = groups[n] if n < SLOTS else []
                        if n >= 6 and n % 2 == 0:
                            q = (n - 6) // 2
                            h = (2 * q // TB) % 2
                            act.wait_ge(pv_done, NGROUPS * i + last_group_of_pair(groups, q) + 1)
                            after(act, o_done, 16 * i + max(q - 1, 0))
                            src, dst = (slice(HD, P), slice(0, HD)) if h == 0 else (slice(0, HD), slice(HD, P))
                            act.activation(otmp[q % 2][dst, :], pv[src, 0:2 * P], ACT.Copy).then_inc(half_out, 1)
                        copied = copied_at(n)
                        if copied and not (last and copied[0] == SB):
                            target, c = copied
                            k = ordinal(i, target, c)
                            e_before = 0
                            if c == 5:
                                e_before = e0 + v_event(aux, target, 4) + 1
                            elif c == 0:
                                if target == FX:
                                    e_before = e0
                                else:
                                    e_before = e0 + v_event(aux, FX, 5) + 1
                            stage_copy(k, c, HD ** -0.5 if (target == SB and c < 2) else 1.0,
                                       qk_ordinal(i, target, min(c, 4)), e_before)
                            if target == FX and c < 4:
                                act.wait_ge(staged, k + 1)
                                act.activation(sqt[:], stage[:], ACT.Square).then_inc(squared, 1)
                        fin = copied_at(n - 1) if n else None
                        if fin and last and fin[0] == SB:
                            fin = None
                        fin_e = aux[n - 1]["e"] if fin and aux[n - 1] else None
                        if fin and fin[0] == FX and fin[1] < 4:
                            act.wait_ge(turned, e0 + fin_e + 1)
                            act.activation(sqt[:], turn_ps[fin_e % 2][:], ACT.Ln, scale=1.0 / HD, bias=eps_t[:, 0:1]).then_inc(turned_h, 1)
                            act.wait_ge(turned_h, e0 + fin_e + 1)
                            act.activation(sqt[:], sqt[:], ACT.Exp, scale=-0.5).then_inc(inv_rms, 1)
                        if fin and fin[1] >= 4:
                            act.wait_ge(turned, e0 + fin_e + 1)
                            after(act, pv_done, NGROUPS * i + (0 if fin[0] == FX else NGROUPS // 2))
                            v_high(fin[0], fin[1], fin_e)
                        if n < BLOCKS:
                            unit, b, h, br = block_of(n)
                        if n < 2 * TB:
                            pr, s = prob[b], scores[n % 2]
                            act.wait_ge(scored, BLOCKS * i + n + 1)
                            after(act, turned, e0 + (last_event_of_pair(groups, n // 2 - 4) + 1 if n >= TB else 0))
                            if n == 5:
                                act.wait_ge(cum_stored, 16)
                            act.activation(pr[:], s[:, 0:P * (b + 1)], ACT.Abs).then_inc(absd, 1)
                            act.wait_ge(absd, 16 * i + n + 1)
                            act.activation(pr[:], pr[:], ACT.Exp, scale=-1.0).then_inc(expd, 1)
                            if gs:
                                group_high(gs[0])
                            act.wait_ge(expd, 16 * i + n + 1)
                            act.activation(pr[:], pr[:], ACT.Ln, bias=1.0).then_inc(lned, 1)
                            for g in gs[1:]:
                                group_high(g)
                        else:
                            for g in gs:
                                group_high(g)
                        if 1 <= n <= 2 * TB:
                            pb = prob[(n - 1) % TB]
                            act.wait_ge(score_used, BLOCKS * i + n)
                            act.activation(pb[:], pb[:], ACT.Exp).then_inc(sb_w, 1)
                        if 2 * TB <= n < BLOCKS:
                            act.wait_ge(score_used, BLOCKS * i + n + 1)
                            act.activation(prob[b][:], prob[b][:], ACT.Exp, scale=-1.0, bias=row_max[:, n:n + 1],
                                           accum_out=den[:, n:n + 1]).then_inc(fx_exp, 1)
                        if fin:
                            target, c = fin
                            if c < 4:
                                if c == 0:
                                    after(act, scored, BLOCKS * i + (0 if target == FX else 16))
                                if target == FX:
                                    act.wait_ge(turned_l, e0 + fin_e + 1)
                                else:
                                    act.wait_ge(staged, ordinal(i, target, c) + 1)
                                split_high(target, c, qk_ordinal(i, target, c))
                with act.Fori(0, PAIRS - 1) as i:
                    iteration(i, False)
                iteration(PAIRS - 1, True)

            @block.vector
            def _(dve):
                dve.memset(eps_t[:], EPS).then_inc(eps_set, 1)

                def split_low(target, c):
                    t = slice(HALF * (c % 2), HALF * (c % 2) + HALF)
                    hi = qs[target] if c < 2 else kh[target]
                    lo = qs[target] if c < 2 else kl[target]
                    a, b = slice(0, HD), slice(HD, P)
                    dve.tensor_tensor(lo[0][b if c < 2 else a, t], stage[a, :], hi[0][a, t].bitcast(F32), ALU.subtract)
                    dve.tensor_tensor(lo[1][a if c < 2 else b, t], stage[b, :], hi[1][b, t].bitcast(F32), ALU.subtract).then_inc(qk_low, 1)

                def v_low(target, c, e):
                    t = slice(4 * (c % 2), 4 * (c % 2) + 4)
                    for h in range(2):
                        d = dve.tensor_tensor(v[target][:, t, h, HD:P],
                                              turn_ps[e % 2][:].rearrange("p (t h c) -> p t h c", h=2, c=HD)[:, :, h, :],
                                              v[target][:, t, h, 0:HD].bitcast(F32), ALU.subtract)
                    d.then_inc(turned_l, 1)

                for c in range(2):
                    xg = prob[6][0:H, 0:HALF] if c == 0 else prob[5][0:H, 0:HALF]
                    dve.wait_ge(fg, 2)
                    dve.tensor_scalar(xg, xg, 0.0, None, ALU.min).then_inc(fgd, 1)
                dve.wait_ge(fg, 4)
                dve.wait_ge(fgd, 2)
                dve.tensor_tensor_scan(prob[7][0:H, 0:HALF], prob[7][0:H, 0:HALF], prob[6][0:H, 0:HALF], 0.0, ALU.add, ALU.subtract).then_inc(fgd, 1)
                dve.wait_ge(fgd, 3)
                dve.tensor_tensor_scan(prob[7][0:H, HALF:S], prob[7][0:H, HALF:S], prob[5][0:H, 0:HALF], prob[7][0:H, HALF - 1:HALF], ALU.add, ALU.subtract).then_inc(fgd, 1)
                for c in range(6):
                    if c < 4:
                        dve.wait_ge(qk_high, c + 1)
                        split_low(SB, c)
                    else:
                        dve.wait_ge(turned_h, c - 4 + 1)
                        v_low(SB, c, c - 4)

                def iteration(i, last):
                    groups, aux = SCHEDULES[last][:2]
                    e0 = PRO_EVENTS + EVENTS * i

                    def group_low(g):
                        w = (4 if g["j"] < g["p"] else 3) * P
                        dve.wait_ge(turned_h, e0 + g["e"] + 1)
                        dve.tensor_tensor(ptl[g["g"] % 2][:, 0:w], turn_ps[g["e"] % 2][:, 0:w],
                                          pth[g["g"] % 2][:, 0:w].bitcast(F32), ALU.subtract).then_inc(turned_l, 1)

                    for n in range(SLOTS + 1):
                        gs = groups[n] if n < SLOTS else []
                        if n >= 6 and n % 2 == 0:
                            q = (n - 6) // 2
                            h, br, p = (2 * q // TB) % 2, q // 8, q % (TB // 2)
                            r = slice(0, HD) if h == 0 else slice(HD, P)
                            dve.wait_ge(half_out, 16 * i + q + 1)
                            if q % 8 == 0:
                                after(dve, o_stored, 32 * i + 16 * br)
                            dve.tensor_tensor(ost[r, 2 * P * p:2 * P * (p + 1)], pv[r, 0:2 * P], otmp[q % 2][r, :], ALU.add).then_inc(o_done, 1)
                        if n < BLOCKS:
                            unit, b, h, br = block_of(n)
                        if 2 * TB < n <= BLOCKS:
                            m = n - 1
                            f = m - 2 * TB
                            dve.wait_ge(fx_exp, 16 * i + f + 1)
                            dve.reciprocal(rden[:, m:m + 1], den[:, m:m + 1]).then_inc(inv_den, 1)
                            dve.wait_ge(inv_den, 16 * i + f + 1)
                            dve.tensor_scalar(prob[m % TB][:], prob[m % TB][:], rden[:, m:m + 1], None, ALU.mult).then_inc(fx_w, 1)
                        fin = copied_at(n - 1) if n else None
                        if fin and last and fin[0] == SB:
                            fin = None
                        fin_e = aux[n - 1]["e"] if fin and aux[n - 1] else None

                        def finish_aux():
                            if not fin:
                                return
                            target, c = fin
                            if c >= 4:
                                dve.wait_ge(turned_h, e0 + fin_e + 1)
                                v_low(target, c, fin_e)
                            elif target == FX:
                                dve.wait_ge(inv_rms, 4 * i + c + 1)
                                dve.scalar_tensor_tensor(out=stage[:], in0=stage[:], scalar=gqk[:, 2:3] if c < 2 else gqk[:, 1:2],
                                                         in1=sqt[:], op0=ALU.mult, op1=ALU.mult).then_inc(turned_l, 1)

                        if n < 2 * TB:
                            pr, s, w = prob[b], scores[n % 2], P * (b + 1)
                            dve.wait_ge(lned, 16 * i + n + 1)
                            dve.scalar_tensor_tensor(out=pr[:], in0=s[:, 0:w], scalar=0.0, in1=pr[:], op0=ALU.max, op1=ALU.add).then_inc(summed, 1)
                            finish_aux()
                            if gs:
                                group_low(gs[0])
                            dve.wait_ge(summed, 16 * i + n + 1)
                            dve.tensor_tensor_scan(pr[:, ::-1], pr[:, ::-1], pr[:, ::-1], 0.0, ALU.add, ALU.bypass).then_inc(scanned, 1)
                            for g in gs[1:]:
                                group_low(g)
                            dve.wait_ge(scanned, 16 * i + n + 1)
                            dve.tensor_tensor(pr[:], s[:, 0:w], pr[:], ALU.subtract).then_inc(score_used, 1)
                        elif n < BLOCKS:
                            w = P * (b + 1)
                            dve.wait_ge(scored, BLOCKS * i + n + 1)
                            dve.wait_ge(turned, e0 + last_event_of_pair(groups, n // 2 - 4) + 1)
                            if b == 0 and h == 0:
                                dve.wait_ge(cum_in, 32 * i + 32)
                            dve.memset(tick[:, n:n + 1], 0.0)
                            dve.tensor_tensor_reduce(out=prob[b][:], in0=scores[n % 2][:, 0:w], in1=cumf[h][:, 0:w], scale=-1.0,
                                                     scalar=3.0e38, op0=ALU.add, op1=ALU.min,
                                                     accum_out=row_max[:, n:n + 1]).then_inc(score_used, 1)
                            finish_aux()
                            for g in gs:
                                group_low(g)
                        else:
                            for g in gs:
                                group_low(g)
                        if fin and fin[1] < 4:
                            dve.wait_ge(qk_high, qk_ordinal(i, *fin) + 1)
                            split_low(*fin)
                with dve.Fori(0, PAIRS - 1) as i:
                    iteration(i, False)
                iteration(PAIRS - 1, True)

        mixing = whole.enter_context(ExitStack())
        sbm, _, _ = maker(mixing)
        mix = sbm("mix", [P, KT, S])
        with ExitStack() as ctx:
            sb, ps, sem = maker(ctx)
            raw = [sb(f"raw3{j}", [P, KT, P]) for j in range(2)]
            wh = [sb(f"wh3{j}", [P, KT, P], F32R) for j in range(2)]
            wl = [sb(f"wl3{j}", [P, KT, P], F32R) for j in range(2)]
            oh = sb("oh", [P, KT, S], F32R)
            ol = sb("ol", [P, KT, S], F32R)
            sig = [sb(f"sig{b}", [P, S]) for b in range(2)]
            gate_ps = [ps(f"gate{b}") for b in range(2)]
            y_ps = [ps(f"y{b}") for b in range(2)]
            o_in = [sem(f"o_in{j}") for j in range(2)]
            o_high, o_low = sem("o_high"), sem("o_low")
            raw_in = [sem(f"raw3_in{j}") for j in range(2)]
            w_high, w_low, w_used = sem("w3_high"), sem("w3_low"), sem("w3_used")
            gated, y_done = sem("gate_done"), sem("y_done")
            sig_done, mulled, mixed = sem("sig_done"), sem("mulled"), sem("mixed")
            block = ctx.enter_context(nc.Block())

            @block.sync
            def _(sp):
                def gate(m, b, slot):
                    sp.dma_start(raw[slot][:], win_v[:, :, bass.ds(OFF_GATE + D * b + m * P, P)]).then_inc(raw_in[slot], 16)

                def branches(m, slot):
                    sp.dma_start(raw[slot][:, 0:4, :], wosb_v[:, :, bass.ds(m * P, P)]).then_inc(raw_in[slot], 16)
                    sp.dma_start(raw[slot][:, 4:8, :], wofx_v[:, :, bass.ds(m * P, P)]).then_inc(raw_in[slot], 16)

                def weights(m, j):
                    sp.wait_ge(w_low, 3 * m - 1)
                    gate(m, 0, j)
                    sp.wait_ge(w_low, 3 * m + 1)
                    gate(m, 1, 1 - j)
                    branches(m, j)
                gate(0, 0, 0)
                gate(0, 1, 1)
                for k in range(KT):
                    after(sp, o_low, k - 1)
                    sp.dma_start(sig[k % 2][:], o_dram[k * P:(k + 1) * P, :]).then_inc(o_in[k % 2], 16)
                    if k == 0:
                        sp.wait_ge(w_low, 1)
                        branches(0, 0)
                weights(1, 1)
                with sp.Fori(1, KT // 2) as i:
                    weights(2 * i, 0)
                    weights(2 * i + 1, 1)

            @block.gpsimd
            def _(pool):
                def split(m, i, j, t):
                    w, slot = 3 * m + t, (3 * j + t) % 2
                    count = {0: {(0, 0): 1, (0, 2): 3, (1, 1): 4}, 1: {(0, 1): 1, (1, 0): 2, (1, 2): 4}}[slot][(j, t)]
                    pool.wait_ge(raw_in[slot], 16 * (4 * i + count))
                    after(pool, w_used, w - 1)
                    pool.tensor_tensor(wh[slot][:], raw[slot][:], zero3, ALU.add).then_inc(w_high, 1)
                    pool.wait_ge(w_high, w + 1)
                    pool.tensor_tensor(wl[slot][:], raw[slot][:], wh[slot][:].bitcast(F32), ALU.subtract).then_inc(w_low, 1)
                for t in range(6):
                    split(t // 3, 0, t // 3, t % 3)
                with pool.Fori(1, KT // 2) as i:
                    for t in range(6):
                        split(2 * i + t // 3, i, t // 3, t % 3)

            @block.tensor
            def _(pe):
                def product(o, slot, kts, first_kt, mh, ml):
                    for kt in kts:
                        for stat_, mov in ((wh, mh), (wh, ml), (wl, mh)):
                            for c in range(2):
                                mm = pe.matmul(o[:, HALF * c:HALF * c + HALF], stat_[slot][:, kt, :],
                                               mov[:, kt, HALF * c:HALF * c + HALF],
                                               start=(kt == kts[0] and stat_ is wh and mov is mh),
                                               stop=(kt == kts[-1] and stat_ is wl))
                    return mm

                def output_tile(m, j):
                    for b in range(2):
                        pe.wait_ge(w_low, 3 * m + b + 1)
                        after(pe, sig_done, 2 * m + b - 1)
                        product(gate_ps[b], (3 * j + b) % 2, range(KT), 0, hTh, hTl).then_inc(w_used, 1)
                    pe.wait_ge(w_low, 3 * m + 3)
                    if isinstance(m, int) and m == 0:
                        pe.wait_ge(o_low, KT)
                        pe.wait_ge(o_high, KT)
                    after(pe, mulled, 2 * m)
                    for b in range(2):
                        mm = product(y_ps[b], (3 * j + 2) % 2, range(4 * b, 4 * b + 4), 0, oh, ol)
                    mm.then_inc(w_used, 1)
                output_tile(0, 0)
                output_tile(1, 1)
                with pe.Fori(1, KT // 2) as i:
                    output_tile(2 * i, 0)
                    output_tile(2 * i + 1, 1)

            @block.scalar
            def _(act):
                for k in range(KT):
                    act.wait_ge(o_in[k % 2], 16 * (k // 2) + 16)
                    act.activation(oh[:, k, :], sig[k % 2][:], ACT.Copy).then_inc(o_high, 1)

                def output_tile(m):
                    for b in range(2):
                        act.wait_ge(w_used, 3 * m + b + 1)
                        if isinstance(m, int) and m == 0:
                            act.wait_ge(o_low, KT)
                        after(act, mixed, m)
                        act.activation(sig[b][:], gate_ps[b][:], ACT.Sigmoid,
                                       bias=cols[:, 4, bass.ds(m + b * KT, 1)]).then_inc(sig_done, 1)
                output_tile(0)
                with act.Fori(1, KT) as m:
                    output_tile(m)

            @block.vector
            def _(dve):
                for k in range(KT):
                    dve.wait_ge(o_high, k + 1)
                    dve.tensor_tensor(ol[:, k, :], sig[k % 2][:], oh[:, k, :].bitcast(F32), ALU.subtract).then_inc(o_low, 1)

                def output_tile(m):
                    dve.wait_ge(w_used, 3 * m + 3)
                    for b in range(2):
                        dve.wait_ge(sig_done, 2 * m + b + 1)
                        dve.tensor_tensor(sig[b][:], sig[b][:], y_ps[b][:], ALU.mult).then_inc(mulled, 1)
                    dve.wait_ge(mulled, 2 * m + 2)
                    dve.tensor_tensor(mix[:, bass.ds(m, 1), :].rearrange("p a b -> p (a b)"), sig[0][:], sig[1][:], ALU.add).then_inc(mixed, 1)
                with dve.Fori(0, KT) as m:
                    output_tile(m)

        with ExitStack() as ctx:
            sb, ps, sem = maker(ctx)
            woh = sb("woh", [P, KT, D], F32R)
            wol = sb("wol", [P, KT, D], F32R)
            mh = [sb(f"mh{j}", [P, KT, P], F32R) for j in range(2)]
            ml = [sb(f"ml{j}", [P, KT, P], F32R) for j in range(2)]
            gain = sb("gain4", [P, D])
            xt = [sb(f"xt4{j}", [P, D]) for j in range(2)]
            xn = [sb(f"xn4{j}", [P, D]) for j in range(2)]
            stat = sb("stat4", [P, 3, 2])
            proj = [ps(f"outp{j}") for j in range(2)]
            turned = [ps(f"turned4{j}") for j in range(2)]
            w_in_s = [sem(f"w4_in{j}") for j in range(2)]
            w_high, w_low = sem("w4_high"), sem("w4_low")
            x_in = [sem(f"x4_in{j}") for j in range(2)]
            gain_in, x2_out = sem("gain4_in"), [sem(f"x2_out{j}") for j in range(2)]
            m_high, m_low, proj_done, x2_done = sem("m_high"), sem("m_low"), sem("proj4"), sem("x2_done")
            sq_done, root_done, inv_done, xn_done = (sem(n + "4") for n in ("sq", "root", "inv", "xn"))
            tr_done, hi_done, lo_done = sem("tr4"), sem("hi4"), sem("lo4")
            eps_set = sem("eps_set4")
            eps_t = sb("eps_t4", [P, 1])
            block = ctx.enter_context(nc.Block())

            @block.sync
            def _(sp):
                for k in range(KT):
                    after(sp, w_low, k - 1)
                    sp.dma_start(xn[k % 2][:], w_out[0, k * P:(k + 1) * P, :]).then_inc(w_in_s[k % 2], 16)
                sp.dma_start(gain[:], g_ffn.to_broadcast([P, D])).then_inc(gain_in, 16)

                def load(t, j, turn):
                    after(sp, xn_done, t - 1)
                    after(sp, x2_out[j], 16 * turn)
                    sp.dma_start(xt[j][:], x[0, bass.ds(t * P, P), :]).then_inc(x_in[j], 16)

                def store(t, j):
                    sp.wait_ge(x2_done, t + 1)
                    sp.dma_start(x2_dram[bass.ds(t * P, P), :], xt[j][:]).then_inc(x2_out[j], 16)
                load(0, 0, 0)
                load(1, 1, 0)
                with sp.Fori(0, TB // 2 - 1) as i:
                    for j in range(2):
                        store(2 * i + j, j)
                    for j in range(2):
                        load(2 * i + 2 + j, j, i + 1)
                for j in range(2):
                    store(TB - 2 + j, j)
                for j in range(2):
                    sp.wait_ge(x2_out[j], 16 * (TB // 2))

            @block.tensor
            def _(pe):
                def project(t, j):
                    pe.wait_ge(m_low, t + 1)
                    after(pe, x2_done, t - 1)
                    for kt in range(KT):
                        if isinstance(t, int) and t == 0:
                            pe.wait_ge(w_low, kt + 1)
                        for stat_, mov in ((mh, woh), (mh, wol), (ml, woh)):
                            for c in range(2):
                                mm = pe.matmul(proj[j][:, HALF * c:HALF * c + HALF], stat_[j][:, kt, :],
                                               mov[:, kt, HALF * c:HALF * c + HALF],
                                               start=(kt == 0 and stat_ is mh and mov is woh),
                                               stop=(kt == KT - 1 and stat_ is ml))
                    mm.then_inc(proj_done, 1)

                def turn(t, j):
                    pe.wait_ge(xn_done, t + 1)
                    after(pe, hi_done, t - 1)
                    after(pe, lo_done, t - 1)
                    for k in range(KT):
                        mm = pe.transpose(turned[j][:, k * P:(k + 1) * P], xn[j][:, k * P:(k + 1) * P], ident[:])
                    mm.then_inc(tr_done, 1)
                project(0, 0)
                project(1, 1)
                turn(0, 0)
                with pe.Fori(1, TB // 2) as i:
                    project(2 * i, 0)
                    turn(2 * i - 1, 1)
                    project(2 * i + 1, 1)
                    turn(2 * i, 0)
                turn(TB - 1, 1)

            @block.scalar
            def _(act):
                for k in range(KT):
                    act.wait_ge(w_in_s[k % 2], 16 * (k // 2) + 16)
                    act.activation(woh[:, k, :], xn[k % 2][:], ACT.Copy).then_inc(w_high, 1)
                    if k < 2:
                        act.activation(mh[k][:], mix[:, :, k * P:(k + 1) * P], ACT.Copy).then_inc(m_high, 1)
                act.wait_ge(eps_set, 1)
                act.wait_ge(w_low, KT)

                def stats(t, j):
                    act.wait_ge(x2_done, t + 1)
                    after(act, tr_done, t - 1)
                    act.activation(xn[j][:], xt[j][:], ACT.Square, accum_out=stat[:, 0, j:j + 1]).then_inc(sq_done, 1)
                    act.wait_ge(sq_done, t + 1)
                    after(act, inv_done, t - 1)
                    act.activation(stat[:, 1, j:j + 1], stat[:, 0, j:j + 1], ACT.Sqrt, scale=1.0 / D, bias=eps_t[:, 0:1]).then_inc(root_done, 1)

                def mix_high(t, j):
                    act.wait_ge(proj_done, t - 1)
                    act.activation(mh[j][:], mix[:, :, bass.ds(t * P, P)], ACT.Copy).then_inc(m_high, 1)

                def high(t, j):
                    act.wait_ge(tr_done, t + 1)
                    act.activation(hTh[:, :, bass.ds(t * P, P)], turned[j][:].rearrange("p (k t) -> p k t", k=KT), ACT.Copy).then_inc(hi_done, 1)
                stats(0, 0)
                mix_high(2, 0)
                with act.Fori(0, TB // 2 - 2) as i:
                    stats(2 * i + 1, 1)
                    mix_high(2 * i + 3, 1)
                    high(2 * i, 0)
                    stats(2 * i + 2, 0)
                    mix_high(2 * i + 4, 0)
                    high(2 * i + 1, 1)
                stats(TB - 3, 1)
                mix_high(TB - 1, 1)
                high(TB - 4, 0)
                stats(TB - 2, 0)
                high(TB - 3, 1)
                stats(TB - 1, 1)
                high(TB - 2, 0)
                high(TB - 1, 1)

            @block.vector
            def _(dve):
                dve.memset(eps_t[:], EPS).then_inc(eps_set, 1)
                for k in range(KT):
                    dve.wait_ge(w_high, k + 1)
                    dve.tensor_tensor(wol[:, k, :], xn[k % 2][:], woh[:, k, :].bitcast(F32), ALU.subtract).then_inc(w_low, 1)
                    if k < 2:
                        dve.wait_ge(m_high, k + 1)
                        dve.tensor_tensor(ml[k][:], mix[:, :, k * P:(k + 1) * P], mh[k][:].bitcast(F32), ALU.subtract).then_inc(m_low, 1)
                dve.wait_ge(gain_in, 16)

                def norm(t, j, turn):
                    dve.wait_ge(proj_done, t + 1)
                    dve.wait_ge(x_in[j], 16 * turn + 16)
                    dve.tensor_tensor(xt[j][:], proj[j][:], xt[j][:], ALU.add).then_inc(x2_done, 1)
                    dve.wait_ge(root_done, t + 1)
                    after(dve, xn_done, t - 1)
                    dve.reciprocal(stat[:, 2, j:j + 1], stat[:, 1, j:j + 1]).then_inc(inv_done, 1)
                    dve.wait_ge(inv_done, t + 1)
                    dve.scalar_tensor_tensor(out=xn[j][:], in0=xt[j][:], scalar=stat[:, 2, j:j + 1], in1=gain[:],
                                             op0=ALU.mult, op1=ALU.mult).then_inc(xn_done, 1)

                def mix_low(t, j):
                    dve.wait_ge(m_high, t + 1)
                    dve.tensor_tensor(ml[j][:], mix[:, :, bass.ds(t * P, P)], mh[j][:].bitcast(F32), ALU.subtract).then_inc(m_low, 1)

                def low(t, j):
                    dve.wait_ge(hi_done, t + 1)
                    dve.tensor_tensor(hTl[:, :, bass.ds(t * P, P)], turned[j][:].rearrange("p (k t) -> p k t", k=KT),
                                      hTh[:, :, bass.ds(t * P, P)].bitcast(F32), ALU.subtract).then_inc(lo_done, 1)
                norm(0, 0, 0)
                mix_low(2, 0)
                with dve.Fori(0, TB // 2 - 2) as i:
                    norm(2 * i + 1, 1, i)
                    mix_low(2 * i + 3, 1)
                    low(2 * i, 0)
                    norm(2 * i + 2, 0, i + 1)
                    mix_low(2 * i + 4, 0)
                    low(2 * i + 1, 1)
                norm(TB - 3, 1, TB // 2 - 2)
                mix_low(TB - 1, 1)
                low(TB - 4, 0)
                norm(TB - 2, 0, TB // 2 - 1)
                low(TB - 3, 1)
                norm(TB - 1, 1, TB // 2 - 1)
                low(TB - 2, 0)
                low(TB - 1, 1)
        mixing.close()

        sb, _, _ = maker(whole)
        act_t = sb("act_t", [P, FT, S])
        with ExitStack() as ctx:
            sb, ps, sem = maker(ctx)
            raw = [sb(f"raw5{j}", [P, KT, P]) for j in range(2)]
            wh = [sb(f"wh5{j}", [P, KT, P], F32R) for j in range(2)]
            wl = [sb(f"wl5{j}", [P, KT, P], F32R) for j in range(2)]
            u = [[sb(f"u{j}{c}", [P, S]) for c in range(2)] for j in range(2)]
            u_ps = [[ps(f"u_ps{j}{c}") for c in range(2)] for j in range(2)]
            raw_in = [sem(f"raw5_in{c}") for c in range(2)]
            w_high, w_low, u_done = sem("w5_high"), sem("w5_low"), sem("u_done")
            tap2, tap1, tap0, silu_done, act_done = (sem(n) for n in ("tap2", "tap1", "tap0", "silu_done", "act_done"))
            block = ctx.enter_context(nc.Block())

            @block.sync
            def _(sp):
                for c in range(2):
                    sp.dma_start(raw[c][:], wup_v[:, :, c * FF:c * FF + P]).then_inc(raw_in[c], 16)
                with sp.Fori(1, FT) as f:
                    for c in range(2):
                        sp.wait_ge(w_low, 2 * f + c - 1)
                        sp.dma_start(raw[c][:], wup_v[:, :, bass.ds(f * P + c * FF, P)]).then_inc(raw_in[c], 16)

            @block.gpsimd
            def _(pool):
                with pool.Fori(0, FT) as f:
                    for c in range(2):
                        pool.wait_ge(w_high, 2 * f + c + 1)
                        pool.tensor_tensor(wl[c][:], raw[c][:], wh[c][:].bitcast(F32), ALU.subtract).then_inc(w_low, 1)

            @block.tensor
            def _(pe):
                def tile(f, j):
                    for c in range(2):
                        pe.wait_ge(w_low, 2 * f + c + 1)
                        after(pe, tap0, 2 * f + c - 3)
                        for kt in range(KT):
                            for stat_, mov in ((wh, hTh), (wh, hTl), (wl, hTh)):
                                for h in range(2):
                                    mm = pe.matmul(u_ps[j][c][:, HALF * h:HALF * h + HALF], stat_[c][:, kt, :],
                                                   mov[:, kt, HALF * h:HALF * h + HALF],
                                                   start=(kt == 0 and stat_ is wh and mov is hTh),
                                                   stop=(kt == KT - 1 and stat_ is wl))
                        mm.then_inc(u_done, 1)
                tile(0, 0)
                tile(1, 1)
                with pe.Fori(1, FT // 2) as i:
                    tile(2 * i, 0)
                    tile(2 * i + 1, 1)

            @block.scalar
            def _(act):
                def w_split(f, c):
                    act.wait_ge(raw_in[c], 16 * f + 16)
                    after(act, u_done, 2 * f + c - 1)
                    act.activation(wh[c][:], raw[c][:], ACT.Copy).then_inc(w_high, 1)

                def evacuate(f, j, c):
                    act.wait_ge(u_done, 2 * f + c + 1)
                    after(act, act_done, f - 1)
                    act.activation(u[j][c][:], u_ps[j][c][:], ACT.Identity, scale=cols[:, 2, bass.ds(f + c * FT, 1)],
                                   bias=cols[:, 3, bass.ds(f + c * FT, 1)]).then_inc(tap2, 1)

                def silu(f, j):
                    act.wait_ge(tap0, 2 * f + 1)
                    act.activation(u[j][0][:], u[j][0][:], ACT.Silu).then_inc(silu_done, 1)

                def tile(f, j, more):
                    evacuate(f, j, 0)
                    if more:
                        w_split(f + 1, 0)
                    evacuate(f, j, 1)
                    if more:
                        w_split(f + 1, 1)
                    silu(f, j)
                w_split(0, 0)
                w_split(0, 1)
                tile(0, 0, True)
                tile(1, 1, True)
                with act.Fori(1, FT // 2 - 1) as i:
                    tile(2 * i, 0, True)
                    tile(2 * i + 1, 1, True)
                tile(FT - 2, 0, True)
                tile(FT - 1, 1, False)

            @block.vector
            def _(dve):
                def tile(f, j):
                    for c in range(2):
                        dve.wait_ge(tap2, 2 * f + c + 1)
                        dve.scalar_tensor_tensor(out=u[j][c][:, 1:S], in0=u_ps[j][c][:, 0:S - 1], scalar=cols[:, 1, bass.ds(f + c * FT, 1)],
                                                 in1=u[j][c][:, 1:S], op0=ALU.mult, op1=ALU.add).then_inc(tap1, 1)
                        dve.wait_ge(tap1, 2 * f + c + 1)
                        dve.scalar_tensor_tensor(out=u[j][c][:, 2:S], in0=u_ps[j][c][:, 0:S - 2], scalar=cols[:, 0, bass.ds(f + c * FT, 1)],
                                                 in1=u[j][c][:, 2:S], op0=ALU.mult, op1=ALU.add).then_inc(tap0, 1)
                    dve.wait_ge(silu_done, f + 1)
                    dve.wait_ge(tap0, 2 * f + 2)
                    dve.tensor_tensor(act_t[:, bass.ds(f, 1), :].rearrange("p a b -> p (a b)"), u[j][0][:], u[j][1][:], ALU.mult).then_inc(act_done, 1)
                with dve.Fori(0, FT // 2) as i:
                    tile(2 * i, 0)
                    tile(2 * i + 1, 1)

        with ExitStack() as ctx:
            sb, ps, sem = maker(ctx)
            raw = [sb(f"raw6{j}", [P, D]) for j in range(2)]
            wh = [sb(f"wh6{j}", [P, D], F32R) for j in range(2)]
            wl = [sb(f"wl6{j}", [P, D], F32R) for j in range(2)]
            ah = [sb(f"ah{j}", [P, HALF], F32R) for j in range(2)]
            al = [sb(f"al{j}", [P, HALF], F32R) for j in range(2)]
            x2 = [sb(f"x2{t}", [P, D]) for t in range(4)]
            acc = [ps(f"acc{t}") for t in range(4)]
            raw_in = [sem(f"raw6_in{j}") for j in range(2)]
            w_high, w_low, a_high, a_low, used = sem("w6_high"), sem("w6_low"), sem("a_high"), sem("a_low"), sem("used6")
            x2_in = [sem(f"x2_in{t}") for t in range(4)]
            summed, stored = sem("summed6"), [sem(f"stored{t}") for t in range(4)]
            block = ctx.enter_context(nc.Block())
            QT = HALF // P

            @block.sync
            def _(sp):
                for half in range(2):
                    for j in range(2):
                        after(sp, w_low, j - 1 + half * FT)
                        sp.dma_start(raw[j][:], w_down[0, j * P:(j + 1) * P, :]).then_inc(raw_in[j], 16)
                    with sp.Fori(1, FT // 2) as i:
                        for j in range(2):
                            sp.wait_ge(w_low, 2 * i + j - 1 + half * FT)
                            sp.dma_start(raw[j][:], w_down[0, bass.ds((2 * i + j) * P, P), :]).then_inc(raw_in[j], 16)

            @block.gpsimd
            def _(pool):
                for half in range(2):
                    for t in range(QT):
                        if half:
                            pool.wait_ge(stored[t], 16)
                        pool.dma_start(x2[t][:], x2_dram[(QT * half + t) * P:(QT * half + t + 1) * P, :]).then_inc(x2_in[t], 16)
                    with pool.Fori(0, FT // 2) as i:
                        for j in range(2):
                            g = 2 * i + j + half * FT
                            pool.wait_ge(w_high, g + 1)
                            pool.tensor_tensor(wl[j][:], raw[j][:], wh[j][:].bitcast(F32), ALU.subtract).then_inc(w_low, 1)

            @block.tensor
            def _(pe):
                def step(half, f, j, first, last):
                    g = half * FT + f
                    pe.wait_ge(w_low, g + 1)
                    pe.wait_ge(a_low, g + 1)
                    for t in range(QT):
                        if first and half:
                            pe.wait_ge(summed, t + 1)
                        for stat_, mov in ((ah, wh), (ah, wl), (al, wh)):
                            for c in range(2):
                                mm = pe.matmul(acc[t][:, HALF * c:HALF * c + HALF], stat_[j][:, t * P:(t + 1) * P],
                                               mov[j][:, HALF * c:HALF * c + HALF],
                                               start=(first and stat_ is ah and mov is wh), stop=(last and stat_ is al))
                    mm.then_inc(used, 1)
                for half in range(2):
                    step(half, 0, 0, True, False)
                    step(half, 1, 1, False, False)
                    with pe.Fori(1, FT // 2 - 1) as i:
                        step(half, 2 * i, 0, False, False)
                        step(half, 2 * i + 1, 1, False, False)
                    step(half, FT - 2, 0, False, False)
                    step(half, FT - 1, 1, False, True)

            @block.scalar
            def _(act):
                def step(half, f, j, turn):
                    g = half * FT + f
                    act.wait_ge(raw_in[j], 16 * turn + 16)
                    after(act, used, g - 1)
                    act.activation(wh[j][:], raw[j][:], ACT.Copy).then_inc(w_high, 1)
                    act.activation(ah[j][:], act_t[:, bass.ds(f, 1), HALF * half:HALF * half + HALF].rearrange("p a b -> p (a b)"),
                                   ACT.Copy).then_inc(a_high, 1)

                def out_store(half, t):
                    act.wait_ge(summed, QT * half + t + 1)
                    act.dma_start(out[0, (QT * half + t) * P:(QT * half + t + 1) * P, :], x2[t][:]).then_inc(stored[t], 16)
                step(0, 0, 0, 0)
                step(0, 1, 1, 0)
                with act.Fori(1, FT // 2) as i:
                    for j in range(2):
                        step(0, 2 * i + j, j, i)
                step(1, 0, 0, FT // 2)
                step(1, 1, 1, FT // 2)
                for t in range(QT):
                    out_store(0, t)
                with act.Fori(1, FT // 2) as i:
                    for j in range(2):
                        step(1, 2 * i + j, j, FT // 2 + i)
                for t in range(QT):
                    out_store(1, t)
                for t in range(QT):
                    act.wait_ge(stored[t], 32)

            @block.vector
            def _(dve):
                def step(half, f, j):
                    g = half * FT + f
                    dve.wait_ge(a_high, g + 1)
                    dve.tensor_tensor(al[j][:], act_t[:, bass.ds(f, 1), HALF * half:HALF * half + HALF].rearrange("p a b -> p (a b)"),
                                      ah[j][:].bitcast(F32), ALU.subtract).then_inc(a_low, 1)

                def sums(half):
                    dve.wait_ge(used, (half + 1) * FT)
                    for t in range(QT):
                        dve.wait_ge(x2_in[t], 16 * half + 16)
                        dve.tensor_tensor(x2[t][:], acc[t][:], x2[t][:], ALU.add).then_inc(summed, 1)
                with dve.Fori(0, FT // 2) as i:
                    for j in range(2):
                        step(0, 2 * i + j, j)
                sums(0)
                with dve.Fori(0, FT // 2) as i:
                    for j in range(2):
                        step(1, 2 * i + j, j)
                sums(1)


_INS = ["x", "g_mix", "w_in", "b_forget", "b_gate", "g_q", "g_k", "w_o_sb", "w_o_fox", "w_out",
        "g_ffn", "w_up", "conv_w", "conv_b", "w_down"]


def kernel(**inputs):
    import numpy as np
    import concourse.bacc as bacc
    from concourse.bass_utils import run_bass_kernel_spmd

    nc = bacc.Bacc("TRN2", target_bir_lowering=False, num_devices=1)
    arrays, args = {}, []
    for name in _INS:
        a = np.ascontiguousarray(inputs[name])
        arrays[f"in_{name}"] = a
        args.append(nc.dram_tensor(f"in_{name}", a.shape, mybir.dt.from_np(a.dtype), kind="ExternalInput").ap())
    out = nc.dram_tensor("out", (1, S, D), F32, kind="ExternalOutput").ap()
    build(nc, *args, out)
    r = run_bass_kernel_spmd(nc, [arrays], core_ids=[0])
    return r.results[0]["out"]
```

```python
from contextlib import ExitStack

import concourse.bass as bass
from concourse import mybir

F32 = mybir.dt.float32
F32R = mybir.dt.float32r
ALU = mybir.AluOpType
ACT = mybir.ActivationFunctionType

P = 128
S = 1024
D = 1024
H = 8
HD = 64
FF = 2816
EPS = 1e-6
NEG = -1e30
KT = D // P
TB = S // P
HALF = 512
FT = FF // P
PAIRS = H // 2
OFF_FOX = 3 * H * HD
OFF_FORGET = 2 * OFF_FOX
OFF_GATE = OFF_FORGET + H
SB, FX = 0, 1


def after(eng, sem, value):
    if isinstance(value, int) and value <= 0:
        return
    eng.wait_ge(sem, value)


def since(eng, sem, value):
    eng.wait_ge(sem, value + 1)


BLOCKS = 4 * TB
PAIR_ORDER = (1, 3, 0, 2)
SLOTS = BLOCKS + 4
CHUNK_MMS = 3 * KT
CHUNKS = [dict(target=(FX, SB)[k // 6], c=k % 6, start=3 * k, slots=3 if k < 11 else 2) for k in range(12)]


def block_of(n):
    return n // TB, 2 * PAIR_ORDER[n % TB // 2] + n % 2, (n // TB) % 2, n // (2 * TB)


def chunk_at(n):
    for k in CHUNKS:
        if 0 <= n - k["start"] < k["slots"]:
            per = CHUNK_MMS // k["slots"]
            return k["target"], k["c"], per * (n - k["start"]), per * (n - k["start"] + 1)
    return None


def copied_at(n):
    for k in CHUNKS:
        if n == k["start"] + k["slots"]:
            return k["target"], k["c"]
    return None


def make_schedule(last):
    groups, aux, e, g = [[] for _ in range(SLOTS)], [None] * SLOTS, 0, 0
    for n in range(SLOTS):
        k = n - n % 2
        if k >= 4:
            q = (k - 4) // 2
            p = PAIR_ORDER[q % (TB // 2)]
            mine = range(p + 1)
            split = (p + 2) // 2
            for j in (mine[:split] if n % 2 == 0 else mine[split:]):
                groups[n].append(dict(e=e, g=g, q=q, p=p, j=j, unit=(2 * q) // TB))
                e, g = e + 1, g + 1
        done = copied_at(n)
        if done and (done[1] >= 4 or done[0] == FX) and not (last and done[0] == SB):
            aux[n] = dict(e=e, c=done[1], target=done[0])
            e += 1
    return groups, aux, e, g


SCHEDULES = {last: make_schedule(last) for last in (False, True)}
EVENTS, NGROUPS = SCHEDULES[False][2:]
assert EVENTS % 2 == 0 and NGROUPS % 2 == 0
PRO_EVENTS = 2


def v_event(aux, target, c):
    return next(a["e"] for a in aux if a and a["target"] == target and a["c"] == c)


def last_event_of_pair(groups, q):
    return max(g["e"] for gs in groups for g in gs if g["q"] == q)


def last_group_of_pair(groups, q):
    return max(g["g"] for gs in groups for g in gs if g["q"] == q)


def build(nc, x, g_mix, w_in, b_forget, b_gate, g_q, g_k, w_o_sb, w_o_fox, w_out, g_ffn, w_up,
          conv_w, conv_b, w_down, out):
    o_dram = nc.dram_tensor("attn_out_t", (2 * PAIRS * P, S), F32, kind="Internal").ap()
    cum_dram = nc.dram_tensor("neg_cum_forget", (H, S), F32, kind="Internal").ap()
    x2_dram = nc.dram_tensor("mid_residual", (S, D), F32, kind="Internal").ap()
    win_v = w_in[0].rearrange("(k p) n -> p k n", p=P)
    wup_v = w_up[0].rearrange("(k p) n -> p k n", p=P)
    wosb_v = w_o_sb[0].rearrange("(k p) n -> p k n", p=P)
    wofx_v = w_o_fox[0].rearrange("(k p) n -> p k n", p=P)

    with ExitStack() as whole:
        def maker(ctx):
            def sb(name, shape, dt=F32):
                return ctx.enter_context(nc.sbuf_tensor(name, shape, dt))

            def ps(name, shape=(P, S)):
                return ctx.enter_context(nc.psum_tensor(name, list(shape), F32))

            def sem(name):
                return ctx.enter_context(nc.semaphore(name))
            return sb, ps, sem

        sb, ps_whole, sem = maker(whole)
        raw = [sb(f"raw{j}", [P, KT, P]) for j in range(2)]
        wh = [sb(f"wh{j}", [P, KT, P], F32R) for j in range(2)]
        wl = [sb(f"wl{j}", [P, KT, P], F32R) for j in range(2)]
        flat = "p k n -> p (k n)"
        ring = {p: ([sem(f"raw{p}_in{j}") for j in range(2)], sem(f"w{p}_high"), sem(f"w{p}_low")) for p in (2, 3, 4, 5, 6)}
        proj_done = sem("proj_done")
        ident = sb("ident", [P, P])
        head_ones = sb("head_ones", [P, P])
        mask_f = sb("mask_f", [P, 2, P])
        maskr = sb("maskr", [P, 2, P], F32R)
        identr = sb("identr", [P, P], F32R)
        zero = sb("zero", [P, 1])
        zero3 = zero[:].rearrange("p (a b) -> p a b", a=1).to_broadcast([P, KT, P])
        cols = sb("cols", [P, 5, FT * 2])
        gqk = sb("gqk", [P, 4])
        bfc = sb("bfc", [H, 1])

        projecting = whole.enter_context(ExitStack())
        proj = projecting.enter_context(nc.psum_tensor("proj", [P, HALF], F32))
        early = whole.enter_context(ExitStack())
        sbh, _, _ = maker(early)
        hTh = sbh("hTh", [P, KT, S], F32R)
        hTl = sbh("hTl", [P, KT, S], F32R)

        def project_chunk(pe, o, slot, c, lo, hi):
            for n in range(lo, hi):
                kt, kind = n // 3, n % 3
                stat_ = wl if kind == 2 else wh
                mov = hTl if kind == 1 else hTh
                mm = pe.matmul(o[:], stat_[slot][:, kt, :], mov[:, kt, HALF * c:HALF * c + HALF],
                               start=(n == 0), stop=(n == CHUNK_MMS - 1))
            return mm

        with ExitStack() as ctx:
            sb, ps, sem = maker(ctx)
            gain = sb("gain", [P, D])
            rows = sb("rows", [2 * FT, 5, P])
            xt = [sb(f"xt{j}", [P, D]) for j in range(2)]
            xn = [sb(f"xn{j}", [P, D]) for j in range(2)]
            stat = sb("stat", [P, 3, 2])
            turned = [ps(f"turned{j}") for j in range(2)]
            turned_c = ps("turned_c", (P, 512))
            gain_in, consts_in, small_in = sem("gain_in"), sem("consts_in"), sem("small_in")
            x_in = [sem(f"x_in{j}") for j in range(2)]
            const0, const1, const2 = sem("const0"), sem("const1"), sem("const2")
            sq_done, root_done, inv_done, xn_done = (sem(n) for n in ("sq", "root", "inv", "xn"))
            tr_done, hi_done, lo_done = sem("tr1"), sem("hi1"), sem("lo1")
            colt_done, col_done, gq_done = sem("colt"), sem("col"), sem("gq8")
            eps_set = sem("eps_set")
            eps_t = sb("eps_t", [P, 1])
            eps_col = eps_t[:, 0:1]
            next_in, next_high, next_low = ring[2]
            block = ctx.enter_context(nc.Block())

            @block.sync
            def _(sp):
                def load(t, j):
                    after(sp, xn_done, t - 1)
                    sp.dma_start(xt[j][:], x[0, bass.ds(t * P, P), :]).then_inc(x_in[j], 16)
                load(0, 0)
                sp.dma_start(gain[:], g_mix.to_broadcast([P, D])).then_inc(gain_in, 16)
                load(1, 1)
                sp.dma_start(raw[0][:], win_v[:, :, OFF_FORGET:OFF_FORGET + P]).then_inc(next_in[0], 16)
                for c in range(3):
                    sp.dma_start(rows[0:2 * FT, c, :], conv_w[0, c].rearrange("(a b) -> a b", b=P)).then_inc(consts_in, 16)
                sp.dma_start(rows[0:2 * FT, 3, :], conv_b[0].rearrange("(a b) -> a b", b=P)).then_inc(consts_in, 16)
                sp.dma_start(rows[0:16, 4, :], b_gate[0].rearrange("(a b) -> a b", b=P)).then_inc(consts_in, 16)
                with nc.allow_non_contiguous_dma(reason="a few gains, one to a partition"):
                    for half in range(2):
                        for c, g in ((0, g_q), (1, g_k)):
                            sp.dma_start(gqk[HD * half:HD * half + HD, c:c + 1], g.rearrange("a b -> b a")).then_inc(small_in, 16)
                    sp.dma_start(bfc[:], b_forget.rearrange("a b -> b a")).then_inc(small_in, 16)
                with sp.Fori(1, TB // 2) as i:
                    for j in range(2):
                        load(2 * i + j, j)
                sp.dma_start(raw[1][:], win_v[:, :, 0:P]).then_inc(next_in[1], 16)

            @block.gpsimd
            def _(pool):
                pool.memset(ident[:], 0.0).then_inc(const0, 1)
                pool.memset(mask_f[:], 0.0).then_inc(const0, 1)
                pool.memset(zero[:], 0.0).then_inc(const0, 1)
                pool.memset(head_ones[:], 0.0).then_inc(const0, 1)
                pool.wait_ge(const0, 4)
                pool.affine_select(out=ident[:], in_=ident[:], compare_op=ALU.not_equal, fill=1.0,
                                   base=0, pattern=[[-1, P]], channel_multiplier=1).then_inc(const1, 1)
                pool.affine_select(out=mask_f[:, SB, :], in_=mask_f[:, SB, :], compare_op=ALU.is_gt, fill=NEG,
                                   base=0, pattern=[[-1, P]], channel_multiplier=1).then_inc(const1, 1)
                pool.affine_select(out=mask_f[:, FX, :], in_=mask_f[:, FX, :], compare_op=ALU.is_ge, fill=NEG,
                                   base=0, pattern=[[-1, P]], channel_multiplier=1).then_inc(const1, 1)
                for half in range(2):
                    pool.wait_ge(const1, 3 + half)
                    r = slice(HD * half, HD * half + HD)
                    pool.memset(head_ones[r, r], 1.0).then_inc(const1, 1)
                pool.wait_ge(const1, 5)
                pool.tensor_copy(maskr[:], mask_f[:]).then_inc(const2, 1)
                pool.tensor_copy(identr[:], ident[:]).then_inc(const2, 1)
                for j in range(2):
                    pool.wait_ge(next_in[j], 16)
                    pool.tensor_tensor(wh[j][:], raw[j][:], zero3, ALU.add).then_inc(next_high, 1)
                    pool.wait_ge(next_high, j + 1)
                    pool.tensor_tensor(wl[j][:], raw[j][:], wh[j][:].bitcast(F32), ALU.subtract).then_inc(next_low, 1)

            @block.scalar
            def _(act):
                def stats(t, j):
                    act.wait_ge(x_in[j], (t // 2 + 1) * 16)
                    after(act, tr_done, t - 1)
                    act.activation(xn[j][:], xt[j][:], ACT.Square, accum_out=stat[:, 0, j:j + 1]).then_inc(sq_done, 1)
                    act.wait_ge(sq_done, t + 1)
                    after(act, inv_done, t - 1)
                    act.activation(stat[:, 1, j:j + 1], stat[:, 0, j:j + 1], ACT.Sqrt, scale=1.0 / D, bias=eps_col).then_inc(root_done, 1)

                def high(t, j):
                    act.wait_ge(tr_done, t + 1)
                    act.activation(hTh[:, :, bass.ds(t * P, P)], turned[j][:].rearrange("p (k t) -> p k t", k=KT), ACT.Copy).then_inc(hi_done, 1)
                act.wait_ge(eps_set, 1)
                stats(0, 0)
                stats(1, 1)
                high(0, 0)
                with act.Fori(1, TB // 2) as i:
                    stats(2 * i, 0)
                    high(2 * i - 1, 1)
                    stats(2 * i + 1, 1)
                    high(2 * i, 0)
                high(TB - 1, 1)

            @block.vector
            def _(dve):
                dve.memset(eps_t[:], EPS).then_inc(eps_set, 1)
                dve.wait_ge(gain_in, 16)

                def norm(t, j):
                    dve.wait_ge(root_done, t + 1)
                    after(dve, xn_done, t - 1)
                    dve.reciprocal(stat[:, 2, j:j + 1], stat[:, 1, j:j + 1]).then_inc(inv_done, 1)
                    dve.wait_ge(inv_done, t + 1)
                    dve.scalar_tensor_tensor(out=xn[j][:], in0=xt[j][:], scalar=stat[:, 2, j:j + 1], in1=gain[:],
                                             op0=ALU.mult, op1=ALU.mult).then_inc(xn_done, 1)

                def low(t, j):
                    dve.wait_ge(hi_done, t + 1)
                    dve.tensor_tensor(hTl[:, :, bass.ds(t * P, P)], turned[j][:].rearrange("p (k t) -> p k t", k=KT),
                                      hTh[:, :, bass.ds(t * P, P)].bitcast(F32), ALU.subtract).then_inc(lo_done, 1)
                norm(0, 0)
                norm(1, 1)
                low(0, 0)
                with dve.Fori(1, TB // 2) as i:
                    norm(2 * i, 0)
                    low(2 * i - 1, 1)
                    norm(2 * i + 1, 1)
                    low(2 * i, 0)
                low(TB - 1, 1)
                dve.wait_ge(colt_done, 1)
                dve.tensor_copy(cols[:].rearrange("p a b -> p (a b)")[:, 0:8 * FT + 16], turned_c[:, 0:8 * FT + 16]).then_inc(col_done, 1)
                dve.wait_ge(small_in, 80)
                dve.tensor_scalar(gqk[:, 2:3], gqk[:, 0:1], HD ** -0.5, None, ALU.mult).then_inc(gq_done, 1)

            @block.tensor
            def _(pe):
                def turn(t, j):
                    pe.wait_ge(xn_done, t + 1)
                    after(pe, hi_done, t - 1)
                    after(pe, lo_done, t - 1)
                    for k in range(KT):
                        mm = pe.transpose(turned[j][:, k * P:(k + 1) * P], xn[j][:, k * P:(k + 1) * P], ident[:])
                    mm.then_inc(tr_done, 1)
                pe.wait_ge(const1, 5)
                turn(0, 0)
                turn(1, 1)
                with pe.Fori(1, TB // 2 - 1) as i:
                    turn(2 * i, 0)
                    turn(2 * i + 1, 1)
                pe.wait_ge(hi_done, TB // 2)
                pe.wait_ge(lo_done, TB // 2)
                pe.wait_ge(next_low, 1)
                project_chunk(pe, proj, 0, 0, 0, KT)
                turn(TB - 2, 0)
                project_chunk(pe, proj, 0, 0, KT, 2 * KT)
                turn(TB - 1, 1)
                project_chunk(pe, proj, 0, 0, 2 * KT, 3 * KT).then_inc(proj_done, 1)
                pe.wait_ge(consts_in, 80)
                for c in range(5):
                    n = 2 * FT if c < 4 else 16
                    mm = pe.transpose(turned_c[:, 2 * FT * c:2 * FT * c + n], rows[0:n, c, :], ident[0:n, 0:n])
                mm.then_inc(colt_done, 1)

        with ExitStack() as ctx:
            sb, ps, sem = maker(ctx)
            qs = [[sb(f"qs{b}{h}", [P, S], F32R) for h in range(2)] for b in range(2)]
            kh = [[sb(f"kh{b}{h}", [P, S], F32R) for h in range(2)] for b in range(2)]
            kl = [[sb(f"kl{b}{h}", [P, S], F32R) for h in range(2)] for b in range(2)]
            v = [sb(f"v{b}", [P, TB, 2, P], F32R) for b in range(2)]
            prob = [sb(f"prob{b}", [P, P * (b + 1)]) for b in range(TB)]
            pth = [sb(f"pth{j}", [P, HALF], F32R) for j in range(2)]
            ptl = [sb(f"ptl{j}", [P, HALF], F32R) for j in range(2)]
            stage = sb("stage", [P, HALF])
            sqt = sb("sqt", [P, HALF])
            cumf = [sb(f"cumf{h}", [P, S]) for h in range(2)]
            otmp = [sb(f"otmp{j}", [P, 2 * P]) for j in range(2)]
            ost = sb("ost", [P, S])
            tick = sb("tick", [P, BLOCKS])
            row_max = sb("row_max", [P, BLOCKS])
            den = sb("den", [P, BLOCKS])
            rden = sb("rden", [P, BLOCKS])
            scores = [ps(f"scores{j}") for j in range(2)]
            turn_ps = [ps(f"turn{j}", (P, HALF)) for j in range(2)]
            pv = ps("pv", (P, HALF))

            raw_in, w_high, w_low = ring[2]
            next_in, next_high, next_low = ring[3]
            staged, squared = sem("staged"), sem("squared")
            inv_rms, qk_high, qk_low = sem("inv_rms"), sem("qk_high"), sem("qk_low")
            k_doubled = [sem(f"k_doubled{b}") for b in range(2)]
            turned, turned_h, turned_l = sem("turned"), sem("turned_h"), sem("turned_l")
            scored, score_used = sem("scored"), sem("score_used")
            absd, expd, lned, summed, scanned = (sem(n) for n in ("absd", "expd", "lned", "summed", "scanned"))
            sb_w, fx_exp, inv_den, fx_w = (sem(n) for n in ("sb_w", "fx_exp", "inv_den", "fx_w"))
            pv_done, half_out, o_done = sem("pv_done"), sem("half_out"), sem("o_done")
            o_stored = sem("o_stored")
            cum_in = sem("cum_in")
            fg, fgd, cum_stored = sem("fg"), sem("fgd"), sem("cum_stored")
            eps_set = sem("eps_set2")
            eps_t = sb("eps_t2", [P, 1])
            block = ctx.enter_context(nc.Block())

            def ordinal(i, target, c):
                return 8 + 12 * i + c + (6 if target == SB else 0)

            def qk_ordinal(i, target, c):
                return 4 + 8 * i + c + (4 if target == SB else 0)

            @block.sync
            def _(sp):
                def load(w, slot, col):
                    after(sp, w_low, w - 1)
                    sp.dma_start(raw[slot][:], win_v[:, :, bass.ds(col, P)]).then_inc(raw_in[slot], 16)

                def double_k(br, f):
                    sp.wait_ge(qk_low, f + 1)
                    sp.wait_ge(qk_high, f + 1)
                    for t in (kh, kl):
                        sp.dma_start(t[br][0][HD:P, :].bitcast(F32), t[br][0][0:HD, :].bitcast(F32)).then_inc(k_doubled[br], 16)
                        sp.dma_start(t[br][1][0:HD, :].bitcast(F32), t[br][1][HD:P, :].bitcast(F32)).then_inc(k_doubled[br], 16)

                def store(i, br):
                    since(sp, o_done, 16 * i + 8 * (br + 1))
                    sp.dma_start(o_dram[bass.ds((i + PAIRS * br) * P, P), :], ost[:]).then_inc(o_stored, 16)

                load(2, 0, H * HD)
                load(3, 1, 2 * H * HD)
                load(4, 0, OFF_FOX)
                load(5, 1, OFF_FOX + H * HD)
                sp.wait_ge(fgd, 4)
                sp.dma_start(cum_dram[:, :], prob[7][0:H, :]).then_inc(cum_stored, 16)
                double_k(SB, 3)
                sp.wait_ge(cum_stored, 16)

                def iteration(i, last):
                    w = 4 + 6 * i
                    load(w + 2, 0, OFF_FOX + 2 * H * HD + i * P)
                    since(sp, fx_w, 16 * i)
                    for h in range(2):
                        sp.dma_start(cumf[h][:], cum_dram[bass.ds(2 * i + h, 1), :].to_broadcast([P, S])).then_inc(cum_in, 16)
                    if not last:
                        load(w + 3, 1, (i + 1) * P)
                        load(w + 4, 0, H * HD + (i + 1) * P)
                    double_k(FX, qk_ordinal(i, FX, 3))
                    if last:
                        for j in range(2):
                            sp.wait_ge(w_low, w + 2 + (1 - j))
                            sp.dma_start(raw[j][:], win_v[:, :, OFF_GATE + D * j:OFF_GATE + D * j + P]).then_inc(next_in[j], 16)
                    if not last:
                        load(w + 5, 1, 2 * H * HD + (i + 1) * P)
                    store(i, SB)
                    if not last:
                        load(w + 6, 0, OFF_FOX + (i + 1) * P)
                        load(w + 7, 1, OFF_FOX + H * HD + (i + 1) * P)
                        double_k(SB, qk_ordinal(i, SB, 3))
                    store(i, FX)
                with sp.Fori(0, PAIRS - 1) as i:
                    iteration(i, False)
                iteration(PAIRS - 1, True)
                since(sp, o_stored, 16 * 2 * PAIRS)

            @block.gpsimd
            def _(pool):
                def split(w, turn, slot):
                    pool.wait_ge(raw_in[slot], 16 * turn + 16)
                    after(pool, proj_done, 2 * w - 2)
                    pool.tensor_tensor(wh[slot][:], raw[slot][:], zero3, ALU.add).then_inc(w_high, 1)
                    pool.wait_ge(w_high, w + 1)
                    pool.tensor_tensor(wl[slot][:], raw[slot][:], wh[slot][:].bitcast(F32), ALU.subtract).then_inc(w_low, 1)
                for w in range(2, 4):
                    split(w, w // 2, w % 2)
                with pool.Fori(0, PAIRS - 1) as i:
                    for c in range(6):
                        split(4 + 6 * i + c, 2 + 3 * i + c // 2, c % 2)
                tiles = 4 + 6 * (PAIRS - 1) + 3
                for w in range(tiles - 3, tiles):
                    split(w, w // 2, w % 2)
                for j in range(2):
                    pool.wait_ge(next_in[j], 16)
                    pool.wait_ge(proj_done, 2 * tiles)
                    pool.tensor_tensor(wh[j][:], raw[j][:], zero3, ALU.add).then_inc(next_high, 1)
                    pool.wait_ge(next_high, j + 1)
                    pool.tensor_tensor(wl[j][:], raw[j][:], wh[j][:].bitcast(F32), ALU.subtract).then_inc(next_low, 1)

            @block.tensor
            def _(pe):
                def multiply(k, slot, w, c, lo, hi):
                    if lo == 0:
                        pe.wait_ge(w_low, w + 1)
                        after(pe, staged, k)
                    mm = project_chunk(pe, proj, slot, c % 2, lo, hi)
                    if hi == CHUNK_MMS:
                        mm.then_inc(proj_done, 1)

                def turn_free(e, i):
                    after(pe, turned_h, PRO_EVENTS + EVENTS * i + max(e - 1, 0))
                    after(pe, turned_l, PRO_EVENTS + EVENTS * i + max(e - 1, 0))

                def turn_v(k, e):
                    pe.wait_ge(staged, k + 1)
                    for j in range(4):
                        mm = pe.transpose(turn_ps[e % 2][:, j * P:(j + 1) * P], stage[:, j * P:(j + 1) * P], ident[:])
                    mm.then_inc(turned, 1)

                for w in range(4):
                    for c in range(2):
                        k = 2 * w + c
                        if k:
                            multiply(k, w % 2, w, c, 0, CHUNK_MMS)
                        if w == 3:
                            turn_v(k, c)

                def iteration(i, last):
                    groups, aux = SCHEDULES[last][:2]
                    pending = None

                    def weigh(g):
                        slot, h, br = g["g"] % 2, g["unit"] % 2, g["unit"] // 2
                        pe.wait_ge(turned_h, PRO_EVENTS + EVENTS * i + g["e"] + 1)
                        pe.wait_ge(turned_l, PRO_EVENTS + EVENTS * i + g["e"] + 1)
                        if g["j"] == 0:
                            since(pe, o_done, 16 * i + g["q"])
                        diag = g["j"] == g["p"]
                        for kb in range(2):
                            for pt in (pth, ptl):
                                first = g["j"] == 0 and kb == 0 and pt is pth
                                final = diag and kb == 1 and pt is ptl
                                if diag and kb == 1:
                                    mm = pe.matmul(pv[:, P:2 * P], v[br][:, 2 * g["j"] + kb, h, :],
                                                   pt[slot][:, 2 * P:3 * P], start=False, stop=final)
                                else:
                                    mm = pe.matmul(pv[:, 0:2 * P], v[br][:, 2 * g["j"] + kb, h, :],
                                                   pt[slot][:, 2 * P * kb:2 * P * kb + 2 * P], start=first, stop=False)
                        mm.then_inc(pv_done, 1)

                    def score(n):
                        if n < BLOCKS:
                            unit, b, h, br = block_of(n)
                            if n % (2 * TB) == 0:
                                if br == SB:
                                    pe.wait_ge(qk_low, 8 * i + 4)
                                    pe.wait_ge(qk_high, 8 * i + 4)
                                else:
                                    pe.wait_ge(qk_low, qk_ordinal(i, FX, 3) + 1)
                                    pe.wait_ge(qk_high, qk_ordinal(i, FX, 3) + 1)
                                pe.wait_ge(k_doubled[br], 64 * i + 64)
                            since(pe, score_used, BLOCKS * i + max(n - 1, 0))
                            width = P * (b + 1)
                            for c0 in range(0, width, HALF):
                                c1 = min(c0 + HALF, width)
                                o = scores[n % 2]
                                q_t = qs[br][h][:, b * P:(b + 1) * P]
                                pe.matmul(o[:, c0:c1], q_t, kh[br][h][:, c0:c1], start=True, stop=False)
                                mm = pe.matmul(o[:, c0:c1], q_t, kl[br][h][:, c0:c1], start=False, stop=(c1 < width))
                            mm = pe.matmul(o[:, width - P:width], identr[:], maskr[:, br, :], start=False, stop=True)
                            mm.then_inc(scored, 1)

                    def project(chunk, part, parts):
                        if chunk:
                            target, c, lo, hi = chunk
                            tile = (0 if target == FX else 3) + c // 2
                            cut = [lo + (hi - lo) * p // parts for p in (part, part + 1)]
                            multiply(ordinal(i, target, c), tile % 2, 4 + 6 * i + tile, c, *cut)

                    for n in range(SLOTS):
                        chunk = chunk_at(n)
                        if last and chunk and chunk[0] == SB:
                            chunk = None
                        for g in groups[n]:
                            blk = 2 * g["q"] + 1
                            if blk < 2 * TB:
                                pe.wait_ge(sb_w, 16 * i + blk + 1)
                            else:
                                since(pe, fx_w, 16 * i + blk - 15)
                            turn_free(g["e"], i)
                            o, col = turn_ps[g["e"] % 2], 0
                            for kb in (2 * g["j"], 2 * g["j"] + 1):
                                for b in (2 * g["p"], 2 * g["p"] + 1):
                                    if kb <= b:
                                        mm = pe.transpose(o[:, col:col + P], prob[b][:, kb * P:(kb + 1) * P], ident[:])
                                        col += P
                            mm.then_inc(turned, 1)
                            if pending is not None:
                                weigh(pending)
                            pending = g
                            if g is groups[n][0]:
                                score(n)
                            project(chunk, groups[n].index(g), len(groups[n]))
                        if not groups[n]:
                            score(n)
                            project(chunk, 0, 1)
                        a = aux[n]
                        if a:
                            turn_free(a["e"], i)
                            if a["c"] >= 4:
                                turn_v(ordinal(i, a["target"], a["c"]), a["e"])
                            else:
                                pe.wait_ge(squared, 4 * i + a["c"] + 1)
                                pe.matmul(turn_ps[a["e"] % 2][:], head_ones[:], sqt[:], start=True, stop=True).then_inc(turned, 1)
                    weigh(pending)
                with pe.Fori(0, PAIRS - 1) as i:
                    iteration(i, False)
                iteration(PAIRS - 1, True)

            @block.scalar
            def _(act):
                act.preload_act_table_set("natural_log_exp_and_others")
                act.wait_ge(eps_set, 1)

                def stage_copy(k, c, scale, qk_before, e_before):
                    act.wait_ge(proj_done, k + 1)
                    if c in (0, 5):
                        after(act, turned, e_before)
                    else:
                        after(act, qk_low, qk_before)
                        after(act, qk_high, qk_before)
                    act.activation(stage[:], proj[:], ACT.Copy, scale=scale).then_inc(staged, 1)

                def split_high(target, c, ordi):
                    t = slice(HALF * (c % 2), HALF * (c % 2) + HALF)
                    dst = qs[target] if c < 2 else kh[target]
                    act.activation(dst[0][0:HD, t], stage[0:HD, :], ACT.Copy)
                    act.activation(dst[1][HD:P, t], stage[HD:P, :], ACT.Copy).then_inc(qk_high, 1)

                def v_high(target, c, e):
                    dst = v[target][:, 4 * (c % 2):4 * (c % 2) + 4, :, 0:HD]
                    for h in range(2):
                        a = act.activation(dst[:, :, h, :], turn_ps[e % 2][:].rearrange("p (t h c) -> p t h c", h=2, c=HD)[:, :, h, :], ACT.Copy)
                    a.then_inc(turned_h, 1)

                for c in range(2):
                    t = slice(HALF * c, HALF * c + HALF)
                    act.wait_ge(proj_done, c + 1)
                    act.activation(prob[6][0:H, 0:HALF] if c == 0 else prob[5][0:H, 0:HALF], proj[0:H, :], ACT.Identity, bias=bfc[:, 0:1]).then_inc(staged, 1)
                act.wait_ge(staged, 2)
                for c in range(2):
                    xg = prob[6][0:H, 0:HALF] if c == 0 else prob[5][0:H, 0:HALF]
                    act.activation(prob[7][0:H, HALF * c:HALF * c + HALF], xg, ACT.Abs).then_inc(fg, 1)
                act.wait_ge(fg, 2)
                act.activation(prob[7][0:H, :], prob[7][0:H, :], ACT.Exp, scale=-1.0).then_inc(fg, 1)
                act.wait_ge(fg, 3)
                act.activation(prob[7][0:H, :], prob[7][0:H, :], ACT.Ln, bias=1.0).then_inc(fg, 1)

                for c in range(6):
                    k = 2 + c
                    stage_copy(k, c, HD ** -0.5 if c < 2 else 1.0, c if c else 0, 1 if c == 5 else 0)
                    act.wait_ge(staged, k + 1)
                    if c < 4:
                        split_high(SB, c, c)
                    else:
                        act.wait_ge(turned, c - 4 + 1)
                        v_high(SB, c, c - 4)

                def iteration(i, last):
                    groups, aux = SCHEDULES[last][:2]
                    e0 = PRO_EVENTS + EVENTS * i

                    def group_high(g):
                        w = (4 if g["j"] < g["p"] else 3) * P
                        act.wait_ge(turned, e0 + g["e"] + 1)
                        since(act, pv_done, NGROUPS * i + max(g["g"] - 1, 0))
                        act.activation(pth[g["g"] % 2][:, 0:w], turn_ps[g["e"] % 2][:, 0:w], ACT.Copy).then_inc(turned_h, 1)

                    for n in range(SLOTS + 1):
                        gs = groups[n] if n < SLOTS else []
                        copied = copied_at(n)
                        if copied and not (last and copied[0] == SB):
                            target, c = copied
                            k = ordinal(i, target, c)
                            e_before = 0
                            if c == 5:
                                e_before = e0 + v_event(aux, target, 4) + 1
                            elif c == 0:
                                if target == FX:
                                    e_before = e0
                                else:
                                    e_before = e0 + v_event(aux, FX, 5) + 1
                            stage_copy(k, c, HD ** -0.5 if (target == SB and c < 2) else 1.0,
                                       qk_ordinal(i, target, min(c, 4)), e_before)
                        if n >= 6 and n % 2 == 0:
                            q = (n - 6) // 2
                            h = (2 * q // TB) % 2
                            since(act, pv_done, NGROUPS * i + last_group_of_pair(groups, q) + 1)
                            since(act, o_done, 16 * i + max(q - 1, 0))
                            src, dst = (slice(HD, P), slice(0, HD)) if h == 0 else (slice(0, HD), slice(HD, P))
                            act.activation(otmp[q % 2][dst, :], pv[src, 0:2 * P], ACT.Copy).then_inc(half_out, 1)
                        if copied and copied[0] == FX and copied[1] < 4:
                            act.wait_ge(staged, ordinal(i, *copied) + 1)
                            act.activation(sqt[:], stage[:], ACT.Square).then_inc(squared, 1)
                        fin = copied_at(n - 1) if n else None
                        if fin and last and fin[0] == SB:
                            fin = None
                        fin_e = aux[n - 1]["e"] if fin and aux[n - 1] else None
                        if fin and fin[0] == FX and fin[1] < 4:
                            act.wait_ge(turned, e0 + fin_e + 1)
                            act.activation(sqt[:], turn_ps[fin_e % 2][:], ACT.Ln, scale=1.0 / HD, bias=eps_t[:, 0:1]).then_inc(turned_h, 1)
                            act.wait_ge(turned_h, e0 + fin_e + 1)
                            act.activation(sqt[:], sqt[:], ACT.Exp, scale=-0.5).then_inc(inv_rms, 1)
                        if fin and fin[1] >= 4:
                            act.wait_ge(turned, e0 + fin_e + 1)
                            since(act, pv_done, NGROUPS * i + (0 if fin[0] == FX else NGROUPS // 2))
                            v_high(fin[0], fin[1], fin_e)
                        if n < BLOCKS:
                            unit, b, h, br = block_of(n)
                        if gs:
                            group_high(gs[0])
                        if n < 2 * TB:
                            pr, s = prob[b], scores[n % 2]
                            since(act, scored, BLOCKS * i + n + 1)
                            after(act, turned, e0 + (last_event_of_pair(groups, n // 2 - 4) + 1 if n >= TB else 0))
                            if n == 2 * PAIR_ORDER.index(3):
                                act.wait_ge(cum_stored, 16)
                            act.activation(pr[:], s[:, 0:P * (b + 1)], ACT.Abs).then_inc(absd, 1)
                            act.wait_ge(absd, 16 * i + n + 1)
                            act.activation(pr[:], pr[:], ACT.Exp, scale=-1.0).then_inc(expd, 1)
                            for g in gs[1:]:
                                group_high(g)
                            act.wait_ge(expd, 16 * i + n + 1)
                            act.activation(pr[:], pr[:], ACT.Ln, bias=1.0).then_inc(lned, 1)
                        else:
                            for g in gs[1:]:
                                group_high(g)
                        if 1 <= n <= 2 * TB:
                            pb = prob[block_of(n - 1)[1]]
                            since(act, score_used, BLOCKS * i + n)
                            act.activation(pb[:], pb[:], ACT.Exp).then_inc(sb_w, 1)
                        if 2 * TB <= n < BLOCKS:
                            since(act, score_used, BLOCKS * i + n + 1)
                            act.activation(prob[b][:], prob[b][:], ACT.Exp, scale=-1.0, bias=row_max[:, n:n + 1],
                                           accum_out=den[:, n:n + 1]).then_inc(fx_exp, 1)
                        if fin:
                            target, c = fin
                            if c < 4:
                                if c == 0:
                                    since(act, scored, BLOCKS * i + (0 if target == FX else 16))
                                if target == FX:
                                    act.wait_ge(turned_l, e0 + fin_e + 1)
                                else:
                                    act.wait_ge(staged, ordinal(i, target, c) + 1)
                                split_high(target, c, qk_ordinal(i, target, c))
                with act.Fori(0, PAIRS - 1) as i:
                    iteration(i, False)
                iteration(PAIRS - 1, True)

            @block.vector
            def _(dve):
                dve.memset(eps_t[:], EPS).then_inc(eps_set, 1)
                for c, start in enumerate((fx_w, score_used, o_done, pv_done, scored, o_stored)):
                    dve.memset(tick[:, c:c + 1], 0.0).then_inc(start, 1)

                def split_low(target, c):
                    t = slice(HALF * (c % 2), HALF * (c % 2) + HALF)
                    hi = qs[target] if c < 2 else kh[target]
                    lo = qs[target] if c < 2 else kl[target]
                    a, b = slice(0, HD), slice(HD, P)
                    dve.tensor_tensor(lo[0][b if c < 2 else a, t], stage[a, :], hi[0][a, t].bitcast(F32), ALU.subtract)
                    dve.tensor_tensor(lo[1][a if c < 2 else b, t], stage[b, :], hi[1][b, t].bitcast(F32), ALU.subtract).then_inc(qk_low, 1)

                def v_low(target, c, e):
                    t = slice(4 * (c % 2), 4 * (c % 2) + 4)
                    for h in range(2):
                        d = dve.tensor_tensor(v[target][:, t, h, HD:P],
                                              turn_ps[e % 2][:].rearrange("p (t h c) -> p t h c", h=2, c=HD)[:, :, h, :],
                                              v[target][:, t, h, 0:HD].bitcast(F32), ALU.subtract)
                    d.then_inc(turned_l, 1)

                for c in range(2):
                    xg = prob[6][0:H, 0:HALF] if c == 0 else prob[5][0:H, 0:HALF]
                    dve.wait_ge(fg, 2)
                    dve.tensor_scalar(xg, xg, 0.0, None, ALU.min).then_inc(fgd, 1)
                dve.wait_ge(fg, 4)
                dve.wait_ge(fgd, 2)
                dve.tensor_tensor_scan(prob[7][0:H, 0:HALF], prob[7][0:H, 0:HALF], prob[6][0:H, 0:HALF], 0.0, ALU.add, ALU.subtract).then_inc(fgd, 1)
                dve.wait_ge(fgd, 3)
                dve.tensor_tensor_scan(prob[7][0:H, HALF:S], prob[7][0:H, HALF:S], prob[5][0:H, 0:HALF], prob[7][0:H, HALF - 1:HALF], ALU.add, ALU.subtract).then_inc(fgd, 1)
                for c in range(6):
                    if c < 4:
                        dve.wait_ge(qk_high, c + 1)
                        split_low(SB, c)
                    else:
                        dve.wait_ge(turned_h, c - 4 + 1)
                        v_low(SB, c, c - 4)

                def iteration(i, last):
                    groups, aux = SCHEDULES[last][:2]
                    e0 = PRO_EVENTS + EVENTS * i

                    def group_low(g):
                        w = (4 if g["j"] < g["p"] else 3) * P
                        dve.wait_ge(turned_h, e0 + g["e"] + 1)
                        dve.tensor_tensor(ptl[g["g"] % 2][:, 0:w], turn_ps[g["e"] % 2][:, 0:w],
                                          pth[g["g"] % 2][:, 0:w].bitcast(F32), ALU.subtract).then_inc(turned_l, 1)

                    for n in range(SLOTS + 1):
                        gs = groups[n] if n < SLOTS else []
                        if n >= 6 and n % 2 == 0:
                            q = (n - 6) // 2
                            h, br, p = (2 * q // TB) % 2, q // 8, PAIR_ORDER[q % (TB // 2)]
                            r = slice(0, HD) if h == 0 else slice(HD, P)
                            dve.wait_ge(half_out, 16 * i + q + 1)
                            if q % 8 == 0:
                                since(dve, o_stored, 32 * i + 16 * br)
                            dve.tensor_tensor(ost[r, 2 * P * p:2 * P * (p + 1)], pv[r, 0:2 * P], otmp[q % 2][r, :], ALU.add).then_inc(o_done, 1)
                        if n < BLOCKS:
                            unit, b, h, br = block_of(n)
                        if 2 * TB < n <= BLOCKS:
                            m = n - 1
                            f = m - 2 * TB
                            dve.wait_ge(fx_exp, 16 * i + f + 1)
                            dve.reciprocal(rden[:, m:m + 1], den[:, m:m + 1]).then_inc(inv_den, 1)
                            dve.wait_ge(inv_den, 16 * i + f + 1)
                            pb = prob[block_of(m)[1]]
                            dve.tensor_scalar(pb[:], pb[:], rden[:, m:m + 1], None, ALU.mult).then_inc(fx_w, 1)
                        fin = copied_at(n - 1) if n else None
                        if fin and last and fin[0] == SB:
                            fin = None
                        fin_e = aux[n - 1]["e"] if fin and aux[n - 1] else None

                        def finish_aux():
                            if not fin:
                                return
                            target, c = fin
                            if c >= 4:
                                dve.wait_ge(turned_h, e0 + fin_e + 1)
                                v_low(target, c, fin_e)
                            elif target == FX:
                                dve.wait_ge(inv_rms, 4 * i + c + 1)
                                dve.scalar_tensor_tensor(out=stage[:], in0=stage[:], scalar=gqk[:, 2:3] if c < 2 else gqk[:, 1:2],
                                                         in1=sqt[:], op0=ALU.mult, op1=ALU.mult).then_inc(turned_l, 1)

                        finish_aux()
                        if gs:
                            group_low(gs[0])
                        if n < 2 * TB:
                            pr, s, w = prob[b], scores[n % 2], P * (b + 1)
                            dve.wait_ge(lned, 16 * i + n + 1)
                            dve.scalar_tensor_tensor(out=pr[:], in0=s[:, 0:w], scalar=0.0, in1=pr[:], op0=ALU.max, op1=ALU.add).then_inc(summed, 1)
                            for g in gs[1:]:
                                group_low(g)
                            dve.wait_ge(summed, 16 * i + n + 1)
                            dve.tensor_tensor_scan(pr[:, ::-1], pr[:, ::-1], pr[:, ::-1], 0.0, ALU.add, ALU.bypass).then_inc(scanned, 1)
                            dve.wait_ge(scanned, 16 * i + n + 1)
                            dve.tensor_tensor(pr[:], s[:, 0:w], pr[:], ALU.subtract).then_inc(score_used, 1)
                        elif n < BLOCKS:
                            w = P * (b + 1)
                            since(dve, scored, BLOCKS * i + n + 1)
                            dve.wait_ge(turned, e0 + last_event_of_pair(groups, n // 2 - 4) + 1)
                            if n == 2 * TB:
                                dve.wait_ge(cum_in, 32 * i + 32)
                            dve.memset(tick[:, n:n + 1], 0.0)
                            dve.tensor_tensor_reduce(out=prob[b][:], in0=scores[n % 2][:, 0:w], in1=cumf[h][:, 0:w], scale=-1.0,
                                                     scalar=3.0e38, op0=ALU.add, op1=ALU.min,
                                                     accum_out=row_max[:, n:n + 1]).then_inc(score_used, 1)
                            for g in gs[1:]:
                                group_low(g)
                        else:
                            for g in gs[1:]:
                                group_low(g)
                        if fin and fin[1] < 4:
                            dve.wait_ge(qk_high, qk_ordinal(i, *fin) + 1)
                            split_low(*fin)
                with dve.Fori(0, PAIRS - 1) as i:
                    iteration(i, False)
                iteration(PAIRS - 1, True)

        projecting.close()
        mixing = whole.enter_context(ExitStack())
        sbm, _, _ = maker(mixing)
        mix = sbm("mix", [P, KT, S])
        with ExitStack() as ctx:
            sb, ps, sem = maker(ctx)
            oh = sb("oh", [P, KT, S], F32R)
            ol = sb("ol", [P, KT, S], F32R)
            sig = [sb(f"sig{b}", [P, S]) for b in range(2)]
            gate_ps = [ps(f"gate{b}") for b in range(2)]
            y_ps = [ps(f"y{b}") for b in range(2)]
            o_in = [sem(f"o_in{j}") for j in range(2)]
            o_high, o_low = sem("o_high"), sem("o_low")
            raw_in, w_high, w_low = ring[3]
            next_in, next_high, next_low = ring[4]
            w_used = sem("w3_used")
            gated, y_done = sem("gate_done"), sem("y_done")
            sig_done, mulled, mixed = sem("sig_done"), sem("mulled"), sem("mixed")
            block = ctx.enter_context(nc.Block())

            @block.sync
            def _(sp):
                def gate(m, b, slot):
                    sp.dma_start(raw[slot][:], win_v[:, :, bass.ds(OFF_GATE + D * b + m * P, P)]).then_inc(raw_in[slot], 16)

                def branches(m, slot):
                    sp.dma_start(raw[slot][:, 0:4, :], wosb_v[:, :, bass.ds(m * P, P)]).then_inc(raw_in[slot], 16)
                    sp.dma_start(raw[slot][:, 4:8, :], wofx_v[:, :, bass.ds(m * P, P)]).then_inc(raw_in[slot], 16)

                def weights(m, j):
                    sp.wait_ge(w_low, 3 * m - 1)
                    gate(m, 0, j)
                    sp.wait_ge(w_low, 3 * m + 1)
                    gate(m, 1, 1 - j)
                    branches(m, j)
                for k in range(KT):
                    after(sp, o_low, k - 1)
                    sp.dma_start(sig[k % 2][:], o_dram[k * P:(k + 1) * P, :]).then_inc(o_in[k % 2], 16)
                    if k == 0:
                        sp.wait_ge(w_low, 1)
                        branches(0, 0)
                weights(1, 1)
                with sp.Fori(1, KT // 2) as i:
                    weights(2 * i, 0)
                    weights(2 * i + 1, 1)
                for j in range(2):
                    sp.wait_ge(w_low, 3 * KT - 1 + j)
                    sp.dma_start(raw[j][:].rearrange(flat), w_out[0, j * P:(j + 1) * P, :]).then_inc(next_in[j], 16)

            @block.gpsimd
            def _(pool):
                def split(m, i, j, t):
                    w, slot = 3 * m + t, (3 * j + t) % 2
                    count = {0: {(0, 0): 1, (0, 2): 3, (1, 1): 4}, 1: {(0, 1): 1, (1, 0): 2, (1, 2): 4}}[slot][(j, t)]
                    pool.wait_ge(raw_in[slot], 16 * (4 * i + count))
                    after(pool, w_used, w - 1)
                    pool.tensor_tensor(wh[slot][:], raw[slot][:], zero3, ALU.add).then_inc(w_high, 1)
                    pool.wait_ge(w_high, w + 1)
                    pool.tensor_tensor(wl[slot][:], raw[slot][:], wh[slot][:].bitcast(F32), ALU.subtract).then_inc(w_low, 1)
                for t in range(2, 6):
                    split(t // 3, 0, t // 3, t % 3)
                with pool.Fori(1, KT // 2) as i:
                    for t in range(6):
                        split(2 * i + t // 3, i, t // 3, t % 3)
                pool.wait_ge(next_in[0], 16)
                pool.wait_ge(w_used, 3 * KT - 1)
                pool.tensor_tensor(wh[0][:], raw[0][:], zero3, ALU.add).then_inc(next_high, 1)
                pool.wait_ge(next_high, 1)
                pool.tensor_tensor(wl[0][:], raw[0][:], wh[0][:].bitcast(F32), ALU.subtract).then_inc(next_low, 1)

            @block.tensor
            def _(pe):
                def product(o, slot, kts, first_kt, mh, ml):
                    for kt in kts:
                        for stat_, mov in ((wh, mh), (wh, ml), (wl, mh)):
                            for c in range(2):
                                mm = pe.matmul(o[:, HALF * c:HALF * c + HALF], stat_[slot][:, kt, :],
                                               mov[:, kt, HALF * c:HALF * c + HALF],
                                               start=(kt == kts[0] and stat_ is wh and mov is mh),
                                               stop=(kt == kts[-1] and stat_ is wl))
                    return mm

                def output_tile(m, j):
                    for b in range(2):
                        pe.wait_ge(w_low, 3 * m + b + 1)
                        after(pe, sig_done, 2 * m + b - 1)
                        product(gate_ps[b], (3 * j + b) % 2, range(KT), 0, hTh, hTl).then_inc(w_used, 1)
                    pe.wait_ge(w_low, 3 * m + 3)
                    if isinstance(m, int) and m == 0:
                        pe.wait_ge(o_low, KT)
                        pe.wait_ge(o_high, KT)
                    after(pe, mulled, 2 * m)
                    for b in range(2):
                        mm = product(y_ps[b], (3 * j + 2) % 2, range(4 * b, 4 * b + 4), 0, oh, ol)
                    mm.then_inc(w_used, 1)
                output_tile(0, 0)
                output_tile(1, 1)
                with pe.Fori(1, KT // 2) as i:
                    output_tile(2 * i, 0)
                    output_tile(2 * i + 1, 1)

            @block.scalar
            def _(act):
                for k in range(KT):
                    act.wait_ge(o_in[k % 2], 16 * (k // 2) + 16)
                    act.activation(oh[:, k, :], sig[k % 2][:], ACT.Copy).then_inc(o_high, 1)

                def output_tile(m):
                    for b in range(2):
                        act.wait_ge(w_used, 3 * m + b + 1)
                        if isinstance(m, int) and m == 0:
                            act.wait_ge(o_low, KT)
                        after(act, mixed, m)
                        act.activation(sig[b][:], gate_ps[b][:], ACT.Sigmoid,
                                       bias=cols[:, 4, bass.ds(m + b * KT, 1)]).then_inc(sig_done, 1)
                output_tile(0)
                with act.Fori(1, KT) as m:
                    output_tile(m)

            @block.vector
            def _(dve):
                for k in range(KT):
                    dve.wait_ge(o_high, k + 1)
                    dve.tensor_tensor(ol[:, k, :], sig[k % 2][:], oh[:, k, :].bitcast(F32), ALU.subtract).then_inc(o_low, 1)

                def output_tile(m):
                    dve.wait_ge(w_used, 3 * m + 3)
                    for b in range(2):
                        dve.wait_ge(sig_done, 2 * m + b + 1)
                        dve.tensor_tensor(sig[b][:], sig[b][:], y_ps[b][:], ALU.mult).then_inc(mulled, 1)
                    dve.wait_ge(mulled, 2 * m + 2)
                    dve.tensor_tensor(mix[:, bass.ds(m, 1), :].rearrange("p a b -> p (a b)"), sig[0][:], sig[1][:], ALU.add).then_inc(mixed, 1)
                with dve.Fori(0, KT) as m:
                    output_tile(m)

        with ExitStack() as ctx:
            sb, ps, sem = maker(ctx)
            woh_rest = sb("woh", [P, KT - 2, D], F32R)
            wol_rest = sb("wol", [P, KT - 2, D], F32R)
            woh = [wh[k][:].rearrange(flat) if k < 2 else woh_rest[:, k - 2, :] for k in range(KT)]
            wol = [wl[k][:].rearrange(flat) if k < 2 else wol_rest[:, k - 2, :] for k in range(KT)]
            mh = [sb(f"mh{j}", [P, KT, P], F32R) for j in range(2)]
            ml = [sb(f"ml{j}", [P, KT, P], F32R) for j in range(2)]
            gain = sb("gain4", [P, D])
            xt = [sb(f"xt4{j}", [P, D]) for j in range(2)]
            xn = [raw[j][:].rearrange(flat) for j in range(2)]
            stages = [raw[0][:].rearrange(flat), raw[1][:].rearrange(flat), xt[0][:], xt[1][:]]
            stage_of = [0, 1, 0, 2, 3, 1, 0, 2]
            turn_of = [stage_of[:k].count(stage_of[k]) for k in range(KT)]
            stat = sb("stat4", [P, 3, 2])
            proj = [ps(f"outp{j}") for j in range(2)]
            turned = [ps(f"turned4{j}") for j in range(2)]
            first_in, w_high, w_low = ring[4]
            w_in_s = first_in + [sem(f"w4_in{j}") for j in (2, 3)]
            next_in, next_high, next_low = ring[5]
            x_in = [sem(f"x4_in{j}") for j in range(2)]
            gain_in, x2_out = sem("gain4_in"), [sem(f"x2_out{j}") for j in range(2)]
            m_high, m_low, proj_done, x2_done = sem("m_high"), sem("m_low"), sem("proj4"), sem("x2_done")
            sq_done, root_done, inv_done, xn_done = (sem(n + "4") for n in ("sq", "root", "inv", "xn"))
            tr_done, hi_done, lo_done = sem("tr4"), sem("hi4"), sem("lo4")
            eps_set = sem("eps_set4")
            eps_t = sb("eps_t4", [P, 1])
            tick = sb("tick4", [P, 5])
            block = ctx.enter_context(nc.Block())

            @block.sync
            def _(sp):
                for k in range(2, KT):
                    if turn_of[k]:
                        sp.wait_ge(w_low, max(m for m in range(k) if stage_of[m] == stage_of[k]) + 1)
                    sp.dma_start(stages[stage_of[k]], w_out[0, k * P:(k + 1) * P, :]).then_inc(w_in_s[stage_of[k]], 16)
                sp.wait_ge(w_low, KT)
                sp.dma_start(gain[:], g_ffn.to_broadcast([P, D])).then_inc(gain_in, 16)

                def load(t, j, turn):
                    since(sp, xn_done, t - 1)
                    after(sp, x2_out[j], 16 * turn)
                    sp.dma_start(xt[j][:], x[0, bass.ds(t * P, P), :]).then_inc(x_in[j], 16)

                def store(t, j):
                    sp.wait_ge(x2_done, t + 1)
                    sp.dma_start(x2_dram[bass.ds(t * P, P), :], xt[j][:]).then_inc(x2_out[j], 16)
                load(0, 0, 0)
                load(1, 1, 0)
                with sp.Fori(0, TB // 2 - 1) as i:
                    for j in range(2):
                        store(2 * i + j, j)
                    for j in range(2):
                        load(2 * i + 2 + j, j, i + 1)
                for j in range(2):
                    store(TB - 2 + j, j)
                for j in range(2):
                    since(sp, tr_done, TB - 1 + j)
                    sp.dma_start(raw[j][:], wup_v[:, :, j * FF:j * FF + P]).then_inc(next_in[j], 16)
                for j in range(2):
                    sp.wait_ge(x2_out[j], 16 * (TB // 2))

            @block.gpsimd
            def _(pool):
                for j in range(2):
                    pool.wait_ge(next_high, j + 1)
                    pool.tensor_tensor(wl[j][:], raw[j][:], wh[j][:].bitcast(F32), ALU.subtract).then_inc(next_low, 1)

            @block.tensor
            def _(pe):
                def product(j, kt):
                    for stat_, mov in ((mh, woh), (mh, wol), (ml, woh)):
                        for c in range(2):
                            mm = pe.matmul(proj[j][:, HALF * c:HALF * c + HALF], stat_[j][:, kt, :],
                                           mov[kt][:, HALF * c:HALF * c + HALF],
                                           start=(kt == 0 and stat_ is mh and mov is woh),
                                           stop=(kt == KT - 1 and stat_ is ml))
                    return mm

                def project(t, j):
                    pe.wait_ge(m_low, t + 1)
                    pe.wait_ge(x2_done, t - 1)
                    for kt in range(KT):
                        mm = product(j, kt)
                    mm.then_inc(proj_done, 1)

                def turn(t, j):
                    since(pe, xn_done, t + 1)
                    since(pe, hi_done, t - 1)
                    since(pe, lo_done, t - 1)
                    for k in range(KT):
                        mm = pe.transpose(turned[j][:, k * P:(k + 1) * P], xn[j][:, k * P:(k + 1) * P], ident[:])
                    mm.then_inc(tr_done, 1)
                for kt in range(KT):
                    pe.wait_ge(w_low, kt + 1)
                    for t in range(2):
                        if kt == 0:
                            pe.wait_ge(m_low, t + 1)
                        mm = product(t, kt)
                        if kt == KT - 1:
                            mm.then_inc(proj_done, 1)
                turn(0, 0)
                with pe.Fori(1, TB // 2) as i:
                    project(2 * i, 0)
                    turn(2 * i - 1, 1)
                    project(2 * i + 1, 1)
                    turn(2 * i, 0)
                turn(TB - 1, 1)

            @block.scalar
            def _(act):
                for k in range(KT):
                    if k:
                        act.wait_ge(w_in_s[stage_of[k]], 16 * turn_of[k] + 16)
                        act.activation(woh[k], stages[stage_of[k]], ACT.Copy).then_inc(w_high, 1)
                    if k < 2:
                        act.activation(mh[k][:], mix[:, :, k * P:(k + 1) * P], ACT.Copy).then_inc(m_high, 1)
                act.wait_ge(eps_set, 1)
                act.wait_ge(w_low, KT)

                def stats(t, j):
                    act.wait_ge(x2_done, t + 1)
                    since(act, tr_done, t - 1)
                    act.activation(xn[j], xt[j][:], ACT.Square, accum_out=stat[:, 0, j:j + 1]).then_inc(sq_done, 1)
                    act.wait_ge(sq_done, t + 1)
                    since(act, inv_done, t - 1)
                    act.activation(stat[:, 1, j:j + 1], stat[:, 0, j:j + 1], ACT.Sqrt, scale=1.0 / D, bias=eps_t[:, 0:1]).then_inc(root_done, 1)

                def mix_high(t, j):
                    act.wait_ge(proj_done, t - 1)
                    act.activation(mh[j][:], mix[:, :, bass.ds(t * P, P)], ACT.Copy).then_inc(m_high, 1)

                def high(t, j):
                    since(act, tr_done, t + 1)
                    act.activation(hTh[:, :, bass.ds(t * P, P)], turned[j][:].rearrange("p (k t) -> p k t", k=KT), ACT.Copy).then_inc(hi_done, 1)
                stats(0, 0)
                mix_high(2, 0)
                with act.Fori(0, TB // 2 - 2) as i:
                    stats(2 * i + 1, 1)
                    mix_high(2 * i + 3, 1)
                    high(2 * i, 0)
                    stats(2 * i + 2, 0)
                    mix_high(2 * i + 4, 0)
                    high(2 * i + 1, 1)
                stats(TB - 3, 1)
                mix_high(TB - 1, 1)
                high(TB - 4, 0)
                stats(TB - 2, 0)
                high(TB - 3, 1)
                stats(TB - 1, 1)
                high(TB - 2, 0)
                high(TB - 1, 1)
                act.wait_ge(proj_done, TB)
                for j in range(2):
                    act.wait_ge(next_in[j], 16)
                    act.activation(wh[j][:], raw[j][:], ACT.Copy).then_inc(next_high, 1)

            @block.vector
            def _(dve):
                dve.memset(eps_t[:], EPS).then_inc(eps_set, 1)
                for c, start in enumerate((tr_done, hi_done, lo_done, inv_done, xn_done)):
                    dve.memset(tick[:, c:c + 1], 0.0).then_inc(start, 1)
                for k in range(KT):
                    if k:
                        dve.wait_ge(w_high, k + 1)
                        dve.tensor_tensor(wol[k], stages[stage_of[k]], woh[k].bitcast(F32), ALU.subtract).then_inc(w_low, 1)
                    if k < 2:
                        dve.wait_ge(m_high, k + 1)
                        dve.tensor_tensor(ml[k][:], mix[:, :, k * P:(k + 1) * P], mh[k][:].bitcast(F32), ALU.subtract).then_inc(m_low, 1)
                dve.wait_ge(gain_in, 16)

                def norm(t, j, turn):
                    dve.wait_ge(proj_done, t + 1)
                    dve.wait_ge(x_in[j], 16 * turn + 16)
                    dve.tensor_tensor(xt[j][:], proj[j][:], xt[j][:], ALU.add).then_inc(x2_done, 1)
                    dve.wait_ge(root_done, t + 1)
                    since(dve, xn_done, t - 1)
                    dve.reciprocal(stat[:, 2, j:j + 1], stat[:, 1, j:j + 1]).then_inc(inv_done, 1)
                    since(dve, inv_done, t + 1)
                    dve.scalar_tensor_tensor(out=xn[j], in0=xt[j][:], scalar=stat[:, 2, j:j + 1], in1=gain[:],
                                             op0=ALU.mult, op1=ALU.mult).then_inc(xn_done, 1)

                def mix_low(t, j):
                    dve.wait_ge(m_high, t + 1)
                    dve.tensor_tensor(ml[j][:], mix[:, :, bass.ds(t * P, P)], mh[j][:].bitcast(F32), ALU.subtract).then_inc(m_low, 1)

                def low(t, j):
                    since(dve, hi_done, t + 1)
                    dve.tensor_tensor(hTl[:, :, bass.ds(t * P, P)], turned[j][:].rearrange("p (k t) -> p k t", k=KT),
                                      hTh[:, :, bass.ds(t * P, P)].bitcast(F32), ALU.subtract).then_inc(lo_done, 1)
                norm(0, 0, 0)
                mix_low(2, 0)
                with dve.Fori(0, TB // 2 - 2) as i:
                    norm(2 * i + 1, 1, i)
                    mix_low(2 * i + 3, 1)
                    low(2 * i, 0)
                    norm(2 * i + 2, 0, i + 1)
                    mix_low(2 * i + 4, 0)
                    low(2 * i + 1, 1)
                norm(TB - 3, 1, TB // 2 - 2)
                mix_low(TB - 1, 1)
                low(TB - 4, 0)
                norm(TB - 2, 0, TB // 2 - 1)
                low(TB - 3, 1)
                norm(TB - 1, 1, TB // 2 - 1)
                low(TB - 2, 0)
                low(TB - 1, 1)
        mixing.close()

        sb, _, sem = maker(whole)
        act_t = sb("act_t", [P, FT, S])
        ah = [sb(f"ah{j}", [P, HALF], F32R) for j in range(2)]
        al = [sb(f"al{j}", [P, HALF], F32R) for j in range(2)]
        a_high, a_low = sem("a_high"), sem("a_low")
        with ExitStack() as ctx:
            sb, ps, sem = maker(ctx)
            u = [[sb(f"u{j}{c}", [P, S]) for c in range(2)] for j in range(2)]
            u_ps = [[ps(f"u_ps{j}{c}") for c in range(2)] for j in range(2)]
            raw_in, w_high, w_low = ring[5]
            next_in, next_high, next_low = ring[6]
            u_done = sem("u_done")
            tap2, tap1, tap0, silu_done, act_done = (sem(n) for n in ("tap2", "tap1", "tap0", "silu_done", "act_done"))
            block = ctx.enter_context(nc.Block())

            @block.sync
            def _(sp):
                with sp.Fori(1, FT) as f:
                    for c in range(2):
                        sp.wait_ge(w_low, 2 * f + c - 1)
                        sp.dma_start(raw[c][:], wup_v[:, :, bass.ds(f * P + c * FF, P)]).then_inc(raw_in[c], 16)
                for j in range(2):
                    sp.wait_ge(w_low, 2 * FT - 1 + j)
                    sp.dma_start(raw[j][:].rearrange(flat), w_down[0, j * P:(j + 1) * P, :]).then_inc(next_in[j], 16)

            @block.gpsimd
            def _(pool):
                with pool.Fori(1, FT) as f:
                    for c in range(2):
                        pool.wait_ge(w_high, 2 * f + c + 1)
                        pool.tensor_tensor(wl[c][:], raw[c][:], wh[c][:].bitcast(F32), ALU.subtract).then_inc(w_low, 1)
                for j in range(2):
                    pool.wait_ge(next_high, j + 1)
                    pool.tensor_tensor(wl[j][:], raw[j][:], wh[j][:].bitcast(F32), ALU.subtract).then_inc(next_low, 1)

            @block.tensor
            def _(pe):
                def tile(f, j):
                    for c in range(2):
                        pe.wait_ge(w_low, 2 * f + c + 1)
                        after(pe, tap0, 2 * f + c - 3)
                        for kt in range(KT):
                            for stat_, mov in ((wh, hTh), (wh, hTl), (wl, hTh)):
                                for h in range(2):
                                    mm = pe.matmul(u_ps[j][c][:, HALF * h:HALF * h + HALF], stat_[c][:, kt, :],
                                                   mov[:, kt, HALF * h:HALF * h + HALF],
                                                   start=(kt == 0 and stat_ is wh and mov is hTh),
                                                   stop=(kt == KT - 1 and stat_ is wl))
                        mm.then_inc(u_done, 1)
                tile(0, 0)
                tile(1, 1)
                with pe.Fori(1, FT // 2) as i:
                    tile(2 * i, 0)
                    tile(2 * i + 1, 1)

            @block.scalar
            def _(act):
                def w_split(f, c):
                    act.wait_ge(raw_in[c], 16 * f + 16)
                    after(act, u_done, 2 * f + c - 1)
                    act.activation(wh[c][:], raw[c][:], ACT.Copy).then_inc(w_high, 1)

                def evacuate(f, j, c):
                    act.wait_ge(u_done, 2 * f + c + 1)
                    after(act, act_done, f - 1)
                    act.activation(u[j][c][:], u_ps[j][c][:], ACT.Identity, scale=cols[:, 2, bass.ds(f + c * FT, 1)],
                                   bias=cols[:, 3, bass.ds(f + c * FT, 1)]).then_inc(tap2, 1)

                def silu(f, j):
                    act.wait_ge(tap0, 2 * f + 1)
                    act.activation(u[j][0][:], u[j][0][:], ACT.Silu).then_inc(silu_done, 1)

                def tile(f, j, more):
                    for c in range(2):
                        evacuate(f, j, c)
                        if more:
                            w_split(f + 1, c)
                        else:
                            act.wait_ge(next_in[c], 16)
                            act.activation(wh[c][:], raw[c][:], ACT.Copy).then_inc(next_high, 1)
                            act.wait_ge(act_done, c + 1)
                            act.activation(ah[c][:], act_t[:, c, 0:HALF], ACT.Copy).then_inc(a_high, 1)
                    silu(f, j)
                tile(0, 0, True)
                tile(1, 1, True)
                with act.Fori(1, FT // 2 - 1) as i:
                    tile(2 * i, 0, True)
                    tile(2 * i + 1, 1, True)
                tile(FT - 2, 0, True)
                tile(FT - 1, 1, False)

            @block.vector
            def _(dve):
                def tile(f, j):
                    for c in range(2):
                        dve.wait_ge(tap2, 2 * f + c + 1)
                        dve.scalar_tensor_tensor(out=u[j][c][:, 1:S], in0=u_ps[j][c][:, 0:S - 1], scalar=cols[:, 1, bass.ds(f + c * FT, 1)],
                                                 in1=u[j][c][:, 1:S], op0=ALU.mult, op1=ALU.add).then_inc(tap1, 1)
                        dve.wait_ge(tap1, 2 * f + c + 1)
                        dve.scalar_tensor_tensor(out=u[j][c][:, 2:S], in0=u_ps[j][c][:, 0:S - 2], scalar=cols[:, 0, bass.ds(f + c * FT, 1)],
                                                 in1=u[j][c][:, 2:S], op0=ALU.mult, op1=ALU.add).then_inc(tap0, 1)
                    dve.wait_ge(silu_done, f + 1)
                    dve.wait_ge(tap0, 2 * f + 2)
                    dve.tensor_tensor(act_t[:, bass.ds(f, 1), :].rearrange("p a b -> p (a b)"), u[j][0][:], u[j][1][:], ALU.mult).then_inc(act_done, 1)
                with dve.Fori(0, FT // 2) as i:
                    tile(2 * i, 0)
                    tile(2 * i + 1, 1)
                for j in range(2):
                    dve.wait_ge(a_high, j + 1)
                    dve.tensor_tensor(al[j][:], act_t[:, j, 0:HALF], ah[j][:].bitcast(F32), ALU.subtract).then_inc(a_low, 1)

        with ExitStack() as ctx:
            sb, ps, sem = maker(ctx)
            rawf, whf, wlf = ([t[j][:].rearrange(flat) for j in range(2)] for t in (raw, wh, wl))
            x2 = [sb(f"x2{t}", [P, D]) for t in range(4)]
            acc = [ps(f"acc{t}") for t in range(4)]
            raw_in, w_high, w_low = ring[6]
            used, acc_done = sem("used6"), sem("acc_done")
            x2_in = [sem(f"x2_in{t}") for t in range(4)]
            summed, stored = sem("summed6"), [sem(f"stored{t}") for t in range(4)]
            block = ctx.enter_context(nc.Block())
            QT = HALF // P

            @block.sync
            def _(sp):
                for half in range(2):
                    for j in range(2 if half else 0):
                        sp.wait_ge(w_low, j - 1 + half * FT)
                        sp.dma_start(rawf[j], w_down[0, j * P:(j + 1) * P, :]).then_inc(raw_in[j], 16)
                    with sp.Fori(1, FT // 2) as i:
                        for j in range(2):
                            sp.wait_ge(w_low, 2 * i + j - 1 + half * FT)
                            sp.dma_start(rawf[j], w_down[0, bass.ds((2 * i + j) * P, P), :]).then_inc(raw_in[j], 16)

            @block.gpsimd
            def _(pool):
                def low(g, j):
                    pool.wait_ge(w_high, g + 1)
                    pool.tensor_tensor(wlf[j], rawf[j], whf[j].bitcast(F32), ALU.subtract).then_inc(w_low, 1)

                for half in range(2):
                    if half:
                        for j in range(2):
                            low(FT + j, j)
                    for t in range(QT):
                        if half:
                            pool.wait_ge(stored[t], 16)
                        pool.dma_start(x2[t][:], x2_dram[(QT * half + t) * P:(QT * half + t + 1) * P, :]).then_inc(x2_in[t], 16)
                    with pool.Fori(1, FT // 2) as i:
                        for j in range(2):
                            low(2 * i + j + half * FT, j)

            @block.tensor
            def _(pe):
                def step(half, f, j, first, last):
                    g = half * FT + f
                    pe.wait_ge(w_low, g + 1)
                    pe.wait_ge(a_low, g + 1)
                    for t in range(QT):
                        if first and half:
                            pe.wait_ge(summed, t + 1)
                        for stat_, mov in ((ah, whf), (ah, wlf), (al, whf)):
                            for c in range(2):
                                mm = pe.matmul(acc[t][:, HALF * c:HALF * c + HALF], stat_[j][:, t * P:(t + 1) * P],
                                               mov[j][:, HALF * c:HALF * c + HALF],
                                               start=(first and stat_ is ah and mov is whf), stop=(last and stat_ is al))
                        if last:
                            mm.then_inc(acc_done, 1)
                    if not last:
                        mm.then_inc(used, 1)
                for half in range(2):
                    step(half, 0, 0, True, False)
                    step(half, 1, 1, False, False)
                    with pe.Fori(1, FT // 2 - 1) as i:
                        step(half, 2 * i, 0, False, False)
                        step(half, 2 * i + 1, 1, False, False)
                    step(half, FT - 2, 0, False, False)
                    step(half, FT - 1, 1, False, True)

            @block.scalar
            def _(act):
                def step(half, f, j, turn):
                    act.wait_ge(raw_in[j], 16 * turn + 16)
                    if half and isinstance(f, int) and f < 2:
                        act.wait_ge(used, FT - 1)
                        if f == 1:
                            act.wait_ge(acc_done, QT)
                    else:
                        act.wait_ge(used, half * (FT - 1) + f - 1)
                    act.activation(whf[j], rawf[j], ACT.Copy).then_inc(w_high, 1)
                    act.activation(ah[j][:], act_t[:, bass.ds(f, 1), HALF * half:HALF * half + HALF].rearrange("p a b -> p (a b)"),
                                   ACT.Copy).then_inc(a_high, 1)

                def out_store(half, t):
                    act.wait_ge(summed, QT * half + t + 1)
                    act.dma_start(out[0, (QT * half + t) * P:(QT * half + t + 1) * P, :], x2[t][:]).then_inc(stored[t], 16)
                with act.Fori(1, FT // 2) as i:
                    for j in range(2):
                        step(0, 2 * i + j, j, i)
                step(1, 0, 0, FT // 2)
                step(1, 1, 1, FT // 2)
                for t in range(QT):
                    out_store(0, t)
                with act.Fori(1, FT // 2) as i:
                    for j in range(2):
                        step(1, 2 * i + j, j, FT // 2 + i)
                for t in range(QT):
                    out_store(1, t)
                for t in range(QT):
                    act.wait_ge(stored[t], 32)

            @block.vector
            def _(dve):
                def step(half, f, j):
                    g = half * FT + f
                    dve.wait_ge(a_high, g + 1)
                    dve.tensor_tensor(al[j][:], act_t[:, bass.ds(f, 1), HALF * half:HALF * half + HALF].rearrange("p a b -> p (a b)"),
                                      ah[j][:].bitcast(F32), ALU.subtract).then_inc(a_low, 1)

                def row_sum(half, t):
                    dve.wait_ge(acc_done, QT * half + t + 1)
                    dve.wait_ge(x2_in[t], 16 * half + 16)
                    dve.tensor_tensor(x2[t][:], acc[t][:], x2[t][:], ALU.add).then_inc(summed, 1)
                with dve.Fori(1, FT // 2) as i:
                    for j in range(2):
                        step(0, 2 * i + j, j)
                step(1, 0, 0)
                for t in range(QT):
                    row_sum(0, t)
                step(1, 1, 1)
                with dve.Fori(1, FT // 2) as i:
                    for j in range(2):
                        step(1, 2 * i + j, j)
                for t in range(QT):
                    row_sum(1, t)


_INS = ["x", "g_mix", "w_in", "b_forget", "b_gate", "g_q", "g_k", "w_o_sb", "w_o_fox", "w_out",
        "g_ffn", "w_up", "conv_w", "conv_b", "w_down"]


def kernel(**inputs):
    import numpy as np
    import concourse.bacc as bacc
    from concourse.bass_utils import run_bass_kernel_spmd

    nc = bacc.Bacc("TRN2", target_bir_lowering=False, num_devices=1)
    arrays, args = {}, []
    for name in _INS:
        a = np.ascontiguousarray(inputs[name])
        arrays[f"in_{name}"] = a
        args.append(nc.dram_tensor(f"in_{name}", a.shape, mybir.dt.from_np(a.dtype), kind="ExternalInput").ap())
    out = nc.dram_tensor("out", (1, S, D), F32, kind="ExternalOutput").ap()
    build(nc, *args, out)
    r = run_bass_kernel_spmd(nc, [arrays], core_ids=[0])
    return r.results[0]["out"]
```

```python
from contextlib import ExitStack

import concourse.bass as bass
from concourse import mybir

F32 = mybir.dt.float32
F32R = mybir.dt.float32r
ALU = mybir.AluOpType
ACT = mybir.ActivationFunctionType

P = 128
S = 1024
D = 1024
H = 8
HD = 64
FF = 2816
EPS = 1e-6
NEG = -1e30
KT = D // P
TB = S // P
HALF = 512
FT = FF // P
PAIRS = H // 2
OFF_FOX = 3 * H * HD
OFF_FORGET = 2 * OFF_FOX
OFF_GATE = OFF_FORGET + H
SB, FX = 0, 1


def after(eng, sem, value):
    if isinstance(value, int) and value <= 0:
        return
    eng.wait_ge(sem, value)


def since(eng, sem, value):
    if isinstance(value, int) and value < 0:
        return
    eng.wait_ge(sem, value + 1)


BLOCKS = 4 * TB
PAIR_ORDER = (1, 3, 0, 2)
TAIL = 5
CHUNK_MMS = 3 * KT
CHUNKS = [dict(target=(FX, SB)[k // 6], c=k % 6, start=8 * (k // 3) + 3 * (k % 3), slots=(3, 3, 2)[k % 3]) for k in range(12)]
FIRST_GROUP, FIRST_SUM, FIRST_COPY, FIRST_RATIO = 4, 6, 3, 1


def block_of(n):
    return n // TB, 2 * PAIR_ORDER[n % TB // 2] + n % 2, (n // TB) % 2, n // (2 * TB)


def place(n, first_slot):
    return (n + BLOCKS, 1) if n < first_slot else (n, 0)


def slots(kind):
    return BLOCKS + TAIL if kind == "last" else BLOCKS


def chunk_at(n):
    for k in CHUNKS:
        if 0 <= n - k["start"] < k["slots"]:
            per = CHUNK_MMS // k["slots"]
            return k["target"], k["c"], per * (n - k["start"]), per * (n - k["start"] + 1)
    return None


def copied_at(n, kind):
    m, back = place(n, FIRST_COPY)
    for k in CHUNKS:
        if m == k["start"] + k["slots"] and n >= 0:
            if (back and kind == "first") or (not back and kind == "last" and k["target"] == SB and k["c"] >= 4):
                return None
            return k["target"], k["c"], back
    return None


CARRIED_GROUPS = sum(p + 1 for p in PAIR_ORDER[2:])
CARRIED = CARRIED_GROUPS + 1


def make_schedule(kind):
    count = slots(kind)
    groups, aux = [[] for _ in range(count)], [None] * count
    e, g = (CARRIED, CARRIED_GROUPS) if kind == "first" else (0, 0)
    for n in range(count):
        m, back = place(n, FIRST_GROUP)
        q = (m - m % 2 - FIRST_GROUP) // 2
        if q < BLOCKS // 2 and not (back and kind == "first"):
            p = PAIR_ORDER[q % (TB // 2)]
            mine = range(p + 1)
            split = (p + 2) // 2
            for j in (mine[:split] if n % 2 == 0 else mine[split:]):
                groups[n].append(dict(e=e, g=g, q=q, p=p, j=j, unit=(2 * q) // TB, back=back))
                e, g = e + 1, g + 1
        done = copied_at(n, kind)
        if done and (done[1] >= 4 or done[0] == FX):
            aux[n] = dict(e=e, c=done[1], target=done[0], back=done[2])
            e += 1
    return groups, aux, e, g


SCHEDULES = {kind: make_schedule(kind) for kind in ("first", "middle", "last")}
EVENTS, NGROUPS = SCHEDULES["middle"][2:]
assert EVENTS % 2 == 0 and NGROUPS % 2 == 0 and SCHEDULES["first"][2:] == (EVENTS, NGROUPS)
PRO_EVENTS = 2
EVENT_BASE = PRO_EVENTS - CARRIED


def v_event(kind, target, c, back=0):
    if back and c == 4:
        return v_event("middle", target, c) - EVENTS
    if back and kind == "first":
        return CARRIED - 1
    return next(a["e"] for a in SCHEDULES[kind][1] if a and (a["target"], a["c"], a["back"]) == (target, c, back))


def last_of_pair(kind, q, back, what):
    if back and 2 * q + FIRST_GROUP < BLOCKS:
        return last_of_pair("middle", q, 0, what) - (EVENTS if what == "e" else NGROUPS)
    return max(g[what] for gs in SCHEDULES[kind][0] for g in gs if (g["q"], g["back"]) == (q, back))


def tile_free_event(kind, n):
    q, back = (n // 2 - TB // 2, 0) if n >= TB else (n // 2 + (BLOCKS - TB) // 2, 1)
    if back and kind == "first":
        return None
    return last_of_pair(kind, q, back, "e")


def build(nc, x, g_mix, w_in, b_forget, b_gate, g_q, g_k, w_o_sb, w_o_fox, w_out, g_ffn, w_up,
          conv_w, conv_b, w_down, out):
    o_dram = nc.dram_tensor("attn_out_t", (2 * PAIRS * P, S), F32, kind="Internal").ap()
    cum_dram = nc.dram_tensor("neg_cum_forget", (H, S), F32, kind="Internal").ap()
    gate_dram = nc.dram_tensor("first_gates", (2, P, S), F32, kind="Internal").ap()
    x2_dram = nc.dram_tensor("mid_residual", (S, D), F32, kind="Internal").ap()
    win_v = w_in[0].rearrange("(k p) n -> p k n", p=P)
    wup_v = w_up[0].rearrange("(k p) n -> p k n", p=P)
    wosb_v = w_o_sb[0].rearrange("(k p) n -> p k n", p=P)
    wofx_v = w_o_fox[0].rearrange("(k p) n -> p k n", p=P)

    with ExitStack() as whole:
        def maker(ctx):
            def sb(name, shape, dt=F32):
                return ctx.enter_context(nc.sbuf_tensor(name, shape, dt))

            def ps(name, shape=(P, S)):
                return ctx.enter_context(nc.psum_tensor(name, list(shape), F32))

            def sem(name):
                return ctx.enter_context(nc.semaphore(name))
            return sb, ps, sem

        sb, ps_whole, sem = maker(whole)
        raw = [sb(f"raw{j}", [P, KT, P]) for j in range(2)]
        wh = [sb(f"wh{j}", [P, KT, P], F32R) for j in range(2)]
        wl = [sb(f"wl{j}", [P, KT, P], F32R) for j in range(2)]
        flat = "p k n -> p (k n)"
        ring = {p: ([sem(f"raw{p}_in{j}") for j in range(2)], sem(f"w{p}_high"), sem(f"w{p}_low")) for p in (2, 3, 4, 5, 6)}
        proj_done = sem("proj_done")
        ident = sb("ident", [P, P])
        head_ones = sb("head_ones", [P, P])
        mask_f = sb("mask_f", [P, 2, P])
        maskr = sb("maskr", [P, 2, P], F32R)
        identr = sb("identr", [P, P], F32R)
        zero = sb("zero", [P, 1])
        zero_half = zero[:, 0:1].to_broadcast([P, HALF])
        zero3 = zero[:].rearrange("p (a b) -> p a b", a=1).to_broadcast([P, KT, P])
        cols = sb("cols", [P, 5, FT * 2])
        gqk = sb("gqk", [P, 4])
        bfc = sb("bfc", [H, 1])

        projecting = whole.enter_context(ExitStack())
        proj = projecting.enter_context(nc.psum_tensor("proj", [P, HALF], F32))
        early = whole.enter_context(ExitStack())
        sbh, _, _ = maker(early)
        hTh = sbh("hTh", [P, KT, S], F32R)
        hTl = sbh("hTl", [P, KT, S], F32R)

        def project_chunk(pe, o, slot, c, lo, hi):
            for n in range(lo, hi):
                kt, kind = n // 3, n % 3
                stat_ = wl if kind == 2 else wh
                mov = hTl if kind == 1 else hTh
                mm = pe.matmul(o[:], stat_[slot][:, kt, :], mov[:, kt, HALF * c:HALF * c + HALF],
                               start=(n == 0), stop=(n == CHUNK_MMS - 1))
            return mm

        with ExitStack() as ctx:
            sb, ps, sem = maker(ctx)
            gain = sb("gain", [P, D])
            rows = sb("rows", [2 * FT, 5, P])
            xt = [sb(f"xt{j}", [P, D]) for j in range(2)]
            xn = [sb(f"xn{j}", [P, D]) for j in range(2)]
            stat = sb("stat", [P, 3, 2])
            turned = [ps(f"turned{j}") for j in range(2)]
            turned_c = ps("turned_c", (P, 512))
            gain_in, consts_in, small_in = sem("gain_in"), sem("consts_in"), sem("small_in")
            x_in = [sem(f"x_in{j}") for j in range(2)]
            const0, const1, const2 = sem("const0"), sem("const1"), sem("const2")
            sq_done, root_done, inv_done, xn_done = (sem(n) for n in ("sq", "root", "inv", "xn"))
            tr_done, hi_done, lo_done = sem("tr1"), sem("hi1"), sem("lo1")
            colt_done, col_done, gq_done = sem("colt"), sem("col"), sem("gq8")
            eps_set = sem("eps_set")
            eps_t = sb("eps_t", [P, 1])
            eps_col = eps_t[:, 0:1]
            next_in, next_high, next_low = ring[2]
            block = ctx.enter_context(nc.Block())

            @block.sync
            def _(sp):
                def load(t, j):
                    after(sp, xn_done, t - 1)
                    sp.dma_start(xt[j][:], x[0, bass.ds(t * P, P), :]).then_inc(x_in[j], 16)
                load(0, 0)
                sp.dma_start(gain[:], g_mix.to_broadcast([P, D])).then_inc(gain_in, 16)
                load(1, 1)
                sp.dma_start(raw[0][:], win_v[:, :, OFF_FORGET:OFF_FORGET + P]).then_inc(next_in[0], 16)
                for c in range(3):
                    sp.dma_start(rows[0:2 * FT, c, :], conv_w[0, c].rearrange("(a b) -> a b", b=P)).then_inc(consts_in, 16)
                sp.dma_start(rows[0:2 * FT, 3, :], conv_b[0].rearrange("(a b) -> a b", b=P)).then_inc(consts_in, 16)
                sp.dma_start(rows[0:16, 4, :], b_gate[0].rearrange("(a b) -> a b", b=P)).then_inc(consts_in, 16)
                with nc.allow_non_contiguous_dma(reason="a few gains, one to a partition"):
                    for half in range(2):
                        for c, g in ((0, g_q), (1, g_k)):
                            sp.dma_start(gqk[HD * half:HD * half + HD, c:c + 1], g.rearrange("a b -> b a")).then_inc(small_in, 16)
                    sp.dma_start(bfc[:], b_forget.rearrange("a b -> b a")).then_inc(small_in, 16)
                with sp.Fori(1, TB // 2) as i:
                    for j in range(2):
                        load(2 * i + j, j)
                sp.dma_start(raw[1][:], win_v[:, :, 0:P]).then_inc(next_in[1], 16)

            @block.gpsimd
            def _(pool):
                pool.memset(ident[:], 0.0).then_inc(const0, 1)
                pool.memset(mask_f[:], 0.0).then_inc(const0, 1)
                pool.memset(zero[:], 0.0).then_inc(const0, 1)
                pool.memset(head_ones[:], 0.0).then_inc(const0, 1)
                pool.wait_ge(const0, 4)
                pool.affine_select(out=ident[:], in_=ident[:], compare_op=ALU.not_equal, fill=1.0,
                                   base=0, pattern=[[-1, P]], channel_multiplier=1).then_inc(const1, 1)
                pool.affine_select(out=mask_f[:, SB, :], in_=mask_f[:, SB, :], compare_op=ALU.is_gt, fill=NEG,
                                   base=0, pattern=[[-1, P]], channel_multiplier=1).then_inc(const1, 1)
                pool.affine_select(out=mask_f[:, FX, :], in_=mask_f[:, FX, :], compare_op=ALU.is_ge, fill=NEG,
                                   base=0, pattern=[[-1, P]], channel_multiplier=1).then_inc(const1, 1)
                for half in range(2):
                    pool.wait_ge(const1, 3 + half)
                    r = slice(HD * half, HD * half + HD)
                    pool.memset(head_ones[r, r], 1.0).then_inc(const1, 1)
                pool.wait_ge(const1, 5)
                pool.tensor_copy(maskr[:], mask_f[:]).then_inc(const2, 1)
                pool.tensor_copy(identr[:], ident[:]).then_inc(const2, 1)
                for j in range(2):
                    pool.wait_ge(next_in[j], 16)
                    pool.tensor_tensor(wh[j][:], raw[j][:], zero3, ALU.add).then_inc(next_high, 1)
                    pool.wait_ge(next_high, j + 1)
                    pool.tensor_tensor(wl[j][:], raw[j][:], wh[j][:].bitcast(F32), ALU.subtract).then_inc(next_low, 1)

            @block.scalar
            def _(act):
                def stats(t, j):
                    act.wait_ge(x_in[j], (t // 2 + 1) * 16)
                    after(act, tr_done, t - 1)
                    act.activation(xn[j][:], xt[j][:], ACT.Square, accum_out=stat[:, 0, j:j + 1]).then_inc(sq_done, 1)
                    act.wait_ge(sq_done, t + 1)
                    after(act, inv_done, t - 1)
                    act.activation(stat[:, 1, j:j + 1], stat[:, 0, j:j + 1], ACT.Sqrt, scale=1.0 / D, bias=eps_col).then_inc(root_done, 1)

                def high(t, j):
                    act.wait_ge(tr_done, t + 1)
                    act.activation(hTh[:, :, bass.ds(t * P, P)], turned[j][:].rearrange("p (k t) -> p k t", k=KT), ACT.Copy).then_inc(hi_done, 1)
                act.wait_ge(eps_set, 1)
                stats(0, 0)
                stats(1, 1)
                high(0, 0)
                with act.Fori(1, TB // 2) as i:
                    stats(2 * i, 0)
                    high(2 * i - 1, 1)
                    stats(2 * i + 1, 1)
                    high(2 * i, 0)
                high(TB - 1, 1)

            @block.vector
            def _(dve):
                dve.memset(eps_t[:], EPS).then_inc(eps_set, 1)
                dve.wait_ge(gain_in, 16)

                def norm(t, j):
                    dve.wait_ge(root_done, t + 1)
                    after(dve, xn_done, t - 1)
                    dve.reciprocal(stat[:, 2, j:j + 1], stat[:, 1, j:j + 1]).then_inc(inv_done, 1)
                    dve.wait_ge(inv_done, t + 1)
                    dve.scalar_tensor_tensor(out=xn[j][:], in0=xt[j][:], scalar=stat[:, 2, j:j + 1], in1=gain[:],
                                             op0=ALU.mult, op1=ALU.mult).then_inc(xn_done, 1)

                def low(t, j):
                    dve.wait_ge(hi_done, t + 1)
                    dve.tensor_tensor(hTl[:, :, bass.ds(t * P, P)], turned[j][:].rearrange("p (k t) -> p k t", k=KT),
                                      hTh[:, :, bass.ds(t * P, P)].bitcast(F32), ALU.subtract).then_inc(lo_done, 1)
                norm(0, 0)
                norm(1, 1)
                low(0, 0)
                with dve.Fori(1, TB // 2) as i:
                    norm(2 * i, 0)
                    low(2 * i - 1, 1)
                    norm(2 * i + 1, 1)
                    low(2 * i, 0)
                low(TB - 1, 1)
                dve.wait_ge(colt_done, 1)
                dve.tensor_copy(cols[:].rearrange("p a b -> p (a b)")[:, 0:8 * FT + 16], turned_c[:, 0:8 * FT + 16]).then_inc(col_done, 1)
                dve.wait_ge(small_in, 80)
                dve.tensor_scalar(gqk[:, 2:3], gqk[:, 0:1], HD ** -0.5, None, ALU.mult).then_inc(gq_done, 1)

            @block.tensor
            def _(pe):
                def turn(t, j):
                    pe.wait_ge(xn_done, t + 1)
                    after(pe, hi_done, t - 1)
                    after(pe, lo_done, t - 1)
                    for k in range(KT):
                        mm = pe.transpose(turned[j][:, k * P:(k + 1) * P], xn[j][:, k * P:(k + 1) * P], ident[:])
                    mm.then_inc(tr_done, 1)
                pe.wait_ge(const1, 5)
                turn(0, 0)
                turn(1, 1)
                with pe.Fori(1, TB // 2 - 1) as i:
                    turn(2 * i, 0)
                    turn(2 * i + 1, 1)
                pe.wait_ge(hi_done, TB // 2)
                pe.wait_ge(lo_done, TB // 2)
                pe.wait_ge(next_low, 1)
                project_chunk(pe, proj, 0, 0, 0, KT)
                turn(TB - 2, 0)
                project_chunk(pe, proj, 0, 0, KT, 2 * KT)
                turn(TB - 1, 1)
                project_chunk(pe, proj, 0, 0, 2 * KT, 3 * KT).then_inc(proj_done, 1)
                pe.wait_ge(consts_in, 80)
                for c in range(5):
                    n = 2 * FT if c < 4 else 16
                    mm = pe.transpose(turned_c[:, 2 * FT * c:2 * FT * c + n], rows[0:n, c, :], ident[0:n, 0:n])
                mm.then_inc(colt_done, 1)

        with ExitStack() as ctx:
            sb, ps, sem = maker(ctx)
            qs = [[sb(f"qs{b}{h}", [P, S], F32R) for h in range(2)] for b in range(2)]
            kh = [[sb(f"kh{b}{h}", [P, S], F32R) for h in range(2)] for b in range(2)]
            kl = [[sb(f"kl{b}{h}", [P, S], F32R) for h in range(2)] for b in range(2)]
            v = [sb(f"v{b}", [P, TB, 2, P], F32R) for b in range(2)]
            prob = [sb(f"prob{b}", [P, P * (b + 1)]) for b in range(TB)]
            pth = [sb(f"pth{j}", [P, HALF], F32R) for j in range(2)]
            ptl = [sb(f"ptl{j}", [P, HALF], F32R) for j in range(2)]
            stage = sb("stage", [P, HALF])
            sqt = sb("sqt", [P, HALF])
            cumf = [sb(f"cumf{h}", [P, S]) for h in range(2)]
            otmp = [sb(f"otmp{j}", [P, 2 * P]) for j in range(2)]
            ost = sb("ost", [P, S])
            tick = sb("tick", [P, BLOCKS])
            row_max = sb("row_max", [P, BLOCKS])
            den = sb("den", [P, BLOCKS])
            rden = sb("rden", [P, BLOCKS])
            start_banks = (proj, ps("pv", (P, HALF)))
            pv = start_banks[1]
            scores = [ps(f"scores{j}") for j in range(2)]
            turn_ps = [ps(f"turn{j}", (P, HALF)) for j in range(2)]

            raw_in, w_high, w_low = ring[2]
            next_in, next_high, next_low = ring[3]
            staged, squared = sem("staged"), sem("squared")
            one_head, gate_stored = sem("one_head"), sem("gate_stored")
            inv_rms, qk_high, qk_low = sem("inv_rms"), sem("qk_high"), sem("qk_low")
            k_doubled = [sem(f"k_doubled{b}") for b in range(2)]
            turned, turned_h, turned_l = sem("turned"), sem("turned_h"), sem("turned_l")
            scored, score_used = sem("scored"), sem("score_used")
            absd, expd, lned, summed, scanned = (sem(n) for n in ("absd", "expd", "lned", "summed", "scanned"))
            sb_w, fx_exp, inv_den, fx_w = (sem(n) for n in ("sb_w", "fx_exp", "inv_den", "fx_w"))
            pv_done, half_out, o_done = sem("pv_done"), sem("half_out"), sem("o_done")
            o_stored = sem("o_stored")
            cum_in = sem("cum_in")
            fg, fgd, cum_stored = sem("fg"), sem("fgd"), sem("cum_stored")
            eps_set = sem("eps_set2")
            eps_t = sb("eps_t2", [P, 1])
            block = ctx.enter_context(nc.Block())

            def ordinal(i, target, c):
                return 8 + 12 * i + c + (6 if target == SB else 0)

            def qk_ordinal(i, target, c):
                return 4 + 8 * i + c + (4 if target == SB else 0)

            @block.sync
            def _(sp):
                def load(w, slot, col):
                    after(sp, w_low, w - 1)
                    sp.dma_start(raw[slot][:], win_v[:, :, bass.ds(col, P)]).then_inc(raw_in[slot], 16)

                def double_k(br, f):
                    sp.wait_ge(qk_low, f + 1)
                    sp.wait_ge(qk_high, f + 1)
                    for t in (kh, kl):
                        sp.dma_start(t[br][0][HD:P, :].bitcast(F32), t[br][0][0:HD, :].bitcast(F32)).then_inc(k_doubled[br], 16)
                        sp.dma_start(t[br][1][0:HD, :].bitcast(F32), t[br][1][HD:P, :].bitcast(F32)).then_inc(k_doubled[br], 16)

                def store(i, br):
                    since(sp, o_done, 16 * i + 8 * (br + 1))
                    sp.dma_start(o_dram[bass.ds((i + PAIRS * br) * P, P), :], ost[:]).then_inc(o_stored, 16)

                load(2, 0, H * HD)
                load(3, 1, 2 * H * HD)
                load(4, 0, OFF_FOX)
                load(5, 1, OFF_FOX + H * HD)
                sp.wait_ge(fgd, 4)
                sp.dma_start(cum_dram[:, :], prob[7][0:H, :]).then_inc(cum_stored, 16)
                double_k(SB, 3)
                sp.wait_ge(cum_stored, 16)

                def iteration(i, kind):
                    w = 4 + 6 * i
                    last = kind == "last"
                    load(w + 2, 0, OFF_FOX + 2 * H * HD + i * P)
                    if kind != "first":
                        store(i - 1, FX)
                    since(sp, fx_w, 16 * i)
                    for h in range(2):
                        sp.dma_start(cumf[h][:], cum_dram[bass.ds(2 * i + h, 1), :].to_broadcast([P, S])).then_inc(cum_in, 16)
                    load(w + 3, 1, OFF_GATE if last else (i + 1) * P)
                    load(w + 4, 0, OFF_GATE + D if last else H * HD + (i + 1) * P)
                    double_k(FX, qk_ordinal(i, FX, 3))
                    if last:
                        for j in range(2):
                            sp.wait_ge(w_low, w + 4 + j)
                            sp.dma_start(raw[1 - j][:], win_v[:, :, OFF_GATE + D * j + P:OFF_GATE + D * j + 2 * P]).then_inc(next_in[1 - j], 16)
                    if not last:
                        load(w + 5, 1, 2 * H * HD + (i + 1) * P)
                    store(i, SB)
                    if last:
                        for c in range(4):
                            sp.wait_ge(staged, ordinal(i, SB, c) + 1)
                            sp.dma_start(gate_dram[c // 2, :, HALF * (c % 2):HALF * (c % 2) + HALF], stage[:]).then_inc(gate_stored, 16)
                    if not last:
                        load(w + 6, 0, OFF_FOX + (i + 1) * P)
                        load(w + 7, 1, OFF_FOX + H * HD + (i + 1) * P)
                        double_k(SB, qk_ordinal(i, SB, 3))
                iteration(0, "first")
                with sp.Fori(1, PAIRS - 1) as i:
                    iteration(i, "middle")
                iteration(PAIRS - 1, "last")
                store(PAIRS - 1, FX)
                since(sp, o_stored, 16 * 2 * PAIRS)
                sp.wait_ge(gate_stored, 16 * 4)

            @block.gpsimd
            def _(pool):
                def split(w, turn, slot):
                    pool.wait_ge(raw_in[slot], 16 * turn + 16)
                    after(pool, proj_done, 2 * w - 2)
                    pool.tensor_tensor(wh[slot][:], raw[slot][:], zero3, ALU.add).then_inc(w_high, 1)
                    pool.wait_ge(w_high, w + 1)
                    pool.tensor_tensor(wl[slot][:], raw[slot][:], wh[slot][:].bitcast(F32), ALU.subtract).then_inc(w_low, 1)

                def square(i, k, tiles):
                    target, c = CHUNKS[k]["target"], CHUNKS[k]["c"]
                    if target == SB or c >= 4:
                        return
                    pool.wait_ge(w_low, tiles)
                    pool.wait_ge(qk_low, qk_ordinal(i, target, c))
                    pool.wait_ge(staged, ordinal(i, target, c) + 1)
                    pool.tensor_tensor(sqt[:], stage[:], stage[:], ALU.mult).then_inc(squared, 1)

                def split_qk(i, k, kind, tiles):
                    target, c = CHUNKS[k]["target"], CHUNKS[k]["c"]
                    if c >= 4 or (kind == "last" and target == SB):
                        return
                    aux = SCHEDULES[kind][1]
                    n = CHUNKS[k]["start"] + CHUNKS[k]["slots"]
                    t = slice(HALF * (c % 2), HALF * (c % 2) + HALF)
                    hi, lo = (qs, qs) if c < 2 else (kh, kl)
                    a, b = slice(0, HD), slice(HD, P)
                    if c == 0:
                        since(pool, scored, BLOCKS * i + (0 if target == FX else 16))
                    if target == FX:
                        pool.wait_ge(turned_l, EVENT_BASE + EVENTS * i + aux[n]["e"] + 1)
                    else:
                        pool.wait_ge(staged, ordinal(i, target, c) + 1)
                    done = qk_ordinal(i, target, c)
                    pool.wait_ge(w_low, tiles)
                    pool.wait_ge(qk_low, done)
                    if target == FX:
                        pool.wait_ge(squared, 4 * i + c + 1)
                    pool.tensor_tensor(hi[target][0][a, t], stage[a, :], zero_half[a], ALU.add).then_inc(one_head, 1)
                    pool.wait_ge(one_head, 2 * (done - 4) + 1)
                    pool.tensor_tensor(hi[target][1][b, t], stage[b, :], zero_half[b], ALU.add).then_inc(qk_high, 1)
                    pool.wait_ge(qk_high, done + 1)
                    pool.tensor_tensor(lo[target][0][b if c < 2 else a, t], stage[a, :], hi[target][0][a, t].bitcast(F32), ALU.subtract).then_inc(one_head, 1)
                    pool.wait_ge(one_head, 2 * (done - 4) + 2)
                    pool.tensor_tensor(lo[target][1][a if c < 2 else b, t], stage[b, :], hi[target][1][b, t].bitcast(F32), ALU.subtract).then_inc(qk_low, 1)

                for w in range(2, 5):
                    split(w, w // 2, w % 2)

                def iteration(i, kind):
                    for m in range(6):
                        if m:
                            square(i, 2 * m - 1, 5 + 6 * i + m)
                        if kind != "last" or m < 4:
                            pool.wait_ge(qk_low, 4 + 8 * i + (0, 1, 3, 4, 5, 7)[m])
                            split(5 + 6 * i + m, 2 + 3 * i + (m + 1) // 2, (m + 1) % 2)
                        tiles = 6 + 6 * i + m if kind != "last" else 6 + 6 * i + min(m, 3)
                        if m:
                            split_qk(i, 2 * m - 1, kind, tiles)
                        square(i, 2 * m, tiles)
                        split_qk(i, 2 * m, kind, tiles)
                with pool.Fori(0, PAIRS - 1) as i:
                    iteration(i, "middle")
                iteration(PAIRS - 1, "last")
                tiles = 4 + 6 * (PAIRS - 1) + 5
                for j in range(2):
                    pool.wait_ge(next_in[1 - j], 16)
                    pool.wait_ge(proj_done, 2 * (tiles - 1 + j))
                    pool.tensor_tensor(wh[1 - j][:], raw[1 - j][:], zero3, ALU.add).then_inc(next_high, 1)
                    pool.wait_ge(next_high, j + 1)
                    pool.tensor_tensor(wl[1 - j][:], raw[1 - j][:], wh[1 - j][:].bitcast(F32), ALU.subtract).then_inc(next_low, 1)

            @block.tensor
            def _(pe):
                def multiply(k, slot, w, c, lo, hi):
                    if lo == 0:
                        pe.wait_ge(w_low, w + 1)
                        after(pe, staged, k)
                    mm = project_chunk(pe, proj, slot, c % 2, lo, hi)
                    if hi == CHUNK_MMS:
                        mm.then_inc(proj_done, 1)

                def turn_free(e, i):
                    after(pe, turned_h, EVENT_BASE + EVENTS * i + e - 1)
                    after(pe, turned_l, EVENT_BASE + EVENTS * i + e - 1)

                def turn_v(k, e):
                    pe.wait_ge(staged, k + 1)
                    for j in range(4):
                        mm = pe.transpose(turn_ps[e % 2][:, j * P:(j + 1) * P], stage[:, j * P:(j + 1) * P], ident[:])
                    mm.then_inc(turned, 1)

                for w in range(4):
                    for c in range(2):
                        k = 2 * w + c
                        if k:
                            pe.wait_ge(w_low, w + 1)
                            after(pe, staged, k - 1)
                            project_chunk(pe, start_banks[k % 2], w % 2, c, 0, CHUNK_MMS).then_inc(proj_done, 1)
                for c in range(2):
                    turn_v(6 + c, c + CARRIED)

                def iteration(i, kind):
                    groups, aux = SCHEDULES[kind][:2]
                    pending = None
                    if kind != "first":
                        pending = next(gs[-1] for gs in SCHEDULES["middle"][0][::-1] if gs)
                        pending = dict(pending, e=pending["e"] - EVENTS, g=pending["g"] - NGROUPS, back=1)

                    def weigh(g):
                        slot, h, br = g["g"] % 2, g["unit"] % 2, g["unit"] // 2
                        pe.wait_ge(turned_h, EVENT_BASE + EVENTS * i + g["e"] + 1)
                        pe.wait_ge(turned_l, EVENT_BASE + EVENTS * i + g["e"] + 1)
                        if g["j"] == 0:
                            since(pe, o_done, 16 * (i - g["back"]) + g["q"])
                        diag = g["j"] == g["p"]
                        for kb in range(2):
                            for pt in (pth, ptl):
                                first = g["j"] == 0 and kb == 0 and pt is pth
                                final = diag and kb == 1 and pt is ptl
                                if diag and kb == 1:
                                    mm = pe.matmul(pv[:, P:2 * P], v[br][:, 2 * g["j"] + kb, h, :],
                                                   pt[slot][:, 2 * P:3 * P], start=False, stop=final)
                                else:
                                    mm = pe.matmul(pv[:, 0:2 * P], v[br][:, 2 * g["j"] + kb, h, :],
                                                   pt[slot][:, 2 * P * kb:2 * P * kb + 2 * P], start=first, stop=False)
                        mm.then_inc(pv_done, 1)

                    def score(n):
                        if n < BLOCKS:
                            unit, b, h, br = block_of(n)
                            if n % (2 * TB) == 0:
                                if br == SB:
                                    pe.wait_ge(qk_low, 8 * i + 4)
                                    pe.wait_ge(qk_high, 8 * i + 4)
                                else:
                                    pe.wait_ge(qk_low, qk_ordinal(i, FX, 3) + 1)
                                    pe.wait_ge(qk_high, qk_ordinal(i, FX, 3) + 1)
                                pe.wait_ge(k_doubled[br], 64 * i + 64)
                            since(pe, score_used, BLOCKS * i + n - 1)
                            width = P * (b + 1)
                            for c0 in range(0, width, HALF):
                                c1 = min(c0 + HALF, width)
                                o = scores[n % 2]
                                q_t = qs[br][h][:, b * P:(b + 1) * P]
                                pe.matmul(o[:, c0:c1], q_t, kh[br][h][:, c0:c1], start=True, stop=False)
                                mm = pe.matmul(o[:, c0:c1], q_t, kl[br][h][:, c0:c1], start=False, stop=(c1 < width))
                            mm = pe.matmul(o[:, width - P:width], identr[:], maskr[:, br, :], start=False, stop=True)
                            mm.then_inc(scored, 1)

                    def project(chunk, part, parts):
                        if chunk:
                            target, c, lo, hi = chunk
                            tile = (0 if target == FX else 3) + c // 2
                            cut = [lo + (hi - lo) * p // parts for p in (part, part + 1)]
                            multiply(ordinal(i, target, c), tile % 2, 4 + 6 * i + tile, c, *cut)

                    for n in range(slots(kind)):
                        chunk = chunk_at(n)
                        if kind == "last" and chunk and chunk[0] == SB and chunk[1] >= 4:
                            chunk = None
                        for g in groups[n]:
                            blk = 2 * g["q"] + 1
                            if blk < 2 * TB:
                                pe.wait_ge(sb_w, 16 * i + blk + 1)
                            else:
                                since(pe, fx_w, 16 * (i - g["back"]) + blk - 15)
                            turn_free(g["e"], i)
                            o, col = turn_ps[g["e"] % 2], 0
                            for kb in (2 * g["j"], 2 * g["j"] + 1):
                                for b in (2 * g["p"], 2 * g["p"] + 1):
                                    if kb <= b:
                                        mm = pe.transpose(o[:, col:col + P], prob[b][:, kb * P:(kb + 1) * P], ident[:])
                                        col += P
                            mm.then_inc(turned, 1)
                            if g is groups[n][0]:
                                score(n)
                                if pending is not None:
                                    weigh(pending)
                                project(chunk, 0, len(groups[n]))
                            else:
                                project(chunk, groups[n].index(g), len(groups[n]))
                                weigh(pending)
                            pending = g
                        if not groups[n]:
                            score(n)
                            project(chunk, 0, 1)
                        a = aux[n]
                        if a:
                            turn_free(a["e"], i)
                            if a["c"] >= 4:
                                turn_v(ordinal(i - a["back"], a["target"], a["c"]), a["e"])
                            else:
                                pe.wait_ge(squared, 4 * i + a["c"] + 1)
                                pe.matmul(turn_ps[a["e"] % 2][:], head_ones[:], sqt[:], start=True, stop=True).then_inc(turned, 1)
                    if kind == "last":
                        weigh(pending)
                iteration(0, "first")
                with pe.Fori(1, PAIRS - 1) as i:
                    iteration(i, "middle")
                iteration(PAIRS - 1, "last")

            @block.scalar
            def _(act):
                act.preload_act_table_set("natural_log_exp_and_others")
                act.wait_ge(eps_set, 1)

                def stage_copy(k, c, scale, qk_before, e_before, bank=proj):
                    act.wait_ge(proj_done, k + 1)
                    if c in (0, 5):
                        after(act, turned, e_before)
                    else:
                        after(act, qk_low, qk_before)
                        after(act, qk_high, qk_before)
                    act.activation(stage[:], bank[:], ACT.Copy, scale=scale).then_inc(staged, 1)

                def split_high(target, c):
                    t = slice(HALF * (c % 2), HALF * (c % 2) + HALF)
                    dst = qs[target] if c < 2 else kh[target]
                    act.activation(dst[0][0:HD, t], stage[0:HD, :], ACT.Copy)
                    act.activation(dst[1][HD:P, t], stage[HD:P, :], ACT.Copy).then_inc(qk_high, 1)

                def v_high(target, c, e):
                    dst = v[target][:, 4 * (c % 2):4 * (c % 2) + 4, :, 0:HD]
                    for h in range(2):
                        a = act.activation(dst[:, :, h, :], turn_ps[e % 2][:].rearrange("p (t h c) -> p t h c", h=2, c=HD)[:, :, h, :], ACT.Copy)
                    a.then_inc(turned_h, 1)

                for c in range(2):
                    t = slice(HALF * c, HALF * c + HALF)
                    act.wait_ge(proj_done, c + 1)
                    act.activation(prob[6][0:H, 0:HALF] if c == 0 else prob[5][0:H, 0:HALF], start_banks[c][0:H, :], ACT.Identity, bias=bfc[:, 0:1]).then_inc(staged, 1)
                act.wait_ge(staged, 2)
                for c in range(2):
                    xg = prob[6][0:H, 0:HALF] if c == 0 else prob[5][0:H, 0:HALF]
                    act.activation(prob[7][0:H, HALF * c:HALF * c + HALF], xg, ACT.Abs).then_inc(fg, 1)
                act.wait_ge(fg, 2)
                act.activation(prob[7][0:H, :], prob[7][0:H, :], ACT.Exp, scale=-1.0).then_inc(fg, 1)
                act.wait_ge(fg, 3)
                act.activation(prob[7][0:H, :], prob[7][0:H, :], ACT.Ln, bias=1.0).then_inc(fg, 1)

                for c in range(6):
                    k = 2 + c
                    stage_copy(k, c, HD ** -0.5 if c < 2 else 1.0, c if c else 0, 1 if c == 5 else 0, start_banks[k % 2])
                    act.wait_ge(staged, k + 1)
                    if c < 4:
                        split_high(SB, c)
                    else:
                        act.wait_ge(turned, c - 4 + 1)
                        v_high(SB, c, c - 4 + CARRIED)

                def iteration(i, kind):
                    groups, aux = SCHEDULES[kind][:2]
                    e0 = EVENT_BASE + EVENTS * i

                    g0 = NGROUPS * i - CARRIED_GROUPS

                    def group_high(g):
                        w = (4 if g["j"] < g["p"] else 3) * P
                        act.wait_ge(turned, e0 + g["e"] + 1)
                        since(act, pv_done, g0 + g["g"] - 1)
                        act.activation(pth[g["g"] % 2][:, 0:w], turn_ps[g["e"] % 2][:, 0:w], ACT.Copy).then_inc(turned_h, 1)

                    for n in range(slots(kind)):
                        gs = groups[n]
                        copied = copied_at(n, kind)
                        if copied:
                            target, c, back = copied
                            k = ordinal(i - back, target, c)
                            e_before = 0
                            if c == 5:
                                e_before = e0 + v_event(kind, target, 4, back) + 1
                            elif c == 0:
                                e_before = e0 + (v_event(kind, SB, 5, 1) if target == FX else v_event(kind, FX, 5)) + 1
                            gate = kind == "last" and target == SB and not back
                            if gate and c:
                                act.wait_ge(proj_done, k + 1)
                                act.wait_ge(gate_stored, 16 * c)
                                act.activation(stage[:], proj[:], ACT.Copy).then_inc(staged, 1)
                            else:
                                stage_copy(k, c, HD ** -0.5 if (target == SB and c < 2 and not gate) else 1.0,
                                           qk_ordinal(i - back, target, min(c, 4)), e_before)
                        m, back = place(n, FIRST_SUM)
                        if n % 2 == 0 and not (back and kind == "first"):
                            q = (m - FIRST_SUM) // 2
                            h = (2 * q // TB) % 2
                            since(act, pv_done, g0 + last_of_pair(kind, q, back, "g") + 1)
                            since(act, o_done, 16 * (i - back) + q - 1)
                            src, dst = (slice(HD, P), slice(0, HD)) if h == 0 else (slice(0, HD), slice(HD, P))
                            act.activation(otmp[q % 2][dst, :], pv[src, 0:2 * P], ACT.Copy).then_inc(half_out, 1)
                        fin = copied_at(n - 1, kind)
                        fin_e = aux[n - 1]["e"] if fin and aux[n - 1] else None
                        if fin and fin[0] == FX and fin[1] < 4:
                            act.wait_ge(turned, e0 + fin_e + 1)
                            act.activation(sqt[:], turn_ps[fin_e % 2][:], ACT.Ln, scale=1.0 / HD, bias=eps_t[:, 0:1]).then_inc(turned_h, 1)
                            act.wait_ge(turned_h, e0 + fin_e + 1)
                            act.activation(sqt[:], sqt[:], ACT.Exp, scale=-0.5).then_inc(inv_rms, 1)
                        if fin and fin[1] >= 4:
                            act.wait_ge(turned, e0 + fin_e + 1)
                            since(act, pv_done, NGROUPS * (i - fin[2]) + (0 if fin[0] == FX else NGROUPS // 2))
                            v_high(fin[0], fin[1], fin_e)
                        if n < BLOCKS:
                            unit, b, h, br = block_of(n)
                        if gs:
                            group_high(gs[0])
                        if n < 2 * TB:
                            pr, s = prob[b], scores[n % 2]
                            since(act, scored, BLOCKS * i + n + 1)
                            if tile_free_event(kind, n) is not None:
                                act.wait_ge(turned, e0 + tile_free_event(kind, n) + 1)
                            if n == 2 * PAIR_ORDER.index(3):
                                act.wait_ge(cum_stored, 16)
                            act.activation(pr[:], s[:, 0:P * (b + 1)], ACT.Abs).then_inc(absd, 1)
                            act.wait_ge(absd, 16 * i + n + 1)
                            act.activation(pr[:], pr[:], ACT.Exp, scale=-1.0).then_inc(expd, 1)
                            for g in gs[1:]:
                                group_high(g)
                            act.wait_ge(expd, 16 * i + n + 1)
                            act.activation(pr[:], pr[:], ACT.Ln, bias=1.0).then_inc(lned, 1)
                        else:
                            for g in gs[1:]:
                                group_high(g)
                        if 1 <= n <= 2 * TB:
                            pb = prob[block_of(n - 1)[1]]
                            since(act, score_used, BLOCKS * i + n)
                            act.activation(pb[:], pb[:], ACT.Exp).then_inc(sb_w, 1)
                        if 2 * TB <= n < BLOCKS:
                            since(act, score_used, BLOCKS * i + n + 1)
                            act.activation(prob[b][:], prob[b][:], ACT.Exp, scale=-1.0, bias=row_max[:, n:n + 1],
                                           accum_out=den[:, n:n + 1]).then_inc(fx_exp, 1)
                iteration(0, "first")
                with act.Fori(1, PAIRS - 1) as i:
                    iteration(i, "middle")
                iteration(PAIRS - 1, "last")

            @block.vector
            def _(dve):
                dve.memset(eps_t[:], EPS).then_inc(eps_set, 1)
                for c, start in enumerate((fx_w, score_used, o_done, pv_done, scored, o_stored)):
                    dve.memset(tick[:, c:c + 1], 0.0).then_inc(start, 1)

                def split_low(target, c):
                    t = slice(HALF * (c % 2), HALF * (c % 2) + HALF)
                    hi = qs[target] if c < 2 else kh[target]
                    lo = qs[target] if c < 2 else kl[target]
                    a, b = slice(0, HD), slice(HD, P)
                    dve.tensor_tensor(lo[0][b if c < 2 else a, t], stage[a, :], hi[0][a, t].bitcast(F32), ALU.subtract)
                    dve.tensor_tensor(lo[1][a if c < 2 else b, t], stage[b, :], hi[1][b, t].bitcast(F32), ALU.subtract).then_inc(qk_low, 1)

                def v_low(target, c, e):
                    t = slice(4 * (c % 2), 4 * (c % 2) + 4)
                    for h in range(2):
                        d = dve.tensor_tensor(v[target][:, t, h, HD:P],
                                              turn_ps[e % 2][:].rearrange("p (t h c) -> p t h c", h=2, c=HD)[:, :, h, :],
                                              v[target][:, t, h, 0:HD].bitcast(F32), ALU.subtract)
                    d.then_inc(turned_l, 1)

                for c in range(2):
                    xg = prob[6][0:H, 0:HALF] if c == 0 else prob[5][0:H, 0:HALF]
                    dve.wait_ge(fg, 2)
                    dve.tensor_scalar(xg, xg, 0.0, None, ALU.min).then_inc(fgd, 1)
                dve.wait_ge(fg, 4)
                dve.wait_ge(fgd, 2)
                dve.tensor_tensor_scan(prob[7][0:H, 0:HALF], prob[7][0:H, 0:HALF], prob[6][0:H, 0:HALF], 0.0, ALU.add, ALU.subtract).then_inc(fgd, 1)
                dve.wait_ge(fgd, 3)
                dve.tensor_tensor_scan(prob[7][0:H, HALF:S], prob[7][0:H, HALF:S], prob[5][0:H, 0:HALF], prob[7][0:H, HALF - 1:HALF], ALU.add, ALU.subtract).then_inc(fgd, 1)
                for c in range(6):
                    if c < 4:
                        dve.wait_ge(qk_high, c + 1)
                        split_low(SB, c)
                    else:
                        dve.wait_ge(turned_h, c - 4 + 1)
                        v_low(SB, c, c - 4 + CARRIED)

                def iteration(i, kind):
                    groups, aux = SCHEDULES[kind][:2]
                    e0 = EVENT_BASE + EVENTS * i

                    def group_low(g):
                        w = (4 if g["j"] < g["p"] else 3) * P
                        dve.wait_ge(turned_h, e0 + g["e"] + 1)
                        dve.tensor_tensor(ptl[g["g"] % 2][:, 0:w], turn_ps[g["e"] % 2][:, 0:w],
                                          pth[g["g"] % 2][:, 0:w].bitcast(F32), ALU.subtract).then_inc(turned_l, 1)

                    for n in range(slots(kind)):
                        gs = groups[n]
                        m, back = place(n, FIRST_SUM)
                        if n % 2 == 0 and not (back and kind == "first"):
                            q = (m - FIRST_SUM) // 2
                            h, br, p = (2 * q // TB) % 2, q // 8, PAIR_ORDER[q % (TB // 2)]
                            r = slice(0, HD) if h == 0 else slice(HD, P)
                            dve.wait_ge(half_out, 16 * (i - back) + q + 1)
                            if q % 8 == 0:
                                since(dve, o_stored, 32 * i + 16 * br)
                            dve.tensor_tensor(ost[r, 2 * P * p:2 * P * (p + 1)], pv[r, 0:2 * P], otmp[q % 2][r, :], ALU.add).then_inc(o_done, 1)
                        if n < BLOCKS:
                            unit, b, h, br = block_of(n)
                        m, back = place(n, FIRST_RATIO)
                        m -= 1
                        if 2 * TB <= m < BLOCKS and not (back and kind == "first"):
                            f = m - 2 * TB
                            dve.wait_ge(fx_exp, 16 * (i - back) + f + 1)
                            dve.reciprocal(rden[:, m:m + 1], den[:, m:m + 1]).then_inc(inv_den, 1)
                            dve.wait_ge(inv_den, 16 * (i - back) + f + 1)
                            pb = prob[block_of(m)[1]]
                            dve.tensor_scalar(pb[:], pb[:], rden[:, m:m + 1], None, ALU.mult).then_inc(fx_w, 1)
                        fin = copied_at(n - 1, kind)
                        fin_e = aux[n - 1]["e"] if fin and aux[n - 1] else None

                        def finish_aux():
                            if not fin:
                                return
                            target, c = fin[:2]
                            if c >= 4:
                                dve.wait_ge(turned_h, e0 + fin_e + 1)
                                v_low(target, c, fin_e)
                            elif target == FX:
                                dve.wait_ge(inv_rms, 4 * i + c + 1)
                                dve.scalar_tensor_tensor(out=stage[:], in0=stage[:], scalar=gqk[:, 2:3] if c < 2 else gqk[:, 1:2],
                                                         in1=sqt[:], op0=ALU.mult, op1=ALU.mult).then_inc(turned_l, 1)

                        finish_aux()
                        if gs:
                            group_low(gs[0])
                        if n < 2 * TB:
                            pr, s, w = prob[b], scores[n % 2], P * (b + 1)
                            dve.wait_ge(lned, 16 * i + n + 1)
                            dve.scalar_tensor_tensor(out=pr[:], in0=s[:, 0:w], scalar=0.0, in1=pr[:], op0=ALU.max, op1=ALU.add).then_inc(summed, 1)
                            for g in gs[1:]:
                                group_low(g)
                            dve.wait_ge(summed, 16 * i + n + 1)
                            dve.tensor_tensor_scan(pr[:, ::-1], pr[:, ::-1], pr[:, ::-1], 0.0, ALU.add, ALU.bypass).then_inc(scanned, 1)
                            dve.wait_ge(scanned, 16 * i + n + 1)
                            dve.tensor_tensor(pr[:], s[:, 0:w], pr[:], ALU.subtract).then_inc(score_used, 1)
                        elif n < BLOCKS:
                            w = P * (b + 1)
                            since(dve, scored, BLOCKS * i + n + 1)
                            dve.wait_ge(turned, e0 + tile_free_event(kind, n) + 1)
                            if n == 2 * TB:
                                dve.wait_ge(cum_in, 32 * i + 32)
                            dve.memset(tick[:, n:n + 1], 0.0)
                            dve.tensor_tensor_reduce(out=prob[b][:], in0=scores[n % 2][:, 0:w], in1=cumf[h][:, 0:w], scale=-1.0,
                                                     scalar=3.0e38, op0=ALU.add, op1=ALU.min,
                                                     accum_out=row_max[:, n:n + 1]).then_inc(score_used, 1)
                            for g in gs[1:]:
                                group_low(g)
                        else:
                            for g in gs[1:]:
                                group_low(g)
                iteration(0, "first")
                with dve.Fori(1, PAIRS - 1) as i:
                    iteration(i, "middle")
                iteration(PAIRS - 1, "last")

        projecting.close()
        mixing = whole.enter_context(ExitStack())
        sbm, _, _ = maker(mixing)
        mix = sbm("mix", [P, KT, S])
        with ExitStack() as ctx:
            sb, ps, sem = maker(ctx)
            oh = sb("oh", [P, KT, S], F32R)
            ol = sb("ol", [P, KT, S], F32R)
            sig = [sb(f"sig{b}", [P, S]) for b in range(2)]
            gate_ps = [ps(f"gate{b}") for b in range(2)]
            y_ps = [ps(f"y{b}") for b in range(2)]
            gate0 = [sb(f"gate0{b}", [P, S]) for b in range(2)]
            gate0_in = [sem(f"gate0_in{b}") for b in range(2)]
            gate0_done = sem("gate0_done")
            o_in = [sem(f"o_in{k}") for k in range(KT)]
            o_high, o_low = sem("o_high"), sem("o_low")
            raw_in, w_high, w_low = ring[3]
            next_in, next_high, next_low = ring[4]
            w_used = sem("w3_used")
            gated, y_done = sem("gate_done"), sem("y_done")
            sig_done, mulled, mixed = sem("sig_done"), sem("mulled"), sem("mixed")
            block = ctx.enter_context(nc.Block())

            @block.sync
            def _(sp):
                def gate(m, b, slot):
                    sp.dma_start(raw[slot][:], win_v[:, :, bass.ds(OFF_GATE + D * b + m * P, P)]).then_inc(raw_in[slot], 16)

                def branches(m, slot):
                    sp.dma_start(raw[slot][:, 0:4, :], wosb_v[:, :, bass.ds(m * P, P)]).then_inc(raw_in[slot], 16)
                    sp.dma_start(raw[slot][:, 4:8, :], wofx_v[:, :, bass.ds(m * P, P)]).then_inc(raw_in[slot], 16)

                def weights(m, j):
                    sp.wait_ge(w_low, 3 * m - 3)
                    gate(m, 0, 1 - j)
                    sp.wait_ge(w_low, 3 * m - 1)
                    gate(m, 1, j)
                    branches(m, 1 - j)
                sp.wait_ge(w_low, 1)
                branches(0, 1)
                for k in range(KT):
                    sp.dma_start(ol[:, k, :].bitcast(F32), o_dram[k * P:(k + 1) * P, :]).then_inc(o_in[k], 16)
                for b in range(2):
                    sp.dma_start(gate0[b][:], gate_dram[b]).then_inc(gate0_in[b], 16)
                sp.wait_ge(w_low, 2)
                branches(1, 0)
                with sp.Fori(1, KT // 2) as i:
                    weights(2 * i, 0)
                    weights(2 * i + 1, 1)
                for j in range(2):
                    sp.wait_ge(w_low, 3 * KT - 3 + j)
                    sp.dma_start(raw[1 - j][:].rearrange(flat), w_out[0, j * P:(j + 1) * P, :]).then_inc(next_in[1 - j], 16)

            @block.gpsimd
            def _(pool):
                def split(u, slot, loads):
                    pool.wait_ge(raw_in[slot], 16 * loads)
                    after(pool, w_used, u - 1)
                    pool.tensor_tensor(wh[slot][:], raw[slot][:], zero3, ALU.add).then_inc(w_high, 1)
                    pool.wait_ge(w_high, u + 1)
                    pool.tensor_tensor(wl[slot][:], raw[slot][:], wh[slot][:].bitcast(F32), ALU.subtract).then_inc(w_low, 1)
                split(2, 1, 3)
                split(3, 0, 3)
                with pool.Fori(1, KT // 2) as i:
                    for t, loads in enumerate((1, 1, 3, 2, 4, 4)):
                        split(6 * i - 2 + t, (t + 1) % 2, 4 * i - 1 + loads)
                pool.wait_ge(next_in[1], 16)
                pool.wait_ge(w_used, 3 * KT - 3)
                pool.tensor_tensor(wh[1][:], raw[1][:], zero3, ALU.add).then_inc(next_high, 1)
                pool.wait_ge(next_high, 1)
                pool.tensor_tensor(wl[1][:], raw[1][:], wh[1][:].bitcast(F32), ALU.subtract).then_inc(next_low, 1)

            @block.tensor
            def _(pe):
                def product(o, slot, kts, first_kt, mh, ml):
                    for kt in kts:
                        for stat_, mov in ((wh, mh), (wh, ml), (wl, mh)):
                            for c in range(2):
                                mm = pe.matmul(o[:, HALF * c:HALF * c + HALF], stat_[slot][:, kt, :],
                                               mov[:, kt, HALF * c:HALF * c + HALF],
                                               start=(kt == kts[0] and stat_ is wh and mov is mh),
                                               stop=(kt == kts[-1] and stat_ is wl))
                    return mm

                def gates(u, m, j):
                    for b in range(2):
                        pe.wait_ge(w_low, u + b + 1)
                        after(pe, sig_done, 2 * m + b - 3)
                        product(gate_ps[b], (1 - j + b) % 2, range(KT), 0, hTh, hTl).then_inc(w_used, 1)

                def projections(u, m, slot):
                    pe.wait_ge(w_low, u + 1)
                    after(pe, mulled, 2 * m)
                    for b in range(2):
                        mm = product(y_ps[b], slot, range(4 * b, 4 * b + 4), 0, oh, ol)
                    mm.then_inc(w_used, 1)
                gates(0, 1, 0)
                pe.wait_ge(o_low, KT)
                pe.wait_ge(o_high, KT)
                projections(2, 0, 1)
                projections(3, 1, 0)
                with pe.Fori(1, KT // 2) as i:
                    for j in range(2):
                        m = 2 * i + j
                        gates(3 * m - 2, m, j)
                        projections(3 * m, m, 1 - j)

            @block.scalar
            def _(act):
                for k in range(KT):
                    act.wait_ge(o_in[k], 16)
                    act.activation(oh[:, k, :], ol[:, k, :].bitcast(F32), ACT.Copy).then_inc(o_high, 1)
                for b in range(2):
                    act.wait_ge(gate0_in[b], 16)
                    act.activation(gate0[b][:], gate0[b][:], ACT.Sigmoid, bias=cols[:, 4, b * KT:b * KT + 1]).then_inc(gate0_done, 1)

                def sigmoids(m, used):
                    for b in range(2):
                        act.wait_ge(w_used, used + b)
                        if not isinstance(m, int):
                            act.wait_ge(mixed, m)
                        act.activation(sig[b][:], gate_ps[b][:], ACT.Sigmoid,
                                       bias=cols[:, 4, bass.ds(m + b * KT, 1)]).then_inc(sig_done, 1)
                sigmoids(1, 1)
                with act.Fori(2, KT) as m:
                    sigmoids(m, 3 * m - 1)

            @block.vector
            def _(dve):
                for k in range(KT):
                    dve.wait_ge(o_high, k + 1)
                    dve.tensor_tensor(ol[:, k, :], ol[:, k, :].bitcast(F32), oh[:, k, :].bitcast(F32), ALU.subtract).then_inc(o_low, 1)

                def output_tile(m, used, gates, gates_done, first_gate):
                    dve.wait_ge(w_used, used)
                    for b in range(2):
                        dve.wait_ge(gates_done, first_gate + b)
                        dve.tensor_tensor(gates[b][:], gates[b][:], y_ps[b][:], ALU.mult).then_inc(mulled, 1)
                    dve.wait_ge(mulled, 2 * m + 2)
                    dve.tensor_tensor(mix[:, bass.ds(m, 1), :].rearrange("p a b -> p (a b)"), gates[0][:], gates[1][:], ALU.add).then_inc(mixed, 1)
                output_tile(0, 3, gate0, gate0_done, 1)
                output_tile(1, 4, sig, sig_done, 1)
                with dve.Fori(2, KT) as m:
                    output_tile(m, 3 * m + 1, sig, sig_done, 2 * m - 1)

        with ExitStack() as ctx:
            sb, ps, sem = maker(ctx)
            woh_rest = sb("woh", [P, KT - 2, D], F32R)
            wol_rest = sb("wol", [P, KT - 2, D], F32R)
            woh = [wh[1 - k][:].rearrange(flat) if k < 2 else woh_rest[:, k - 2, :] for k in range(KT)]
            wol = [wl[1 - k][:].rearrange(flat) if k < 2 else wol_rest[:, k - 2, :] for k in range(KT)]
            mh = [sb(f"mh{j}", [P, KT, P], F32R) for j in range(2)]
            ml = [sb(f"ml{j}", [P, KT, P], F32R) for j in range(2)]
            gain = sb("gain4", [P, D])
            xt = [sb(f"xt4{j}", [P, D]) for j in range(2)]
            xn = [raw[j][:].rearrange(flat) for j in range(2)]
            stages = [raw[1][:].rearrange(flat), raw[0][:].rearrange(flat), xt[0][:], xt[1][:]]
            stage_of = [0, 1, 0, 2, 3, 1, 0, 2]
            turn_of = [stage_of[:k].count(stage_of[k]) for k in range(KT)]
            stat = sb("stat4", [P, 3, 2])
            proj = [ps(f"outp{j}") for j in range(2)]
            turned = [ps(f"turned4{j}") for j in range(2)]
            first_in, w_high, w_low = ring[4]
            w_in_s = first_in[::-1] + [sem(f"w4_in{j}") for j in (2, 3)]
            next_in, next_high, next_low = ring[5]
            x_in = [sem(f"x4_in{j}") for j in range(2)]
            gain_in, x2_out = sem("gain4_in"), [sem(f"x2_out{j}") for j in range(2)]
            m_high, m_low, proj_done, x2_done = sem("m_high"), sem("m_low"), sem("proj4"), sem("x2_done")
            sq_done, root_done, inv_done, xn_done = (sem(n + "4") for n in ("sq", "root", "inv", "xn"))
            tr_done, hi_done, lo_done = sem("tr4"), sem("hi4"), sem("lo4")
            eps_set = sem("eps_set4")
            eps_t = sb("eps_t4", [P, 1])
            tick = sb("tick4", [P, 5])
            block = ctx.enter_context(nc.Block())

            @block.sync
            def _(sp):
                for k in range(2, KT):
                    if turn_of[k]:
                        sp.wait_ge(w_low, max(m for m in range(k) if stage_of[m] == stage_of[k]) + 1)
                    sp.dma_start(stages[stage_of[k]], w_out[0, k * P:(k + 1) * P, :]).then_inc(w_in_s[stage_of[k]], 16)
                sp.wait_ge(w_low, KT)
                sp.dma_start(gain[:], g_ffn.to_broadcast([P, D])).then_inc(gain_in, 16)

                def load(t, j, turn):
                    since(sp, xn_done, t - 1)
                    after(sp, x2_out[j], 16 * turn)
                    sp.dma_start(xt[j][:], x[0, bass.ds(t * P, P), :]).then_inc(x_in[j], 16)

                def store(t, j):
                    sp.wait_ge(x2_done, t + 1)
                    sp.dma_start(x2_dram[bass.ds(t * P, P), :], xt[j][:]).then_inc(x2_out[j], 16)
                load(0, 0, 0)
                load(1, 1, 0)
                with sp.Fori(0, TB // 2 - 1) as i:
                    for j in range(2):
                        store(2 * i + j, j)
                    for j in range(2):
                        load(2 * i + 2 + j, j, i + 1)
                for j in range(2):
                    store(TB - 2 + j, j)
                for j in range(2):
                    since(sp, tr_done, TB - 1 + j)
                    sp.dma_start(raw[j][:], wup_v[:, :, j * FF:j * FF + P]).then_inc(next_in[j], 16)
                for j in range(2):
                    sp.wait_ge(x2_out[j], 16 * (TB // 2))

            @block.gpsimd
            def _(pool):
                pool.wait_ge(next_high, 1)
                pool.tensor_tensor(wl[0][:], raw[0][:], wh[0][:].bitcast(F32), ALU.subtract).then_inc(next_low, 1)

            @block.tensor
            def _(pe):
                def product(j, kt):
                    for stat_, mov in ((mh, woh), (mh, wol), (ml, woh)):
                        for c in range(2):
                            mm = pe.matmul(proj[j][:, HALF * c:HALF * c + HALF], stat_[j][:, kt, :],
                                           mov[kt][:, HALF * c:HALF * c + HALF],
                                           start=(kt == 0 and stat_ is mh and mov is woh),
                                           stop=(kt == KT - 1 and stat_ is ml))
                    return mm

                def project(t, j):
                    pe.wait_ge(m_low, t + 1)
                    pe.wait_ge(x2_done, t - 1)
                    for kt in range(KT):
                        mm = product(j, kt)
                    mm.then_inc(proj_done, 1)

                def turn(t, j):
                    since(pe, xn_done, t + 1)
                    since(pe, hi_done, t - 1)
                    since(pe, lo_done, t - 1)
                    for k in range(KT):
                        mm = pe.transpose(turned[j][:, k * P:(k + 1) * P], xn[j][:, k * P:(k + 1) * P], ident[:])
                    mm.then_inc(tr_done, 1)
                for kts in [(kt,) for kt in range(KT - 2)] + [(KT - 2, KT - 1)]:
                    pe.wait_ge(w_low, kts[-1] + 1)
                    for t in range(2):
                        if kts[0] == 0:
                            pe.wait_ge(m_low, t + 1)
                        for kt in kts:
                            mm = product(t, kt)
                        if kt == KT - 1:
                            mm.then_inc(proj_done, 1)
                project(2, 0)
                turn(0, 0)
                project(3, 1)
                turn(1, 1)
                with pe.Fori(2, TB // 2) as i:
                    for j in range(2):
                        project(2 * i + j, j)
                        turn(2 * i + j - 2, j)
                turn(TB - 2, 0)
                turn(TB - 1, 1)

            @block.scalar
            def _(act):
                for k in range(KT):
                    if k:
                        act.wait_ge(w_in_s[stage_of[k]], 16 * turn_of[k] + 16)
                        act.activation(woh[k], stages[stage_of[k]], ACT.Copy).then_inc(w_high, 1)
                    if k < 2:
                        act.activation(mh[k][:], mix[:, :, k * P:(k + 1) * P], ACT.Copy).then_inc(m_high, 1)
                act.wait_ge(eps_set, 1)
                act.wait_ge(w_low, KT)

                def stats(t, j):
                    act.wait_ge(x2_done, t + 1)
                    since(act, tr_done, t - 1)
                    act.activation(xn[j], xt[j][:], ACT.Square, accum_out=stat[:, 0, j:j + 1]).then_inc(sq_done, 1)
                    act.wait_ge(sq_done, t + 1)
                    since(act, inv_done, t - 1)
                    act.activation(stat[:, 1, j:j + 1], stat[:, 0, j:j + 1], ACT.Sqrt, scale=1.0 / D, bias=eps_t[:, 0:1]).then_inc(root_done, 1)

                def mix_high(t, j):
                    act.wait_ge(proj_done, t - 1)
                    act.activation(mh[j][:], mix[:, :, bass.ds(t * P, P)], ACT.Copy).then_inc(m_high, 1)

                def high(t, j):
                    since(act, tr_done, t + 1)
                    act.activation(hTh[:, :, bass.ds(t * P, P)], turned[j][:].rearrange("p (k t) -> p k t", k=KT), ACT.Copy).then_inc(hi_done, 1)
                mix_high(2, 0)
                stats(0, 0)
                mix_high(3, 1)
                stats(1, 1)
                with act.Fori(1, TB // 2 - 1) as i:
                    for j in range(2):
                        stats(2 * i + j, j)
                        mix_high(2 * i + j + 2, j)
                        high(2 * i + j - 2, j)
                stats(TB - 2, 0)
                high(TB - 4, 0)
                high(TB - 3, 1)
                stats(TB - 1, 1)
                high(TB - 2, 0)
                high(TB - 1, 1)
                act.wait_ge(proj_done, TB)
                act.wait_ge(next_in[0], 16)
                act.activation(wh[0][:], raw[0][:], ACT.Copy).then_inc(next_high, 1)

            @block.vector
            def _(dve):
                dve.memset(eps_t[:], EPS).then_inc(eps_set, 1)
                for c, start in enumerate((tr_done, hi_done, lo_done, inv_done, xn_done)):
                    dve.memset(tick[:, c:c + 1], 0.0).then_inc(start, 1)
                for k in range(KT):
                    if k:
                        dve.wait_ge(w_high, k + 1)
                        dve.tensor_tensor(wol[k], stages[stage_of[k]], woh[k].bitcast(F32), ALU.subtract).then_inc(w_low, 1)
                    if k < 2:
                        dve.wait_ge(m_high, k + 1)
                        dve.tensor_tensor(ml[k][:], mix[:, :, k * P:(k + 1) * P], mh[k][:].bitcast(F32), ALU.subtract).then_inc(m_low, 1)
                dve.wait_ge(gain_in, 16)

                def residual(t, j, turn):
                    dve.wait_ge(proj_done, t + 1)
                    dve.wait_ge(x_in[j], 16 * turn + 16)
                    dve.tensor_tensor(xt[j][:], proj[j][:], xt[j][:], ALU.add).then_inc(x2_done, 1)

                def norm(t, j):
                    dve.wait_ge(root_done, t + 1)
                    since(dve, xn_done, t - 1)
                    dve.reciprocal(stat[:, 2, j:j + 1], stat[:, 1, j:j + 1]).then_inc(inv_done, 1)
                    since(dve, inv_done, t + 1)
                    dve.scalar_tensor_tensor(out=xn[j], in0=xt[j][:], scalar=stat[:, 2, j:j + 1], in1=gain[:],
                                             op0=ALU.mult, op1=ALU.mult).then_inc(xn_done, 1)

                def mix_low(t, j):
                    dve.wait_ge(m_high, t + 1)
                    dve.tensor_tensor(ml[j][:], mix[:, :, bass.ds(t * P, P)], mh[j][:].bitcast(F32), ALU.subtract).then_inc(m_low, 1)

                def low(t, j):
                    since(dve, hi_done, t + 1)
                    dve.tensor_tensor(hTl[:, :, bass.ds(t * P, P)], turned[j][:].rearrange("p (k t) -> p k t", k=KT),
                                      hTh[:, :, bass.ds(t * P, P)].bitcast(F32), ALU.subtract).then_inc(lo_done, 1)
                residual(0, 0, 0)
                mix_low(2, 0)
                norm(0, 0)
                residual(1, 1, 0)
                mix_low(3, 1)
                norm(1, 1)
                with dve.Fori(1, TB // 2 - 1) as i:
                    for j in range(2):
                        residual(2 * i + j, j, i)
                        norm(2 * i + j, j)
                        mix_low(2 * i + j + 2, j)
                        low(2 * i + j - 2, j)
                residual(TB - 2, 0, TB // 2 - 1)
                norm(TB - 2, 0)
                low(TB - 4, 0)
                residual(TB - 1, 1, TB // 2 - 1)
                low(TB - 3, 1)
                norm(TB - 1, 1)
                low(TB - 2, 0)
                low(TB - 1, 1)
        mixing.close()

        sb, _, sem = maker(whole)
        act_t = sb("act_t", [P, FT, S])
        ah = [sb(f"ah{j}", [P, HALF], F32R) for j in range(2)]
        al = [sb(f"al{j}", [P, HALF], F32R) for j in range(2)]
        a_high, a_low = sem("a_high"), sem("a_low")
        with ExitStack() as ctx:
            sb, ps, sem = maker(ctx)
            u = [[sb(f"u{j}{c}", [P, S]) for c in range(2)] for j in range(2)]
            u_ps = [[ps(f"u_ps{j}{c}") for c in range(2)] for j in range(2)]
            QT = HALF // P
            rawf, whf, wlf = ([t[j][:].rearrange(flat) for j in range(2)] for t in (raw, wh, wl))
            x2 = [u[t // 2][t % 2] for t in range(QT)]
            acc = [u_ps[t // 2][t % 2] for t in range(QT)]
            used, acc_done, summed = sem("used6"), sem("acc_done"), sem("summed6")
            x2_in, stored = [sem(f"x2_in{t}") for t in range(QT)], [sem(f"stored{t}") for t in range(QT)]
            raw_in, w_high, w_low = ring[5]
            down_in, down_high, down_low = ring[6]
            u_done = sem("u_done")
            tap2, tap1, tap0, silu_done, act_done = (sem(n) for n in ("tap2", "tap1", "tap0", "silu_done", "act_done"))
            block = ctx.enter_context(nc.Block())

            @block.sync
            def _(sp):
                with sp.Fori(1, FT) as f:
                    for c in range(2):
                        sp.wait_ge(w_low, 2 * f + c - 1)
                        sp.dma_start(raw[c][:], wup_v[:, :, bass.ds(f * P + c * FF, P)]).then_inc(raw_in[c], 16)
                for j in range(2):
                    sp.wait_ge(w_low, 2 * FT - 1 + j)
                    sp.dma_start(raw[j][:].rearrange(flat), w_down[0, j * P:(j + 1) * P, :]).then_inc(down_in[j], 16)

                for half in range(2):
                    for j in range(2 if half else 0):
                        sp.wait_ge(down_low, j - 1 + half * FT)
                        sp.dma_start(rawf[j], w_down[0, j * P:(j + 1) * P, :]).then_inc(down_in[j], 16)
                    with sp.Fori(1, FT // 2) as i:
                        for j in range(2):
                            sp.wait_ge(down_low, 2 * i + j - 1 + half * FT)
                            sp.dma_start(rawf[j], w_down[0, bass.ds((2 * i + j) * P, P), :]).then_inc(down_in[j], 16)

            @block.gpsimd
            def _(pool):
                pool.wait_ge(w_high, 2)
                pool.tensor_tensor(wl[1][:], raw[1][:], wh[1][:].bitcast(F32), ALU.subtract).then_inc(w_low, 1)
                with pool.Fori(1, FT) as f:
                    for c in range(2):
                        pool.wait_ge(w_high, 2 * f + c + 1)
                        pool.tensor_tensor(wl[c][:], raw[c][:], wh[c][:].bitcast(F32), ALU.subtract).then_inc(w_low, 1)
                for j in range(2):
                    pool.wait_ge(down_high, j + 1)
                    pool.tensor_tensor(wl[j][:], raw[j][:], wh[j][:].bitcast(F32), ALU.subtract).then_inc(down_low, 1)

                def low(g, j):
                    pool.wait_ge(down_high, g + 1)
                    pool.tensor_tensor(wlf[j], rawf[j], whf[j].bitcast(F32), ALU.subtract).then_inc(down_low, 1)

                for half in range(2):
                    if half:
                        for j in range(2):
                            low(FT + j, j)
                    for t in range(QT):
                        if half:
                            pool.wait_ge(stored[t], 16)
                        else:
                            pool.wait_ge(act_done, FT - 1 + t // 2)
                        pool.dma_start(x2[t][:], x2_dram[(QT * half + t) * P:(QT * half + t + 1) * P, :]).then_inc(x2_in[t], 16)
                    with pool.Fori(1, FT // 2) as i:
                        for j in range(2):
                            low(2 * i + j + half * FT, j)

            @block.tensor
            def _(pe):
                def tile(f, j):
                    for c in range(2):
                        pe.wait_ge(w_low, 2 * f + c + 1)
                        after(pe, tap0, 2 * f + c - 3)
                        for kt in range(KT):
                            for stat_, mov in ((wh, hTh), (wh, hTl), (wl, hTh)):
                                for h in range(2):
                                    mm = pe.matmul(u_ps[j][c][:, HALF * h:HALF * h + HALF], stat_[c][:, kt, :],
                                                   mov[:, kt, HALF * h:HALF * h + HALF],
                                                   start=(kt == 0 and stat_ is wh and mov is hTh),
                                                   stop=(kt == KT - 1 and stat_ is wl))
                        mm.then_inc(u_done, 1)
                tile(0, 0)
                tile(1, 1)
                with pe.Fori(1, FT // 2) as i:
                    tile(2 * i, 0)
                    tile(2 * i + 1, 1)

                def step(half, f, j, first, last):
                    g = half * FT + f
                    pe.wait_ge(down_low, g + 1)
                    pe.wait_ge(a_low, g + 1)
                    for t in range(QT):
                        if first and half:
                            pe.wait_ge(summed, t + 1)
                        elif first:
                            pe.wait_ge(tap0, 2 * (FT - 2) + t + 1)
                        for stat_, mov in ((ah, whf), (ah, wlf), (al, whf)):
                            for c in range(2):
                                mm = pe.matmul(acc[t][:, HALF * c:HALF * c + HALF], stat_[j][:, t * P:(t + 1) * P],
                                               mov[j][:, HALF * c:HALF * c + HALF],
                                               start=(first and stat_ is ah and mov is whf), stop=(last and stat_ is al))
                        if last:
                            mm.then_inc(acc_done, 1)
                    if not last:
                        mm.then_inc(used, 1)
                for half in range(2):
                    step(half, 0, 0, True, False)
                    step(half, 1, 1, False, False)
                    with pe.Fori(1, FT // 2 - 1) as i:
                        step(half, 2 * i, 0, False, False)
                        step(half, 2 * i + 1, 1, False, False)
                    step(half, FT - 2, 0, False, False)
                    step(half, FT - 1, 1, False, True)

            @block.scalar
            def _(act):
                def w_split(f, c):
                    act.wait_ge(raw_in[c], 16 * f + 16)
                    after(act, u_done, 2 * f + c - 1)
                    act.activation(wh[c][:], raw[c][:], ACT.Copy).then_inc(w_high, 1)

                def evacuate(f, j, c):
                    act.wait_ge(u_done, 2 * f + c + 1)
                    after(act, act_done, f - 1)
                    act.activation(u[j][c][:], u_ps[j][c][:], ACT.Identity, scale=cols[:, 2, bass.ds(f + c * FT, 1)],
                                   bias=cols[:, 3, bass.ds(f + c * FT, 1)]).then_inc(tap2, 1)

                def silu(f, j):
                    act.wait_ge(tap0, 2 * f + 1)
                    act.activation(u[j][0][:], u[j][0][:], ACT.Silu).then_inc(silu_done, 1)

                def tile(f, j, more):
                    for c in range(2):
                        evacuate(f, j, c)
                        if more:
                            w_split(f + 1, c)
                        else:
                            act.wait_ge(down_in[c], 16)
                            act.activation(whf[c], rawf[c], ACT.Copy).then_inc(down_high, 1)
                    silu(f, j)
                w_split(0, 1)
                tile(0, 0, True)
                tile(1, 1, True)
                with act.Fori(1, FT // 2 - 1) as i:
                    tile(2 * i, 0, True)
                    tile(2 * i + 1, 1, True)
                tile(FT - 2, 0, True)
                for j in range(2):
                    act.wait_ge(act_done, j + 1)
                    act.activation(ah[j][:], act_t[:, j, 0:HALF], ACT.Copy).then_inc(a_high, 1)
                tile(FT - 1, 1, False)

                def step(half, f, j, turn):
                    act.wait_ge(down_in[j], 16 * turn + 16)
                    if half and isinstance(f, int) and f < 2:
                        act.wait_ge(used, FT - 1)
                        if f == 1:
                            act.wait_ge(acc_done, QT)
                    else:
                        act.wait_ge(used, half * (FT - 1) + f - 1)
                    act.activation(whf[j], rawf[j], ACT.Copy).then_inc(down_high, 1)
                    act.activation(ah[j][:], act_t[:, bass.ds(f, 1), HALF * half:HALF * half + HALF].rearrange("p a b -> p (a b)"),
                                   ACT.Copy).then_inc(a_high, 1)

                def out_store(half, t):
                    act.wait_ge(summed, QT * half + t + 1)
                    act.dma_start(out[0, (QT * half + t) * P:(QT * half + t + 1) * P, :], x2[t][:]).then_inc(stored[t], 16)
                act.wait_ge(act_done, FT)
                with act.Fori(1, FT // 2) as i:
                    for j in range(2):
                        step(0, 2 * i + j, j, i)
                step(1, 0, 0, FT // 2)
                step(1, 1, 1, FT // 2)
                for t in range(QT):
                    out_store(0, t)
                with act.Fori(1, FT // 2) as i:
                    for j in range(2):
                        step(1, 2 * i + j, j, FT // 2 + i)
                for t in range(QT):
                    out_store(1, t)
                for t in range(QT):
                    act.wait_ge(stored[t], 32)

            @block.vector
            def _(dve):
                def tile(f, j):
                    for c in range(2):
                        dve.wait_ge(tap2, 2 * f + c + 1)
                        dve.scalar_tensor_tensor(out=u[j][c][:, 1:S], in0=u_ps[j][c][:, 0:S - 1], scalar=cols[:, 1, bass.ds(f + c * FT, 1)],
                                                 in1=u[j][c][:, 1:S], op0=ALU.mult, op1=ALU.add).then_inc(tap1, 1)
                        dve.wait_ge(tap1, 2 * f + c + 1)
                        dve.scalar_tensor_tensor(out=u[j][c][:, 2:S], in0=u_ps[j][c][:, 0:S - 2], scalar=cols[:, 0, bass.ds(f + c * FT, 1)],
                                                 in1=u[j][c][:, 2:S], op0=ALU.mult, op1=ALU.add).then_inc(tap0, 1)
                    dve.wait_ge(silu_done, f + 1)
                    dve.wait_ge(tap0, 2 * f + 2)
                    dve.tensor_tensor(act_t[:, bass.ds(f, 1), :].rearrange("p a b -> p (a b)"), u[j][0][:], u[j][1][:], ALU.mult).then_inc(act_done, 1)
                with dve.Fori(0, FT // 2 - 1) as i:
                    tile(2 * i, 0)
                    tile(2 * i + 1, 1)
                tile(FT - 2, 0)
                for j in range(2):
                    dve.wait_ge(a_high, j + 1)
                    dve.tensor_tensor(al[j][:], act_t[:, j, 0:HALF], ah[j][:].bitcast(F32), ALU.subtract).then_inc(a_low, 1)
                tile(FT - 1, 1)

                def step(half, f, j):
                    g = half * FT + f
                    dve.wait_ge(a_high, g + 1)
                    dve.tensor_tensor(al[j][:], act_t[:, bass.ds(f, 1), HALF * half:HALF * half + HALF].rearrange("p a b -> p (a b)"),
                                      ah[j][:].bitcast(F32), ALU.subtract).then_inc(a_low, 1)

                def row_sum(half, t):
                    dve.wait_ge(acc_done, QT * half + t + 1)
                    dve.wait_ge(x2_in[t], 16 * half + 16)
                    dve.tensor_tensor(x2[t][:], acc[t][:], x2[t][:], ALU.add).then_inc(summed, 1)
                with dve.Fori(1, FT // 2) as i:
                    for j in range(2):
                        step(0, 2 * i + j, j)
                step(1, 0, 0)
                for t in range(QT):
                    row_sum(0, t)
                step(1, 1, 1)
                with dve.Fori(1, FT // 2) as i:
                    for j in range(2):
                        step(1, 2 * i + j, j)
                for t in range(QT):
                    row_sum(1, t)


_INS = ["x", "g_mix", "w_in", "b_forget", "b_gate", "g_q", "g_k", "w_o_sb", "w_o_fox", "w_out",
        "g_ffn", "w_up", "conv_w", "conv_b", "w_down"]


def kernel(**inputs):
    import numpy as np
    import concourse.bacc as bacc
    from concourse.bass_utils import run_bass_kernel_spmd

    nc = bacc.Bacc("TRN2", target_bir_lowering=False, num_devices=1)
    arrays, args = {}, []
    for name in _INS:
        a = np.ascontiguousarray(inputs[name])
        arrays[f"in_{name}"] = a
        args.append(nc.dram_tensor(f"in_{name}", a.shape, mybir.dt.from_np(a.dtype), kind="ExternalInput").ap())
    out = nc.dram_tensor("out", (1, S, D), F32, kind="ExternalOutput").ap()
    build(nc, *args, out)
    r = run_bass_kernel_spmd(nc, [arrays], core_ids=[0])
    return r.results[0]["out"]
```
